# Optimizing a Trainium2 kernel written in Bass

```python
import jax, jax.numpy as jnp
from jax import lax
import numpy as np

D_MODEL = 1024
BATCH = 1
SEQ = 128
DEPTH = 1
DEC_BATCH = 1
DEC_SEQ = 256
PAST_LEN = 128

GRID_W = 64
MLA_HEADS = 8
QK_NOPE = 64
QK_ROPE = 32
V_HEAD = 64
Q_LORA = 256
KV_LORA = 256
ROPE_THETA = 10000.0
GDN_HEADS = 8
GDN_DK = 64
GDN_DV = 64
CONV_K = 5
CHUNK = 64
N_EXPERTS = 64
TOP_K = 8
N_GROUPS = 8
TOPK_GROUPS = 4
D_EXPERT = 256
D_SHARED = 256
ROUTED_SCALE = 2.5
EPS = 1e-6
Q_BLOCK = 128
TOK_BLOCK = 128

MLA_QK = QK_NOPE + QK_ROPE
MLA_WIDTH = MLA_HEADS * V_HEAD
GDN_QKV = GDN_HEADS * (2 * GDN_DK + GDN_DV)
GDN_WIDTH = GDN_HEADS * GDN_DV
IN_SIZES = (Q_LORA, KV_LORA, QK_ROPE, GDN_QKV, GDN_WIDTH, 2 * GDN_HEADS, 2 * GDN_HEADS, D_MODEL, D_MODEL)
D_IN = sum(IN_SIZES)

kernel_name = 'hybrid_mla_gdn_moe_diffusion_step'

def rms_norm(x, g):
    xf = x.astype(jnp.float32)
    y = xf * lax.rsqrt(jnp.mean(xf * xf, axis=-1, keepdims=True) + EPS)
    return (y * g.astype(jnp.float32)).astype(x.dtype)

def l2_normalize(x):
    return x * lax.rsqrt(jnp.sum(x * x, axis=-1, keepdims=True) + EPS)

def axial_rope(n_tokens):
    rows = n_tokens // GRID_W
    row = jnp.repeat(jnp.arange(rows, dtype=jnp.float32), GRID_W)
    col = jnp.tile(jnp.arange(GRID_W, dtype=jnp.float32), rows)
    n_freq = QK_ROPE // 4
    inv = ROPE_THETA ** (-jnp.arange(n_freq, dtype=jnp.float32) / n_freq)
    ang = jnp.stack([row[:, None] * inv, col[:, None] * inv], axis=1)
    return jnp.cos(ang), jnp.sin(ang)

def apply_rope(x, cos, sin):
    x5 = x.reshape(x.shape[:-1] + (2, 2, QK_ROPE // 4)).astype(jnp.float32)
    a, b = x5[..., 0, :], x5[..., 1, :]
    out = jnp.stack([a * cos - b * sin, b * cos + a * sin], axis=-2)
    return out.reshape(x.shape).astype(x.dtype)

def block_attention(q, k, v):
    b, lq, h, dqk = q.shape
    nb = lq // Q_BLOCK
    scale = dqk ** -0.5
    qb = jnp.moveaxis(q.reshape(b, nb, Q_BLOCK, h, dqk), 1, 0)

    def one(qi):
        s = jnp.einsum('bqhd,bkhd->bhqk', qi, k, preferred_element_type=jnp.float32) * scale
        p = jax.nn.softmax(s, axis=-1).astype(v.dtype)
        return jnp.einsum('bhqk,bkhd->bqhd', p, v)

    o = lax.map(one, qb)
    return jnp.moveaxis(o, 0, 1).reshape(b, lq, h, v.shape[-1])

def project_inputs(h, w_in):
    offs = np.cumsum(IN_SIZES)[:-1].tolist()
    return jnp.split(h @ w_in, offs, axis=-1)

def mla_queries(c_q, q_norm_g, w_uq):
    q = rms_norm(c_q, q_norm_g) @ w_uq
    q = q.reshape(q.shape[:-1] + (MLA_HEADS, MLA_QK))
    return q[..., :QK_NOPE], q[..., QK_NOPE:]

def mla_keys_values(ckv, krope, w_ukv):
    kv = (ckv @ w_ukv).reshape(ckv.shape[:-1] + (MLA_HEADS, QK_NOPE + V_HEAD))
    k_nope, v = kv[..., :QK_NOPE], kv[..., QK_NOPE:]
    k_rope = jnp.broadcast_to(krope[..., None, :], k_nope.shape[:-1] + (QK_ROPE,))
    return jnp.concatenate([k_nope, k_rope], axis=-1), v

def depthwise_conv(x, w):
    return lax.conv_general_dilated(x, w[:, None, :], window_strides=(1,),
                                    padding=[(CONV_K // 2, CONV_K // 2)],
                                    dimension_numbers=('NWC', 'WIO', 'NWC'),
                                    feature_group_count=x.shape[-1])

def gdn_prepare(qkv_raw, a_raw, b_raw, conv_w, a_log, dt_bias):
    bsz, n, _ = qkv_raw.shape
    qkv = jax.nn.silu(depthwise_conv(qkv_raw, conv_w)).astype(jnp.float32)
    nq = GDN_HEADS * GDN_DK
    q = qkv[..., :nq].reshape(bsz, n, GDN_HEADS, GDN_DK)
    k = qkv[..., nq:2 * nq].reshape(bsz, n, GDN_HEADS, GDN_DK)
    v = qkv[..., 2 * nq:].reshape(bsz, n, GDN_HEADS, GDN_DV)
    q = l2_normalize(q) * GDN_DK ** -0.5
    k = l2_normalize(k)
    a = a_raw.astype(jnp.float32).reshape(bsz, n, 2, GDN_HEADS)
    g = -jnp.exp(a_log.astype(jnp.float32)) * jax.nn.softplus(a + dt_bias.astype(jnp.float32))
    beta = jax.nn.sigmoid(b_raw.astype(jnp.float32).reshape(bsz, n, 2, GDN_HEADS))
    return q, k, v, g, beta

def chunk_gated_delta(q, k, v, g, beta, s0):
    bsz, n_tok, nh, _ = q.shape
    n = n_tok // CHUNK

    def chunks(t):
        t = jnp.moveaxis(t, 2, 1)
        return t.reshape((bsz, nh, n, CHUNK) + t.shape[3:])

    q, k, v, g, beta = (chunks(t) for t in (q, k, v, g, beta))
    gc = jnp.cumsum(g, axis=-1)
    idx = jnp.arange(CHUNK)
    incl = idx[:, None] >= idx[None, :]
    strict = idx[:, None] > idx[None, :]
    decay = jnp.exp(jnp.where(incl, gc[..., :, None] - gc[..., None, :], -jnp.inf))
    kb = k * beta[..., None]
    lmat = jnp.where(strict, jnp.einsum('bhncd,bhnsd->bhncs', kb, k) * decay, 0.0)
    eye = jnp.eye(CHUNK, dtype=jnp.float32)
    tmat = lax.linalg.triangular_solve(eye + lmat, jnp.broadcast_to(eye, lmat.shape), left_side=True, lower=True)
    u = tmat @ (v * beta[..., None])
    w = tmat @ (kb * jnp.exp(gc)[..., None])
    a_intra = jnp.einsum('bhncd,bhnsd->bhncs', q, k) * decay
    q_dec = q * jnp.exp(gc)[..., None]
    k_dec = k * jnp.exp(gc[..., -1:] - gc)[..., None]
    g_last = jnp.exp(gc[..., -1])

    def step(s, inp):
        u_c, w_c, a_c, qd_c, kd_c, gl_c = inp
        v_new = u_c - w_c @ s
        o = qd_c @ s + a_c @ v_new
        s = s * gl_c[..., None, None] + jnp.swapaxes(kd_c, -1, -2) @ v_new
        return s, o

    xs = tuple(jnp.moveaxis(t, 2, 0) for t in (u, w, a_intra, q_dec, k_dec, g_last))
    s_fin, o = lax.scan(step, s0, xs)
    o = jnp.moveaxis(o, 0, 2).reshape(bsz, nh, n_tok, -1)
    return jnp.moveaxis(o, 1, 2), s_fin

def bidirectional_gdn(q, k, v, g, beta, s0):
    o_f, s_f = chunk_gated_delta(q, k, v, g[:, :, 0], beta[:, :, 0], s0[:, 0])
    fl = lambda t: jnp.flip(t, axis=1)
    o_b, s_b = chunk_gated_delta(fl(q), fl(k), fl(v), fl(g[:, :, 1]), fl(beta[:, :, 1]), s0[:, 1])
    return o_f + fl(o_b), jnp.stack([s_f, s_b], axis=1)

def gdn_output(o, z, gdn_norm_g, dtype):
    bsz, n = z.shape[:2]
    o = rms_norm(o, gdn_norm_g) * jax.nn.silu(z.astype(jnp.float32).reshape(bsz, n, GDN_HEADS, GDN_DV))
    return o.reshape(bsz, n, GDN_WIDTH).astype(dtype)

def moe(h, p):
    bsz, n, d = h.shape
    tokens = h.reshape(-1, TOK_BLOCK, d)
    per_group = N_EXPERTS // N_GROUPS

    def one(t):
        s = jax.nn.sigmoid((t @ p['w_router']).astype(jnp.float32))
        sel = s + p['e_bias'].astype(jnp.float32)
        grp = lax.top_k(sel.reshape(-1, N_GROUPS, per_group), 2)[0].sum(-1)
        _, gidx = lax.top_k(grp, TOPK_GROUPS)
        gmask = jnp.any(gidx[:, :, None] == jnp.arange(N_GROUPS), axis=1)
        sel = jnp.where(jnp.repeat(gmask, per_group, axis=-1), sel, -jnp.inf)
        _, eidx = lax.top_k(sel, TOP_K)
        wk = jnp.take_along_axis(s, eidx, axis=-1)
        wk = wk / jnp.sum(wk, axis=-1, keepdims=True) * ROUTED_SCALE
        gates = jnp.einsum('tk,tke->te', wk, jax.nn.one_hot(eidx, N_EXPERTS, dtype=jnp.float32)).astype(t.dtype)
        hg = jnp.einsum('td,edf->tef', t, p['w_gate'])
        hu = jnp.einsum('td,edf->tef', t, p['w_up'])
        routed = jnp.einsum('tef,efd->td', jax.nn.silu(hg) * hu * gates[:, :, None], p['w_down'])
        shared = (jax.nn.silu(t @ p['ws_gate']) * (t @ p['ws_up'])) @ p['ws_down']
        return routed + shared

    return lax.map(one, tokens).reshape(bsz, n, d)

def mix_merge(o_mla, o_gdn, gate_a, gate_b, p):
    bsz, n = o_gdn.shape[:2]
    y_a = o_mla.reshape(bsz, n, MLA_WIDTH) @ p['w_oa']
    y_b = o_gdn @ p['w_ob']
    return (jax.nn.sigmoid(gate_a) * y_a + jax.nn.sigmoid(gate_b) * y_b) @ p['w_o']

def channel_sublayer(x, p, shift, scale, gate):
    h = rms_norm(x, p['g_pre_ffn']) * (1 + scale) + shift
    return x + gate * rms_norm(moe(h, p), p['g_post_ffn'])

def context_layer(x, p, mods):
    bsz = x.shape[0]
    h = rms_norm(x, p['g_pre_mix']) * (1 + mods[:, :, 1]) + mods[:, :, 0]
    c_q, ckv_raw, krope, qkv_raw, z, a_raw, b_raw, gate_a, gate_b = project_inputs(h, p['w_in'])
    ckv = rms_norm(ckv_raw, p['kv_norm_g'])
    q_nope, q_rope = mla_queries(c_q, p['q_norm_g'], p['w_uq'])
    k, v = mla_keys_values(ckv, krope, p['w_ukv'])
    o_mla = block_attention(jnp.concatenate([q_nope, q_rope], axis=-1), k, v)
    q_g, k_g, v_g, g_g, b_g = gdn_prepare(qkv_raw, a_raw, b_raw, p['conv_w'], p['a_log'], p['dt_bias'])
    s0 = jnp.zeros((bsz, 2, GDN_HEADS, GDN_DK, GDN_DV), jnp.float32)
    o_g, s_fin = bidirectional_gdn(q_g, k_g, v_g, g_g, b_g, s0)
    y = mix_merge(o_mla, gdn_output(o_g, z, p['gdn_norm_g'], x.dtype), gate_a, gate_b, p)
    x = x + mods[:, :, 2] * rms_norm(y, p['g_post_mix'])
    x = channel_sublayer(x, p, mods[:, :, 3], mods[:, :, 4], mods[:, :, 5])
    return x, ckv, krope, s_fin.astype(x.dtype)

def latent_layer(x, p, mods, ckv_ctx, krope_ctx, s_ctx):
    n = x.shape[1]
    h = rms_norm(x, p['g_pre_mix']) * (1 + mods[:, :, 1]) + mods[:, :, 0]
    c_q, ckv_raw, krope, qkv_raw, z, a_raw, b_raw, gate_a, gate_b = project_inputs(h, p['w_in'])
    cos, sin = axial_rope(n)
    ckv = rms_norm(ckv_raw, p['kv_norm_g'])
    q_nope, q_rope = mla_queries(c_q, p['q_norm_g'], p['w_uq'])
    q_rope = apply_rope(q_rope, cos[:, None], sin[:, None])
    k_lat, v_lat = mla_keys_values(ckv, apply_rope(krope, cos, sin), p['w_ukv'])
    k_ctx, v_ctx = mla_keys_values(ckv_ctx, krope_ctx, p['w_ukv'])
    o_mla = block_attention(jnp.concatenate([q_nope, q_rope], axis=-1),
                            jnp.concatenate([k_ctx, k_lat], axis=1),
                            jnp.concatenate([v_ctx, v_lat], axis=1))
    q_g, k_g, v_g, g_g, b_g = gdn_prepare(qkv_raw, a_raw, b_raw, p['conv_w'], p['a_log'], p['dt_bias'])
    o_g, _ = bidirectional_gdn(q_g, k_g, v_g, g_g, b_g, s_ctx.astype(jnp.float32))
    y = mix_merge(o_mla, gdn_output(o_g, z, p['gdn_norm_g'], x.dtype), gate_a, gate_b, p)
    x = x + mods[:, :, 2] * rms_norm(y, p['g_post_mix'])
    return channel_sublayer(x, p, mods[:, :, 3], mods[:, :, 4], mods[:, :, 5])

def setup_inputs(seed: int = 0) -> dict:
    key = jax.random.key(seed)
    ks = iter(jax.random.split(key, 48))
    f32 = jnp.float32
    D = D_MODEL

    def nrm(shape, scale):
        return jax.random.normal(next(ks), shape, f32) * scale

    def gain(shape):
        return 1.0 + nrm(shape, 0.05)

    dt = jnp.exp(jax.random.uniform(next(ks), (DEPTH, 2, GDN_HEADS), f32, minval=np.log(1e-3), maxval=np.log(1e-1)))
    return {
        'x_prompt': nrm((BATCH, SEQ, D), 1.0),
        'x_sample': nrm((DEC_BATCH, DEC_SEQ, D), 1.0),
        'cache_ckv': nrm((DEC_BATCH, DEPTH, PAST_LEN, KV_LORA), 1.0),
        'cache_krope': nrm((DEC_BATCH, DEPTH, PAST_LEN, QK_ROPE), 1.0),
        'state_delta': nrm((DEC_BATCH, DEPTH, 2, GDN_HEADS, GDN_DK, GDN_DV), 0.1),
        'c': nrm((DEC_BATCH, D), 1.0),
        'c_ctx': nrm((D,), 1.0),
        'w_ada': nrm((DEPTH, D, 6 * D), D ** -0.5),
        'b_ada': nrm((DEPTH, 6 * D), 0.02),
        'g_pre_mix': gain((DEPTH, D)),
        'g_post_mix': gain((DEPTH, D)),
        'g_pre_ffn': gain((DEPTH, D)),
        'g_post_ffn': gain((DEPTH, D)),
        'w_in': nrm((DEPTH, D, D_IN), D ** -0.5),
        'q_norm_g': gain((DEPTH, Q_LORA)),
        'kv_norm_g': gain((DEPTH, KV_LORA)),
        'w_uq': nrm((DEPTH, Q_LORA, MLA_HEADS * MLA_QK), Q_LORA ** -0.5),
        'w_ukv': nrm((DEPTH, KV_LORA, MLA_HEADS * (QK_NOPE + V_HEAD)), KV_LORA ** -0.5),
        'conv_w': nrm((DEPTH, CONV_K, GDN_QKV), CONV_K ** -0.5),
        'a_log': jnp.log(jax.random.uniform(next(ks), (DEPTH, 2, GDN_HEADS), f32, minval=1.0, maxval=16.0)),
        'dt_bias': dt + jnp.log(-jnp.expm1(-dt)),
        'gdn_norm_g': gain((DEPTH, GDN_DV)),
        'w_oa': nrm((DEPTH, MLA_WIDTH, D), MLA_WIDTH ** -0.5),
        'w_ob': nrm((DEPTH, GDN_WIDTH, D), GDN_WIDTH ** -0.5),
        'w_o': nrm((DEPTH, D, D), D ** -0.5),
        'w_router': nrm((DEPTH, D, N_EXPERTS), D ** -0.5),
        'e_bias': nrm((DEPTH, N_EXPERTS), 0.01),
        'w_gate': nrm((DEPTH, N_EXPERTS, D, D_EXPERT), D ** -0.5),
        'w_up': nrm((DEPTH, N_EXPERTS, D, D_EXPERT), D ** -0.5),
        'w_down': nrm((DEPTH, N_EXPERTS, D_EXPERT, D), D_EXPERT ** -0.5),
        'ws_gate': nrm((DEPTH, D, D_SHARED), D ** -0.5),
        'ws_up': nrm((DEPTH, D, D_SHARED), D ** -0.5),
        'ws_down': nrm((DEPTH, D_SHARED, D), D_SHARED ** -0.5),
    }

def reference(x_prompt, x_sample, cache_ckv, cache_krope, state_delta, c, c_ctx,
              w_ada, b_ada, g_pre_mix, g_post_mix, g_pre_ffn, g_post_ffn,
              w_in, q_norm_g, kv_norm_g, w_uq, w_ukv, conv_w, a_log, dt_bias, gdn_norm_g,
              w_oa, w_ob, w_o, w_router, e_bias, w_gate, w_up, w_down, ws_gate, ws_up, ws_down):
    y_p, y_s = x_prompt, x_sample
    ckv_list, krope_list, state_list = [], [], []
    for l in range(DEPTH):
        p = {
            'g_pre_mix': g_pre_mix[l], 'g_post_mix': g_post_mix[l],
            'g_pre_ffn': g_pre_ffn[l], 'g_post_ffn': g_post_ffn[l],
            'w_in': w_in[l], 'q_norm_g': q_norm_g[l], 'kv_norm_g': kv_norm_g[l],
            'w_uq': w_uq[l], 'w_ukv': w_ukv[l], 'conv_w': conv_w[l],
            'a_log': a_log[l], 'dt_bias': dt_bias[l], 'gdn_norm_g': gdn_norm_g[l],
            'w_oa': w_oa[l], 'w_ob': w_ob[l], 'w_o': w_o[l],
            'w_router': w_router[l], 'e_bias': e_bias[l],
            'w_gate': w_gate[l], 'w_up': w_up[l], 'w_down': w_down[l],
            'ws_gate': ws_gate[l], 'ws_up': ws_up[l], 'ws_down': ws_down[l],
        }
        mods_ctx = (jax.nn.silu(c_ctx) @ w_ada[l] + b_ada[l]).reshape(1, 1, 6, D_MODEL)
        mods_lat = (jax.nn.silu(c) @ w_ada[l] + b_ada[l]).reshape(-1, 1, 6, D_MODEL)
        y_p, ckv_l, krope_l, state_l = context_layer(y_p, p, mods_ctx)
        y_s = latent_layer(y_s, p, mods_lat, cache_ckv[:, l], cache_krope[:, l], state_delta[:, l])
        ckv_list.append(ckv_l)
        krope_list.append(krope_l)
        state_list.append(state_l)
    new_ckv = jnp.stack(ckv_list, axis=1)
    new_krope = jnp.stack(krope_list, axis=1)
    new_state = jnp.stack(state_list, axis=1)
    return (y_p, y_s, new_ckv, new_krope, new_state)


_drawn_inputs = setup_inputs


def setup_inputs(seed=0):
    import zlib

    import numpy as np

    out = dict(_drawn_inputs(seed))
    spreads = {}
    factors = {}
    for name, (base, spread) in spreads.items():
        noise = np.random.default_rng([zlib.crc32(name.encode()), seed]).standard_normal(out[name].shape)
        drawn = base * np.exp(spread * noise) if base else spread * noise
        out[name] = __import__('jax').numpy.asarray(drawn.astype(out[name].dtype))
    for name, factor in factors.items():
        out[name] = (out[name] * factor).astype(out[name].dtype)
    return out
```

```python
from contextlib import ExitStack

import numpy as np

import concourse.bass as bass
from concourse import mybir

F32 = mybir.dt.float32
ALU = mybir.AluOpType
ACT = mybir.ActivationFunctionType
AX = mybir.AxisListType.X

P = 128
D = 1024
KD = D // P
CTX, LAT, PAST = 128, 256, 128
TILES = (CTX + LAT) // P
TOK = TILES * P
MH, NOPE, ROPE, VH = 8, 64, 32, 64
QK = NOPE + ROPE
LORA = 256
KL = LORA // P
GH, DK, DV = 8, 64, 64
GW = GH * DV
CONV, CHUNK = 5, 64
EXPERTS, GROUPS, TOPG, TOPK = 64, 8, 4, 8
PER = EXPERTS // GROUPS
FE = 256
KF = FE // P
ROUTED = 2.5
EPS = 1e-6
GRID_W, THETA = 64, 10000.0
GAP = CONV // 2
PADW = TOK + 3 * GAP
OUTW = TOK + GAP
LEVELS = (1, 2, 4, 8, 16, 32)

C_CQ, C_CKV, C_KR, C_QKV, C_Z, C_AB, C_GA, C_GB = 0, 256, 512, 544, 2080, 2592, 2624, 3648


def tok_at(t):
    return t * P + (GAP if t else 0)


def constant_columns():
    i = np.arange(P)[:, None]
    j = np.arange(P)[None, :]
    same = (i // CHUNK) == (j // CHUNK)
    parts = {"ident": i == j, "incl0": same & (i <= j), "incl1": same & (i >= j),
             "strict0": same & (i < j), "strict1": same & (i > j), "block": same,
             "half0": (i < CHUNK) & (j >= 0), "half1": (i >= CHUNK) & (j >= 0),
             "before": i < j, "ones": (i >= 0) & (j >= 0), "iota": j + 1 + 0 * i}
    for s in LEVELS:
        low = ((i // s) == (j // s) + 1) & ((j // s) % 2 == 0)
        parts[f"level0_{s}"] = low
        parts[f"level1_{s}"] = low.T
    inv = THETA ** (-np.arange(ROPE // 4) / (ROPE // 4))
    n = np.arange(LAT)
    ang = np.stack([(n // GRID_W)[:, None] * inv, (n % GRID_W)[:, None] * inv], axis=1).reshape(LAT, ROPE // 2)
    parts["cos"] = np.cos(ang).reshape(LAT // P, P, ROPE // 2).transpose(1, 0, 2).reshape(P, -1)
    parts["sin"] = np.sin(ang).reshape(LAT // P, P, ROPE // 2).transpose(1, 0, 2).reshape(P, -1)
    g = np.arange(GROUPS)
    parts["earlier"] = np.broadcast_to((g[None, :] < g[:, None]).reshape(1, -1), (P, GROUPS * GROUPS))
    at, n = {}, 0
    for name, a in parts.items():
        at[name] = (n, n + a.shape[1])
        n += a.shape[1]
    return np.concatenate([np.asarray(a, np.float32) for a in parts.values()], axis=1), at


class Names:
    pass


class Count:

    def __init__(self, names):
        self.at = {n: i + 1 for i, n in enumerate(names)}
        self.done = 0
        assert len(self.at) == len(names)

    def __getitem__(self, name):
        return self.at[name]

    def step(self, *name):
        name = name if len(name) > 1 else name[0]
        self.done += 1
        assert self.at[name] == self.done, (name, self.at[name], self.done)
        return 1


def over(ap, n, axis):
    a = ap.unsqueeze(axis)
    shape = list(a.shape)
    shape[axis] = n
    return a.broadcast_to(shape)


RING = 3


def build(nc, a, o):
    g = Names()
    with ExitStack() as ctx:
        def sb(name, shape, dt=F32, **kw):
            return ctx.enter_context(nc.sbuf_tensor(name, shape, dt, **kw))

        def sem(name):
            return ctx.enter_context(nc.semaphore(name))

        cols, at = constant_columns()
        g.cst = sb("cst", [P, cols.shape[1]])
        g.c = {n: g.cst[:, lo:hi] for n, (lo, hi) in at.items()}
        g.sem, g.a, g.o, g.ctx = sem, a, o, ctx
        g.ps = ctx.enter_context(nc.psum_tensor("ps", [P, 8, 512], F32))
        g.mods_dram = nc.dram_tensor("mods_scratch", [2, 6, D], F32, kind="Internal").ap()
        g.ring = sb("ring", [P, RING, KD, 512])
        g.hT = sb("hT", [P, KD, TOK])
        g.s_slot = [sem(f"slot_loaded{i}") for i in range(RING)]
        g.loads = 0
        phases(nc, g, sb, sem)


def slot(i):
    return i % RING


def loaded(i):
    return 16 * (i // RING + 1)


N_ADA = 6 * D // 512
IN_CHUNKS = [("cqkv", C_CQ), ("q", C_QKV), ("k", C_QKV + GW), ("v", C_QKV + 2 * GW), ("z", C_Z)]
GATE_CHUNKS = [("ga0", C_GA), ("gb0", C_GB), ("ga1", C_GA + 512), ("gb1", C_GB + 512)]
RING_LOADS = [("ada", n) for n in range(N_ADA)] + [c[0] for c in IN_CHUNKS] + [c[0] for c in GATE_CHUNKS]
LOAD = {n: i for i, n in enumerate(RING_LOADS)}


def ring_source(g, i):
    name = RING_LOADS[i]
    if isinstance(name, tuple):
        w, c0 = g.a["w_ada"][0], name[1] * 512
    else:
        w, c0 = g.a["w_in"][0], dict(IN_CHUNKS + GATE_CHUNKS)[name]
    return w.rearrange("(p k) n -> p k n", k=KD)[:, :, c0:c0 + 512]


def phase_condition(nc, g):
    a, ps, c = g.a, g.ps, g.c
    with ExitStack() as ctx:
        def sb(name, shape):
            return ctx.enter_context(nc.sbuf_tensor(name, shape, F32))
        cond = sb("cond", [P, 2, KD])
        scond = sb("scond", [P, 2, KD])
        bias = sb("bias", [2, 6 * D])
        mods = sb("mods", [2, 6 * D])
        x = sb("x", [P, TILES, D])
        xn = sb("xn", [P, TILES, D])
        stat = sb("stat", [P, 4, TILES])
        modT = sb("modT", [P, 2, 2, KD])
        gpre = sb("gpre", [P, KD])
        scaleT = sb("scaleT", [P, 2, KD])
        convrow = sb("convrow", [CONV * 12, P])
        s_c, s_cst, s_b, s_x, s_conv, s_g = (g.sem(n) for n in
            ("cond_loaded", "const_loaded", "bias_loaded", "x_loaded", "convw_loaded", "gpre_loaded"))
        g.s_cst = s_cst
        s_modst, s_modT, s_mods = g.sem("mods_head_stored"), g.sem("modT_loaded"), g.sem("mods_stored")
        pe_done, dve_done, act_done = g.sem("cond_pe"), g.sem("cond_dve"), g.sem("cond_act")
        pe_order = []
        for n in range(N_ADA):
            pe_order.append(("ada", n))
            if n == 5:
                pe_order += ["convT", ("xT", 0), ("xT", 1)]
            if n == 8:
                pe_order.append(("xT", 2))
        PE = Count(pe_order)
        dve_order = ["ms", "rms"] + [("xn", t) for t in range(TILES)] + [("mods", n) for n in range(4)] \
            + ["A1", "A"] + [("mods", 4), ("mods", 5), "convT", ("hT", 0), ("hT", 1)] \
            + [("mods", n) for n in range(6, 9)] + [("hT", 2)] + [("mods", n) for n in range(9, N_ADA)]
        V = Count(dve_order)
        A = Count(["scond"] + [("ss", t) for t in range(TILES)] + ["rs"])
        with nc.Block() as block:
            @block.sync
            def _(sp):
                for v, src in ((0, a["c_ctx"]), (1, a["c"][0])):
                    sp.dma_start(cond[:, v, :], src.rearrange("(p k) -> p k", k=KD)).then_inc(s_c, 16)
                for n in range(RING):
                    sp.dma_start(g.ring[:, slot(n)], ring_source(g, n)).then_inc(g.s_slot[slot(n)], 16)
                sp.dma_start(bias[:], a["b_ada"][0].partition_broadcast(2)).then_inc(s_b, 16)
                sp.dma_start(g.cst[:], a["table"]).then_inc(s_cst, 16)
                for n in range(RING, LOAD["v"]):
                    last = PE[("ada", n - RING)]
                    sp.wait_ge(pe_done, last)
                    sp.dma_start(g.ring[:, slot(n)], ring_source(g, n)).then_inc(g.s_slot[slot(n)], 16)
                    if n == RING + 4:
                        sp.wait_ge(dve_done, V[("mods", 3)])
                        sp.dma_start(g.mods_dram[:, 0:2, :].rearrange("v m d -> v (m d)"),
                                     mods[:, 0:2 * D]).then_inc(s_modst, 16)
                        sp.wait_ge(s_modst, 16)
                        for v in range(2):
                            sp.dma_start(modT[:, v], g.mods_dram[v, 0:2].rearrange("m (p k) -> p m k", k=KD)) \
                                .then_inc(s_modT, 16)
                sp.wait_ge(dve_done, V[("mods", N_ADA - 1)])
                sp.dma_start(g.mods_dram[:, 2:6, :].rearrange("v m d -> v (m d)"),
                             mods[:, 2 * D:6 * D]).then_inc(s_mods, 16)
                sp.wait_ge(s_mods, 16)

            @block.scalar
            def _(act):
                act.dma_start(x[:, 0, :], a["x_prompt"][0]).then_inc(s_x, 16)
                act.dma_start(x[:, 1:3, :], a["x_sample"][0].rearrange("(t p) d -> p t d", p=P)).then_inc(s_x, 16)
                act.dma_start(convrow[:], a["conv_w"][0].rearrange("j (m p) -> (j m) p", p=P)).then_inc(s_conv, 16)
                act.dma_start(gpre[:], a["g_pre_mix"][0].rearrange("(p k) -> p k", k=KD)).then_inc(s_g, 16)
                act.wait_ge(s_c, 32)
                act.activation(scond[:], cond[:], ACT.Silu).then_inc(act_done, A.step("scond"))
                act.wait_ge(s_x, 32)
                for t in range(TILES):
                    act.activation(xn[:, t, :], x[:, t, :], ACT.Square, accum_out=stat[:, 0, t:t + 1]) \
                        .then_inc(act_done, A.step("ss", t))
                act.wait_ge(dve_done, V["rms"])
                act.activation(stat[:, 3, :], stat[:, 2, :], ACT.Sqrt).then_inc(act_done, A.step("rs"))

            @block.tensor
            def _(pe):
                def transposes(t):
                    for k in range(KD):
                        mm = pe.transpose(ps[:, 4 + 2 * (t % 2) + k // 4, (k % 4) * P:(k % 4 + 1) * P],
                                          xn[:, t, k::KD], c["ident"])
                    mm.then_inc(pe_done, PE.step("xT", t))

                pe.wait_ge(act_done, A["scond"])
                for n in range(N_ADA):
                    pe.wait_ge(g.s_slot[slot(n)], loaded(n))
                    if n >= 4:
                        pe.wait_ge(dve_done, V[("mods", n - 4)])
                    for k in range(KD):
                        mm = pe.matmul(ps[0:2, n % 4, :], scond[:, :, k], g.ring[:, slot(n), k, :],
                                       start=(k == 0), stop=(k == KD - 1))
                    mm.then_inc(pe_done, PE.step("ada", n))
                    if n == 5:
                        pe.wait_ge(s_cst, 16)
                        pe.wait_ge(s_conv, 16)
                        pe.transpose(ps[:, 4, 0:CONV * 12], convrow[:], c["ident"][0:CONV * 12, 0:CONV * 12]) \
                            .then_inc(pe_done, PE.step("convT"))
                        pe.wait_ge(dve_done, V["convT"])
                        transposes(0)
                        transposes(1)
                    if n == 8:
                        pe.wait_ge(dve_done, V[("hT", 0)])
                        transposes(2)

            @block.vector
            def _(dve):
                dve.wait_ge(act_done, A[("ss", TILES - 1)])
                dve.tensor_scalar(stat[:, 1, :], stat[:, 0, :], 1.0 / D, EPS, ALU.mult, ALU.add) \
                    .then_inc(dve_done, V.step("ms"))
                dve.wait_ge(dve_done, V["ms"])
                dve.reciprocal(stat[:, 2, :], stat[:, 1, :]).then_inc(dve_done, V.step("rms"))
                dve.wait_ge(act_done, A["rs"])
                for t in range(TILES):
                    dve.tensor_scalar(xn[:, t, :], x[:, t, :], stat[:, 3, t:t + 1], None, ALU.mult) \
                        .then_inc(dve_done, V.step("xn", t))
                dve.wait_ge(s_b, 16)

                def take_mods(n):
                    dve.wait_ge(pe_done, PE[("ada", n)])
                    dve.tensor_tensor(mods[:, n * 512:(n + 1) * 512], ps[0:2, n % 4, :],
                                      bias[:, n * 512:(n + 1) * 512], ALU.add).then_inc(dve_done, V.step("mods", n))

                def take_hT(t):
                    dve.wait_ge(pe_done, PE[("xT", t)])
                    v = min(t, 1)
                    for k in range(KD):
                        i = dve.tensor_scalar(g.hT[:, k, t * P:(t + 1) * P],
                                              ps[:, 4 + 2 * (t % 2) + k // 4, (k % 4) * P:(k % 4 + 1) * P],
                                              scaleT[:, v, k:k + 1], modT[:, v, 0, k:k + 1], ALU.mult, ALU.add)
                    i.then_inc(dve_done, V.step("hT", t))

                for n in range(4):
                    take_mods(n)
                dve.wait_ge(s_modT, 32)
                dve.wait_ge(s_g, 16)
                dve.tensor_scalar(scaleT[:], modT[:, :, 1, :], 1.0, None, ALU.add).then_inc(dve_done, V.step("A1"))
                dve.wait_ge(dve_done, V["A1"])
                dve.tensor_tensor(scaleT[:], scaleT[:], over(gpre[:], 2, 1), ALU.mult).then_inc(dve_done, V.step("A"))
                dve.wait_ge(dve_done, V["A"])
                take_mods(4)
                take_mods(5)
                dve.wait_ge(pe_done, PE["convT"])
                dve.tensor_copy(g.wconv[:], ps[:, 4, 0:CONV * 12].rearrange("p (j m) -> p j m", j=CONV)) \
                    .then_inc(dve_done, V.step("convT"))
                take_hT(0)
                take_hT(1)
                for n in range(6, 9):
                    take_mods(n)
                take_hT(2)
                for n in range(9, N_ADA):
                    take_mods(n)


def phase_project(nc, g):
    a, ps = g.a, g.ps
    with ExitStack() as ctx:
        def sb(name, shape):
            return ctx.enter_context(nc.sbuf_tensor(name, shape, F32))
        wsmall = sb("wsmall", [P, KD, 64])
        acc = sb("acc", [P, 2, OUTW])
        pad = sb("pad", [P, 2, PADW])
        s_small = g.sem("wsmall_loaded")
        pe_done, dve_done, act_done = g.sem("proj_pe"), g.sem("proj_dve"), g.sem("proj_act")
        units = [("cqkv", t) for t in range(TILES)] + [("small", t) for t in range(TILES)] \
            + [(n, m) for n in "qkv" for m in range(4)] + [("z", t) for t in range(TILES)]
        PE = Count(units)
        A = Count(["gaps"] + [("cqkv", t) for t in range(TILES)] + [("small", t) for t in range(TILES)]
                  + [x for i in range(12) for x in ((("pad", i),) + ((("silu", i - 1),) if i else ()))]
                  + [("silu", 11)] + [("z", t) for t in range(TILES)])
        V = Count([(s, i) for i in range(12) for s in [f"tap{j}" for j in range(CONV)]])
        with nc.Block() as block:
            @block.sync
            def _(sp):
                w = a["w_in"][0].rearrange("(p k) n -> p k n", k=KD)
                sp.dma_start(wsmall[:, :, 0:32], w[:, :, C_KR:C_KR + 32]).then_inc(s_small, 16)
                sp.dma_start(wsmall[:, :, 32:64], w[:, :, C_AB:C_AB + 32]).then_inc(s_small, 16)
                for name, last in (("v", ("cqkv", TILES - 1)), ("z", ("q", 3)), ("ga0", ("k", 3)), ("gb0", ("v", 3)),
                                   ("ga1", ("z", TILES - 1))):
                    n = LOAD[name]
                    sp.wait_ge(pe_done, PE[last])
                    sp.dma_start(g.ring[:, slot(n)], ring_source(g, n)).then_inc(g.s_slot[slot(n)], 16)

            @block.tensor
            def _(pe):
                for i, (name, m) in enumerate(units):
                    b = i % 8
                    if name == "small":
                        pe.wait_ge(s_small, 32)
                    else:
                        n = LOAD[name]
                        pe.wait_ge(g.s_slot[slot(n)], loaded(n))
                    if i >= 8:
                        was = units[i - 8]
                        pe.wait_ge(act_done, A[("pad", "qkv".index(was[0]) * 4 + was[1])
                                               if was[0] in "qkv" else was])
                    for k in range(KD):
                        if name in ("cqkv", "z"):
                            mm = pe.matmul(ps[:, b, :], g.hT[:, k, m * P:(m + 1) * P], g.ring[:, slot(n), k, :],
                                           start=(k == 0), stop=(k == KD - 1))
                        elif name == "small":
                            mm = pe.matmul(ps[:, b, 0:64], g.hT[:, k, m * P:(m + 1) * P], wsmall[:, k, :],
                                           start=(k == 0), stop=(k == KD - 1))
                        else:
                            mm = pe.matmul(ps[:, b, 0:TOK], g.ring[:, slot(n), k, m * P:(m + 1) * P], g.hT[:, k, :],
                                           start=(k == 0), stop=(k == KD - 1))
                    mm.then_inc(pe_done, PE.step(name, m))

            @block.scalar
            def _(act):
                for b in range(2):
                    for z in (0, GAP + CTX, PADW - GAP):
                        i = act.activation(pad[:, b, z:z + GAP], g.c["ident"][:, 0:GAP], ACT.Copy, scale=0.0)
                i.then_inc(act_done, A.step("gaps"))
                at = 0

                def take(dst, width, name, m):
                    nonlocal at
                    act.wait_ge(pe_done, PE[(name, m)])
                    act.activation(dst, ps[:, at % 8, 0:width], ACT.Copy).then_inc(act_done, A.step(name, m))
                    at += 1

                def silu(i):
                    act.wait_ge(dve_done, V[("tap4", i)])
                    act.activation(g.qkv[:, i, :], acc[:, i % 2, :], ACT.Silu).then_inc(act_done, A.step("silu", i))

                for t in range(TILES):
                    take(g.cqkv[:, t, :], 512, "cqkv", t)
                for t in range(TILES):
                    take(g.small[:, t, :], 64, "small", t)
                for i in range(12):
                    act.wait_ge(pe_done, PE[("qkv"[i // 4], i % 4)])
                    if i >= 2:
                        act.wait_ge(dve_done, V[("tap4", i - 2)])
                    act.activation(pad[:, i % 2, GAP:GAP + CTX], ps[:, at % 8, 0:CTX], ACT.Copy)
                    act.activation(pad[:, i % 2, 2 * GAP + CTX:2 * GAP + TOK], ps[:, at % 8, CTX:TOK], ACT.Copy) \
                        .then_inc(act_done, A.step("pad", i))
                    at += 1
                    if i:
                        silu(i - 1)
                silu(11)
                for t in range(TILES):
                    take(g.z[:, t, :], 512, "z", t)

            @block.vector
            def _(dve):
                for i in range(12):
                    dve.wait_ge(act_done, A[("pad", i)])
                    if i >= 2:
                        dve.wait_ge(act_done, A[("silu", i - 2)])
                    for j in range(CONV):
                        src = pad[:, i % 2, j:j + OUTW]
                        w = g.wconv[:, j, i:i + 1]
                        if j == 0:
                            ins = dve.tensor_scalar(acc[:, i % 2, :], src, w, None, ALU.mult)
                        else:
                            dve.wait_ge(dve_done, V[(f"tap{j - 1}", i)])
                            ins = dve.scalar_tensor_tensor(out=acc[:, i % 2, :], in0=src, scalar=w,
                                                           in1=acc[:, i % 2, :], op0=ALU.mult, op1=ALU.add)
                        ins.then_inc(dve_done, V.step(f"tap{j}", i))


def phase_attention(nc, g):
    a, ps, c, o = g.a, g.ps, g.c, g.o
    KT = TILES + 1
    SCALE = float(QK) ** -0.5
    with ExitStack() as ctx:
        def sb(name, shape):
            return ctx.enter_context(nc.sbuf_tensor(name, shape, F32))
        wuq = sb("wuq", [P, KL, MH * QK])
        wukv = sb("wukv", [P, KL, MH * (NOPE + VH)])
        grow = sb("grow", [P, 2, LORA])
        kr = sb("kr", [P, KT, ROPE])
        ckv = sb("ckv", [P, KT, LORA])
        cqn = sb("cqn", [P, TILES, LORA])
        stat = sb("astat", [P, 4, 6])
        cqT = sb("cqT", [P, KL, TOK])
        ckvT = sb("ckvT", [P, KL, KT * P])
        q = sb("q", [P, TILES, MH, QK])
        k = sb("k", [P, KT, MH, QK])
        v = sb("v", [P, KT, MH, VH])
        qT = sb("qT", [QK, MH, TOK])
        kT = sb("kT", [QK, MH, KT * P])
        prob = sb("prob", [P, 2, 3 * P])
        probT = sb("probT", [P, 2, 3, P])
        nmax = sb("nmax", [P, TILES, MH])
        rsum = sb("rsum", [P, TILES, MH])
        rinv = sb("rinv", [P, TILES, MH])
        rope = sb("ropetmp", [P, 4, MH, 2, 8])
        s_w, s_g, s_cache, s_out = (g.sem(n) for n in ("attw_loaded", "gains_loaded", "cache_loaded", "ckv_stored"))
        pe_done, dve_done, act_done = g.sem("att_pe"), g.sem("att_dve"), g.sem("att_act")
        units = [(t, h) for t in range(TILES) for h in range(MH)]
        nk = lambda t: 1 if t == 0 else 3
        k0 = lambda t: 0 if t == 0 else 1
        loop = []
        for i in range(len(units) + 2):
            if i < len(units):
                loop.append(("score", i))
            if 1 <= i <= len(units):
                loop.append(("probT", i - 1))
            if i >= 2:
                loop.append(("pv", i - 2))
        PE = Count(["cqT", "ckvT"] + [("q", t) for t in range(TILES)] + [("kv", t) for t in range(KT)]
                   + [("qT", t) for t in range(TILES)] + [("kT", t) for t in range(KT)] + loop)
        rope_steps = lambda n: [(n, s) for s in ("ac", "bs", "bc", "as", "a", "b")]
        V = Count(["ms", "rms", "cqn0", "cqn", "ckv0", "ckv"] + rope_steps("kr1") + rope_steps("kr2")
                  + ["cqT"]
                  + [x for t in range(TILES) for x in (["q", t],)] * 0
                  + [("q", t) for t in range(TILES)] + rope_steps("q1") + rope_steps("q2")
                  + [("kr", t) for t in range(KT)] + [("qT", t) for t in range(TILES)]
                  + [x for i in range(len(units) + 2) for x in
                     ([("max", i)] if i < len(units) else []) + ([("probT", i - 1)] if 1 <= i <= len(units) else [])]
                  + ["rinv", "o"])
        A = Count([("ss", i) for i in range(6)] + ["rs", "ckvT"] + [("kv", t) for t in range(KT)]
                  + [("kT", t) for t in range(KT)] + [("exp", i) for i in range(len(units))])
        with nc.Block() as block:
            @block.sync
            def _(sp):
                sp.dma_start(grow[:, 0, :], a["q_norm_g"][0].partition_broadcast(P)).then_inc(s_g, 16)
                sp.dma_start(grow[:, 1, :], a["kv_norm_g"][0].partition_broadcast(P)).then_inc(s_g, 16)
                sp.dma_start(ckv[:, 1, :], a["cache_ckv"][0, 0]).then_inc(s_cache, 16)
                sp.dma_start(kr[:, 1, :], a["cache_krope"][0, 0]).then_inc(s_cache, 16)
                sp.dma_start(wuq[:], a["w_uq"][0].rearrange("(p j) n -> p j n", j=KL)).then_inc(s_w, 16)
                sp.dma_start(wukv[:], a["w_ukv"][0].rearrange("(p j) n -> p j n", j=KL)).then_inc(s_w, 16)
                sp.dma_start(o["krope"][0, 0], g.small[:, 0, 0:ROPE]).then_inc(s_out, 16)
                sp.wait_ge(dve_done, V["ckv"])
                sp.dma_start(o["ckv"][0, 0], ckv[:, 0, :]).then_inc(s_out, 16)
                sp.wait_ge(s_out, 32)

            @block.scalar
            def _(act):
                for i in range(6):
                    t, part = i % 3, i // 3
                    junk = cqn[:, t, :] if part == 0 else ckv[:, (0, 2, 3)[t], :]
                    act.activation(junk, g.cqkv[:, t, part * LORA:(part + 1) * LORA], ACT.Square,
                                   accum_out=stat[:, 0, i:i + 1]).then_inc(act_done, A.step("ss", i))
                act.wait_ge(dve_done, V["rms"])
                act.activation(stat[:, 3, :], stat[:, 2, :], ACT.Sqrt).then_inc(act_done, A.step("rs"))
                act.wait_ge(pe_done, PE["ckvT"])
                act.activation(ckvT[:], ps[:, 2:4, :], ACT.Copy).then_inc(act_done, A.step("ckvT"))
                for t in range(KT):
                    b = 2 * (t % 2)
                    act.wait_ge(pe_done, PE[("kv", t)])
                    src = ps[:, b:b + 2, :].rearrange("p b (h e) -> p (b h) e", e=P)
                    act.activation(k[:, t, :, 0:NOPE], src[:, :, 0:NOPE], ACT.Copy)
                    act.activation(v[:, t], src[:, :, NOPE:P], ACT.Copy).then_inc(act_done, A.step("kv", t))
                for t in range(KT):
                    b = 2 * (t % 2)
                    act.wait_ge(pe_done, PE[("kT", t)])
                    act.activation(kT[:, :, t * P:(t + 1) * P],
                                   ps[0:QK, b:b + 2, :].rearrange("p b (h e) -> p (b h) e", e=P), ACT.Copy) \
                        .then_inc(act_done, A.step("kT", t))
                for i, (t, h) in enumerate(units):
                    w = nk(t) * P
                    act.wait_ge(dve_done, V[("max", i)])
                    if i >= 2:
                        act.wait_ge(pe_done, PE[("probT", i - 2)])
                    act.activation(prob[:, i % 2, 0:w], ps[:, i % 2, 0:w], ACT.Exp, bias=nmax[:, t, h:h + 1],
                                   accum_out=rsum[:, t, h:h + 1]).then_inc(act_done, A.step("exp", i))

            @block.tensor
            def _(pe):
                pe.wait_ge(dve_done, V["cqn"])
                for j in range(KL):
                    for t in range(TILES):
                        mm = pe.transpose(ps[:, j, t * P:(t + 1) * P], cqn[:, t, j::KL], c["ident"])
                mm.then_inc(pe_done, PE.step("cqT"))
                pe.wait_ge(dve_done, V["ckv"])
                pe.wait_ge(s_cache, 32)
                for j in range(KL):
                    for t in range(KT):
                        mm = pe.transpose(ps[:, 2 + j, t * P:(t + 1) * P], ckv[:, t, j::KL], c["ident"])
                mm.then_inc(pe_done, PE.step("ckvT"))
                pe.wait_ge(s_w, 32)
                pe.wait_ge(dve_done, V["cqT"])
                for t in range(TILES):
                    b = 4 + 2 * (t % 2)
                    if t >= 2:
                        pe.wait_ge(dve_done, V[("q", t - 2)])
                    for lo, hi in ((0, 512), (512, MH * QK)):
                        for j in range(KL):
                            mm = pe.matmul(ps[:, b + lo // 512, 0:hi - lo], cqT[:, j, t * P:(t + 1) * P],
                                           wuq[:, j, lo:hi], start=(j == 0), stop=(j == KL - 1))
                    mm.then_inc(pe_done, PE.step("q", t))
                pe.wait_ge(act_done, A["ckvT"])
                for t in range(KT):
                    b = 2 * (t % 2)
                    if t >= 2:
                        pe.wait_ge(act_done, A[("kv", t - 2)])
                    for n in range(2):
                        for j in range(KL):
                            mm = pe.matmul(ps[:, b + n, :], ckvT[:, j, t * P:(t + 1) * P],
                                           wukv[:, j, n * 512:(n + 1) * 512], start=(j == 0), stop=(j == KL - 1))
                    mm.then_inc(pe_done, PE.step("kv", t))
                for t in range(TILES):
                    b = 4 + 2 * (t % 2)
                    pe.wait_ge(dve_done, V[("q2", "b")])
                    if t >= 2:
                        pe.wait_ge(dve_done, V[("qT", t - 2)])
                    for h in range(MH):
                        mm = pe.transpose(ps[0:QK, b + h // 4, (h % 4) * P:(h % 4 + 1) * P], q[:, t, h, :], c["ident"])
                    mm.then_inc(pe_done, PE.step("qT", t))
                for t in range(KT):
                    b = 2 * (t % 2)
                    pe.wait_ge(act_done, A[("kv", KT - 1)])
                    pe.wait_ge(dve_done, V[("kr", t)])
                    if t >= 2:
                        pe.wait_ge(act_done, A[("kT", t - 2)])
                    for h in range(MH):
                        mm = pe.transpose(ps[0:QK, b + h // 4, (h % 4) * P:(h % 4 + 1) * P], k[:, t, h, :], c["ident"])
                    mm.then_inc(pe_done, PE.step("kT", t))
                pe.wait_ge(act_done, A[("kT", KT - 1)])
                pe.wait_ge(dve_done, V[("qT", TILES - 1)])
                for i in range(len(units) + 2):
                    if i < len(units):
                        t, h = units[i]
                        if i >= 2:
                            pe.wait_ge(act_done, A[("exp", i - 2)])
                        pe.matmul(ps[:, i % 2, 0:nk(t) * P], qT[:, h, t * P:(t + 1) * P],
                                  kT[:, h, k0(t) * P:(k0(t) + nk(t)) * P], start=True, stop=True) \
                            .then_inc(pe_done, PE.step("score", i))
                    if 1 <= i <= len(units):
                        u = i - 1
                        t, h = units[u]
                        pe.wait_ge(act_done, A[("exp", u)])
                        if u >= 2:
                            pe.wait_ge(dve_done, V[("probT", u - 2)])
                        for n in range(nk(t)):
                            mm = pe.transpose(ps[:, 2 + u % 2, n * P:(n + 1) * P],
                                              prob[:, u % 2, n * P:(n + 1) * P], c["ident"])
                        mm.then_inc(pe_done, PE.step("probT", u))
                    if i >= 2:
                        u = i - 2
                        t, h = units[u]
                        pe.wait_ge(dve_done, V[("probT", u)])
                        for n in range(nk(t)):
                            mm = pe.matmul(ps[:, 4 + t, h * VH:(h + 1) * VH], probT[:, u % 2, n, :],
                                           v[:, k0(t) + n, h, :], start=(n == 0), stop=(n == nk(t) - 1))
                        mm.then_inc(pe_done, PE.step("pv", u))

            @block.vector
            def _(dve):
                dve.wait_ge(act_done, A[("ss", 5)])
                dve.tensor_scalar(stat[:, 1, :], stat[:, 0, :], 1.0 / LORA, EPS, ALU.mult, ALU.add) \
                    .then_inc(dve_done, V.step("ms"))
                dve.wait_ge(dve_done, V["ms"])
                dve.reciprocal(stat[:, 2, :], stat[:, 1, :]).then_inc(dve_done, V.step("rms"))
                dve.wait_ge(act_done, A["rs"])
                dve.wait_ge(s_g, 32)
                for t in range(TILES):
                    i = dve.tensor_scalar(cqn[:, t, :], g.cqkv[:, t, 0:LORA], stat[:, 3, t:t + 1], None, ALU.mult)
                i.then_inc(dve_done, V.step("cqn0"))
                dve.wait_ge(dve_done, V["cqn0"])
                dve.tensor_tensor(cqn[:], cqn[:], over(grow[:, 0, :], TILES, 1), ALU.mult) \
                    .then_inc(dve_done, V.step("cqn"))
                key = (0, 2, 3)
                for t in range(TILES):
                    i = dve.tensor_scalar(ckv[:, key[t], :], g.cqkv[:, t, LORA:2 * LORA], stat[:, 3, 3 + t:4 + t],
                                          None, ALU.mult)
                i.then_inc(dve_done, V.step("ckv0"))
                dve.wait_ge(dve_done, V["ckv0"])
                for t in range(TILES):
                    i = dve.tensor_tensor(ckv[:, key[t], :], ckv[:, key[t], :], grow[:, 1, :], ALU.mult)
                i.then_inc(dve_done, V.step("ckv"))

                def rotate(name, dst, src, heads, t):
                    r = lambda n: rope[:, n, 0:heads]
                    x = src.rearrange("p h (x s f) -> p h x s f", x=2, s=2)
                    y = dst.rearrange("p h (x s f) -> p h x s f", x=2, s=2)
                    tab = lambda n: over(c[n][:, (t - 1) * 16:t * 16].rearrange("p (x f) -> p x f", x=2), heads, 1)
                    dve.tensor_tensor(r(0), x[:, :, :, 0], tab("cos"), ALU.mult).then_inc(dve_done, V.step(name, "ac"))
                    dve.tensor_tensor(r(1), x[:, :, :, 1], tab("sin"), ALU.mult).then_inc(dve_done, V.step(name, "bs"))
                    dve.tensor_tensor(r(2), x[:, :, :, 1], tab("cos"), ALU.mult).then_inc(dve_done, V.step(name, "bc"))
                    dve.tensor_tensor(r(3), x[:, :, :, 0], tab("sin"), ALU.mult).then_inc(dve_done, V.step(name, "as"))
                    dve.wait_ge(dve_done, V[(name, "as")])
                    dve.tensor_tensor(y[:, :, :, 0], r(0), r(1), ALU.subtract).then_inc(dve_done, V.step(name, "a"))
                    dve.tensor_tensor(y[:, :, :, 1], r(2), r(3), ALU.add).then_inc(dve_done, V.step(name, "b"))
                    dve.wait_ge(dve_done, V[(name, "b")])

                for t in (1, 2):
                    rotate(f"kr{t}", kr[:, t + 1:t + 2, :], g.small[:, t:t + 1, 0:ROPE], 1, t)
                dve.wait_ge(pe_done, PE["cqT"])
                dve.tensor_copy(cqT[:], ps[:, 0:2, 0:TOK]).then_inc(dve_done, V.step("cqT"))
                for t in range(TILES):
                    b = 4 + 2 * (t % 2)
                    dve.wait_ge(pe_done, PE[("q", t)])
                    flat = q[:, t].rearrange("p h e -> p (h e)")
                    dve.tensor_scalar(flat[:, 0:512], ps[:, b, :], SCALE, None, ALU.mult)
                    dve.tensor_scalar(flat[:, 512:MH * QK], ps[:, b + 1, 0:MH * QK - 512], SCALE, None, ALU.mult) \
                        .then_inc(dve_done, V.step("q", t))
                dve.wait_ge(dve_done, V[("q", TILES - 1)])
                for t in (1, 2):
                    rotate(f"q{t}", q[:, t, :, NOPE:QK], q[:, t, :, NOPE:QK], MH, t)
                dve.wait_ge(s_cache, 32)
                for t in range(KT):
                    src = g.small[:, 0, 0:ROPE] if t == 0 else kr[:, t, :]
                    dve.tensor_copy(k[:, t, :, NOPE:QK], over(src, MH, 1)).then_inc(dve_done, V.step("kr", t))
                for t in range(TILES):
                    b = 4 + 2 * (t % 2)
                    dve.wait_ge(pe_done, PE[("qT", t)])
                    dve.tensor_copy(qT[:, :, t * P:(t + 1) * P],
                                    ps[0:QK, b:b + 2, :].rearrange("p b (h e) -> p (b h) e", e=P)) \
                        .then_inc(dve_done, V.step("qT", t))
                for i in range(len(units) + 2):
                    if i < len(units):
                        t, h = units[i]
                        dve.wait_ge(pe_done, PE[("score", i)])
                        dve.tensor_reduce(nmax[:, t, h:h + 1], ps[:, i % 2, 0:nk(t) * P], AX, ALU.max, negate=True) \
                            .then_inc(dve_done, V.step("max", i))
                    if 1 <= i <= len(units):
                        u = i - 1
                        t, h = units[u]
                        dve.wait_ge(pe_done, PE[("probT", u)])
                        if u >= 2:
                            dve.wait_ge(pe_done, PE[("pv", u - 2)])
                        dve.tensor_copy(probT[:, u % 2, 0:nk(t), :].rearrange("p n q -> p (n q)"),
                                        ps[:, 2 + u % 2, 0:nk(t) * P]).then_inc(dve_done, V.step("probT", u))
                dve.wait_ge(act_done, A[("exp", len(units) - 1)])
                dve.reciprocal(rinv[:], rsum[:]).then_inc(dve_done, V.step("rinv"))
                dve.wait_ge(dve_done, V["rinv"])
                dve.wait_ge(pe_done, PE[("pv", len(units) - 1)])
                for t in range(TILES):
                    i = dve.tensor_tensor(g.omla[:, t, :].rearrange("p (h e) -> p h e", h=MH),
                                          ps[:, 4 + t, :].rearrange("p (h e) -> p h e", h=MH),
                                          over(rinv[:, t, :], VH, 2), ALU.mult)
                i.then_inc(dve_done, V.step("o"))


def phase_delta(nc, g):
    a, ps, c, o = g.a, g.ps, g.c, g.o
    H2 = GH // 2
    N48 = 2 * TILES * GH
    DIRS = (0, 1)
    STORE = {0: 1, 1: 0, 2: 1}
    TR = [(t, r) for t in range(TILES) for r in DIRS]
    GROUPS_ = {0: [(0, 0), (0, 1)], 1: [(1, 0), (1, 1), (2, 0), (2, 1)]}
    SCANS = [(grp, n, r) for grp in (0, 1) for n in range(len(GROUPS_[grp])) for r in DIRS]

    def where(grp, n, r):
        seq = GROUPS_[grp]
        return seq[n] if r == 0 else seq[len(seq) - 1 - n]

    with ExitStack() as ctx:
        def sb(name, shape):
            return ctx.enter_context(nc.sbuf_tensor(name, shape, F32))
        ktok = sb("ktok", [P, TILES, GW])
        vtok = sb("vtok", [P, TILES, GW])
        LT = sb("LT", [P, 2, GH, P])
        X = sb("X", [P, 2, GH, P])
        Y = sb("Y", [P, 2, GH, P])
        PR = sb("PR", [P, 2, GH, P])
        kb = sb("kb", [P, 2, GW])
        kbg = sb("kbg", [P, 2, GW])
        vb = sb("vb", [P, 2, GW])
        kbT = LT[:, :, 0:H2, :]
        u = sb("u", [P, 2, 2, GH, DV])
        wT = sb("wT", [P, 2, 2, H2, P])
        aT = sb("aT", [P, 2, 2, GH, P])
        kd = sb("kd", [P, 2, 2, GW])
        S = sb("S", [P, 2, H2, DV])
        flatX = X[:].rearrange("p r h n -> p r (h n)")
        vn = flatX[:, :, 0:GW].rearrange("p r (s e) -> p r s e", s=GH)
        qs = flatX[:, :, GW:2 * GW].rearrange("p r (s e) -> p r s e", s=GH)
        og = g.qkv[:, 8:12, :].rearrange("p m n -> p (m n)")[:, 0:TILES * GW].rearrange(
            "p (t s e) -> p t s e", t=TILES, s=GH)
        sq = X[:].rearrange("p r h n -> p (r h n)")[:, 0:4 * OUTW].rearrange("p (m n) -> p m n", m=4)
        rn = Y[:].rearrange("p r h n -> p (r h n)")[:, 0:4 * OUTW].rearrange("p (m n) -> p m n", m=4)
        sq_out = LT[:].rearrange("p r h n -> p (r h n)")[:, 0:TILES * GW].rearrange(
            "p (t s e) -> p t s e", t=TILES, s=GH)
        arow = sb("arow", [P, 2, 2 * GH])
        gw = sb("gw", [P, 4, TILES, 2 * GH])
        gg = sb("gg", [P, TILES, 2, GH])
        beta = sb("beta", [P, TILES, 2, GH])
        gc = sb("gc", [P, 4, 2, TILES, GH])
        ex = sb("ex", [P, 4, 2, TILES, GH])
        glS = sb("glS", [P, 2, 2 * TILES, H2])
        gnrow = sb("gnrow", [P, DV])
        ostat = sb("ostat", [P, 4, TILES * GH])
        s_row, s_state, s_fin = g.sem("gdn_rows_loaded"), g.sem("state_loaded"), g.sem("state_stored")
        pe_done, dve_done, act_done, pool_done = (g.sem("gdn_" + n) for n in ("pe", "dve", "act", "pool"))

        def scan_after(t):
            return [s for s in SCANS if (s[0] == 0 and t == 0) or (s[0] == 1 and t == 2)]

        pe_o, dve_o, act_o, pool_o = [], [], [], ["state0", "og0"]
        for n in "qk":
            act_o += [("sq", n), ("root", n)]
            pe_o += [("norm", n)]
            dve_o += [("normeps", n), ("normrec", n), ("normed", n)]
        pe_o += ["vtok", "ktok"]
        act_o += ["vtok", "ktok"]
        dve_o += ["xa", "na"]
        act_o += ["expna", "ln", "expa", "expb"]
        dve_o += ["sp", "gg", "b1", "beta"]
        pe_o += ["cums"]
        dve_o += ["gc", "tdiff"]
        act_o += ["ex"]
        dve_o += ["glS"]
        for t in range(TILES):
            for r in DIRS:
                dve_o += [("kb", t, r), ("gtri", t, r)]
                pool_o += [("kbg", t, r), ("vb", t, r), ("kd", t, r)]
                pe_o += [("kbT", t, r), ("D", t, r)]
                act_o += [("kbT", t, r), ("E", t, r)]
            for r in DIRS:
                dve_o += [("D", t, r)]
                pool_o += [("Es", t, r), ("Ei", t, r)]
                pe_o += [("KK", t, r), ("QK", t, r)]
            for r in DIRS:
                dve_o += [("LT", t, r), ("aT", t, r)]
                pe_o += [("L", t, r)]
            for r in DIRS:
                dve_o += [("X1", t, r), ("Y1", t, r)]
                pool_o += [("X1", t, r), ("Y1", t, r)]
            for s in LEVELS[1:]:
                for r in DIRS:
                    pe_o += [("P", t, r, s)]
                    dve_o += [("P", t, r, s)]
                for r in DIRS:
                    if s != LEVELS[-1]:
                        pe_o += [("X", t, r, s)]
                    pe_o += [("Y", t, r, s)]
                for r in DIRS:
                    if s != LEVELS[-1]:
                        dve_o += [("X", t, r, s)]
                    dve_o += [("Y", t, r, s)]
            for r in DIRS:
                pe_o += [("u", t, r), ("wT", t, r)]
                dve_o += [("u", t, r)]
                act_o += [("wT", t, r)]
            for sc in scan_after(t):
                pe_o += [("RQ", sc), ("OU", sc)]
                dve_o += [("vn", sc), ("qs", sc), ("Sg", sc), ("S", sc), ("o1", sc), ("o2", sc)]
        act_o += ["silu", "osq", "ors"]
        dve_o += ["oss", "oms", "orec", "on", "og1", "out"]
        PE, V, A, G = Count(pe_o), Count(dve_o), Count(act_o), Count(pool_o)
        LAST = LEVELS[-1]
        slots = [(par * H2 + j, 2 * j + par, par, j) for par in range(2) for j in range(H2)]
        ctx_done = ("S", (0, 1, 1))

        def by_slot(x):
            return x.rearrange("p (j q) -> p q j", q=2)

        def heads(x):
            return x.rearrange("p (h d) -> p h d", h=GH)

        def banks(b):
            return ps[:, b:b + 2, :].rearrange("p b (j n) -> p (b j) n", j=H2)

        with nc.Block() as block:
            @block.sync
            def _(sp):
                sp.dma_start(arow[:, 0, :], a["a_log"][0].rearrange("r h -> (r h)").partition_broadcast(P)).then_inc(s_row, 16)
                sp.dma_start(arow[:, 1, :], a["dt_bias"][0].rearrange("r h -> (r h)").partition_broadcast(P)) \
                    .then_inc(s_row, 16)
                sp.dma_start(gnrow[:], a["gdn_norm_g"][0].partition_broadcast(P)).then_inc(s_row, 16)

                def state(x, r, par):
                    return x[0, 0, r].rearrange("(j q) k v -> q k j v", q=2)[par]

                sp.wait_ge(dve_done, V[ctx_done])
                for r in DIRS:
                    for par in range(2):
                        sp.dma_start(state(o["state"], r, par), S[par * DK:(par + 1) * DK, r]).then_inc(s_fin, 16)
                sp.wait_ge(s_fin, 64)
                for r in DIRS:
                    for par in range(2):
                        sp.dma_start(S[par * DK:(par + 1) * DK, r], state(a["state_delta"], r, par)).then_inc(s_state, 16)
                sp.wait_ge(s_state, 64)

            @block.gpsimd
            def _(pool):
                pool.memset(S[:], 0.0).then_inc(pool_done, G.step("state0"))
                pool.wait_ge(pe_done, PE["vtok"])
                pool.memset(og, 0.0).then_inc(pool_done, G.step("og0"))
                for t in range(TILES):
                    for r in DIRS:
                        d = STORE[t]
                        if t == 0 and r == 0:
                            pool.wait_ge(act_done, A["ktok"])
                            pool.wait_ge(dve_done, V["glS"])
                        if t:
                            pool.wait_ge(pe_done, PE[("wT", t - 1, 1)])
                        pool.wait_ge(dve_done, V[("kb", t, r)])
                        e = lambda n: over(ex[:, n, r, t, :], DK, 2)
                        pool.tensor_tensor(heads(kbg[:, r]), heads(kb[:, r]), e(0), ALU.mult) \
                            .then_inc(pool_done, G.step("kbg", t, r))
                        pool.tensor_tensor(heads(vb[:, r]), heads(vtok[:, t]), over(beta[:, t, r, :], DV, 2), ALU.mult) \
                            .then_inc(pool_done, G.step("vb", t, r))
                        if t == 2:
                            pool.wait_ge(pe_done, PE[("OU", (0, 1, 1))])
                        pool.tensor_tensor(heads(kd[:, d, r]), heads(ktok[:, t]), e(1), ALU.mult) \
                            .then_inc(pool_done, G.step("kd", t, r))
                    for r in DIRS:
                        pool.wait_ge(act_done, A[("E", t, r)])
                        pool.tensor_tensor(Y[:, r], PR[:, r], over(c[f"strict{r}"], GH, 1), ALU.mult) \
                            .then_inc(pool_done, G.step("Es", t, r))
                        pool.wait_ge(pe_done, PE[("D", t, r)])
                        pool.tensor_tensor(X[:, r], PR[:, r], over(c[f"incl{r}"], GH, 1), ALU.mult) \
                            .then_inc(pool_done, G.step("Ei", t, r))
                    for r in DIRS:
                        for n, Z in (("X1", X), ("Y1", Y)):
                            pool.wait_ge(dve_done, V[(n, t, r)])
                            pool.tensor_tensor(Z[:, r], Z[:, r], over(c["ident"], GH, 1), ALU.add) \
                                .then_inc(pool_done, G.step(n, t, r))

            @block.scalar
            def _(act):
                for i, n in enumerate("qk"):
                    if i:
                        act.wait_ge(pe_done, PE[("norm", "q")])
                    act.activation(sq, g.qkv[:, 4 * i:4 * i + 4, :], ACT.Square).then_inc(act_done, A.step("sq", n))
                    act.wait_ge(dve_done, V[("normrec", n)])
                    act.activation(rn, rn, ACT.Sqrt, scale=1.0 / DK if n == "q" else 1.0) \
                        .then_inc(act_done, A.step("root", n))
                act.wait_ge(pe_done, PE["vtok"])
                act.activation(vtok[:], ps[:, 0:TILES, :], ACT.Copy).then_inc(act_done, A.step("vtok"))
                act.wait_ge(pe_done, PE["ktok"])
                act.activation(ktok[:], ps[:, 3:3 + TILES, :], ACT.Copy).then_inc(act_done, A.step("ktok"))
                act.wait_ge(dve_done, V["na"])
                act.activation(gw[:, 1], gw[:, 1], ACT.Exp).then_inc(act_done, A.step("expna"))
                act.wait_ge(act_done, A["expna"])
                act.activation(gw[:, 2], gw[:, 1], ACT.Ln, bias=1.0).then_inc(act_done, A.step("ln"))
                act.wait_ge(s_row, 48)
                act.activation(arow[:, 0, :], arow[:, 0, :], ACT.Exp).then_inc(act_done, A.step("expa"))
                act.activation(gw[:, 3], g.small[:, :, 48:64], ACT.Exp, scale=-1.0).then_inc(act_done, A.step("expb"))
                act.wait_ge(dve_done, V["tdiff"])
                act.activation(ex[:, 0], gc[:, 0], ACT.Exp)
                act.activation(ex[:, 2:4], gc[:, 2:4], ACT.Exp)
                act.activation(ex[:, 1], ex[:, 1], ACT.Exp).then_inc(act_done, A.step("ex"))
                for t in range(TILES):
                    for r in DIRS:
                        act.wait_ge(pe_done, PE[("kbT", t, r)])
                        act.activation(kbT[:, r].rearrange("p j n -> p (j n)"), ps[:, 4 * r + 2, :], ACT.Copy) \
                            .then_inc(act_done, A.step("kbT", t, r))
                        act.wait_ge(dve_done, V[("D", t, r)])
                        act.activation(PR[:, r], PR[:, r], ACT.Exp).then_inc(act_done, A.step("E", t, r))
                    for r in DIRS:
                        act.wait_ge(pe_done, PE[("wT", t, r)])
                        if t == 2:
                            act.wait_ge(pe_done, PE[("OU", (0, 1, 1))])
                        act.activation(wT[:, STORE[t], r].rearrange("p j n -> p (j n)"), ps[:, 4 * r + 3, :],
                                       ACT.Copy).then_inc(act_done, A.step("wT", t, r))
                act.activation(g.z[:], g.z[:], ACT.Silu).then_inc(act_done, A.step("silu"))
                act.wait_ge(dve_done, V[("o2", SCANS[-1])])
                act.activation(sq_out, og, ACT.Square).then_inc(act_done, A.step("osq"))
                act.wait_ge(dve_done, V["orec"])
                act.activation(ostat[:, 3], ostat[:, 2], ACT.Sqrt).then_inc(act_done, A.step("ors"))

            @block.tensor
            def _(pe):
                for i, n in enumerate("qk"):
                    pe.wait_ge(act_done, A[("sq", n)])
                    for m in range(4):
                        mm = pe.matmul(ps[:, 4 * i + m, 0:OUTW], c["block"], sq[:, m, :], start=True, stop=True)
                    mm.then_inc(pe_done, PE.step("norm", n))
                pe.wait_ge(dve_done, V[("normeps", "q")])
                for t in range(TILES):
                    for m in range(4):
                        mm = pe.transpose(ps[:, t, m * P:(m + 1) * P], g.qkv[:, 8 + m, tok_at(t):tok_at(t) + P],
                                          c["ident"])
                mm.then_inc(pe_done, PE.step("vtok"))
                pe.wait_ge(dve_done, V[("normed", "k")])
                for t in range(TILES):
                    for m in range(4):
                        mm = pe.transpose(ps[:, 3 + t, m * P:(m + 1) * P], g.qkv[:, 4 + m, tok_at(t):tok_at(t) + P],
                                          c["ident"])
                mm.then_inc(pe_done, PE.step("ktok"))
                pe.wait_ge(dve_done, V["gg"])
                gv = gg[:].rearrange("p t r h -> p r t h")
                for r in DIRS:
                    pe.matmul(ps[:, 6, r * 24:(r + 1) * 24], c[f"incl{r}"], gv[:, r], start=True, stop=True)
                for n, m in enumerate(("block", "half0", "half1")):
                    mm = pe.matmul(ps[:, 6, (n + 1) * N48:(n + 2) * N48], c[m], gv, start=True, stop=True)
                mm.then_inc(pe_done, PE.step("cums"))
                for t in range(TILES):
                    tc = slice(tok_at(t), tok_at(t) + P)
                    for r in DIRS:
                        pe.wait_ge(dve_done, V[("kb", t, r)])
                        if t == 0:
                            pe.wait_ge(act_done, A["ktok"])
                            pe.wait_ge(dve_done, V["gc"])
                        else:
                            pe.wait_ge(dve_done, V[("u", t - 1, r)])
                            pe.wait_ge(act_done, A[("wT", t - 1, r)])
                            if t == 1:
                                pe.wait_ge(dve_done, V[("o2", (0, 1, r))])
                        for m in range(H2):
                            mm = pe.transpose(ps[:, 4 * r + 2, m * P:(m + 1) * P], kb[:, r, m * P:(m + 1) * P], c["ident"])
                        mm.then_inc(pe_done, PE.step("kbT", t, r))
                        pe.wait_ge(dve_done, V[("gtri", t, r)])
                        for b in range(2):
                            mm = pe.matmul(ps[:, 4 * r + b, :], c["ones"],
                                           X[:, r, 4 * b:4 * b + 4].rearrange("p h n -> p (h n)"), start=True, stop=True)
                        mm.then_inc(pe_done, PE.step("D", t, r))
                    for r in DIRS:
                        pe.wait_ge(act_done, A[("kbT", t, r)])
                        for s, h, par, j in slots:
                            rows = slice(par * DK, (par + 1) * DK)
                            mm = pe.matmul(ps[:, 4 * r + 2 + par, j * P:(j + 1) * P], g.qkv[rows, 4 + j, tc],
                                           kbT[rows, r, j, :], start=True, stop=True)
                        mm.then_inc(pe_done, PE.step("KK", t, r))
                        pe.wait_ge(dve_done, V[("D", t, r)])
                        for s, h, par, j in slots:
                            rows = slice(par * DK, (par + 1) * DK)
                            mm = pe.matmul(ps[:, 4 * r + par, j * P:(j + 1) * P], g.qkv[rows, 4 + j, tc],
                                           g.qkv[rows, j, tc], start=True, stop=True)
                        mm.then_inc(pe_done, PE.step("QK", t, r))
                    for r in DIRS:
                        pe.wait_ge(dve_done, V[("aT", t, r)])
                        for s, h, par, j in slots:
                            mm = pe.transpose(ps[:, 4 * r + par, j * P:(j + 1) * P], LT[:, r, s, :], c["ident"])
                        mm.then_inc(pe_done, PE.step("L", t, r))
                    for lv in LEVELS[1:]:
                        for r in DIRS:
                            if lv == 2:
                                pe.wait_ge(pool_done, G[("Y1", t, r)])
                            else:
                                pe.wait_ge(dve_done, V[("Y", t, r, lv // 2)])
                            for s, h, par, j in slots:
                                mm = pe.matmul(ps[:, 4 * r + par, j * P:(j + 1) * P], LT[:, r, s, :], X[:, r, s, :],
                                               start=True, stop=True)
                            mm.then_inc(pe_done, PE.step("P", t, r, lv))
                        for r in DIRS:
                            pe.wait_ge(dve_done, V[("P", t, r, lv)])
                            if lv != LAST:
                                for s, h, par, j in slots:
                                    mm = pe.matmul(ps[:, 4 * r + 2 + par, j * P:(j + 1) * P], Y[:, r, s, :],
                                                   PR[:, r, s, :], start=True, stop=True)
                                mm.then_inc(pe_done, PE.step("X", t, r, lv))
                            for s, h, par, j in slots:
                                mm = pe.matmul(ps[:, 4 * r + par, j * P:(j + 1) * P], PR[:, r, s, :], Y[:, r, s, :],
                                               start=True, stop=True)
                            mm.then_inc(pe_done, PE.step("Y", t, r, lv))
                    for r in DIRS:
                        pe.wait_ge(dve_done, V[("Y", t, r, LAST)])
                        pe.wait_ge(pool_done, G[("vb", t, r)])
                        for s, h, par, j in slots:
                            mm = pe.matmul(ps[:, 4 * r + 2, s * DV:(s + 1) * DV], Y[:, r, s, :],
                                           vb[:, r, h * DV:(h + 1) * DV], start=True, stop=True)
                        mm.then_inc(pe_done, PE.step("u", t, r))
                        for s, h, par, j in slots:
                            mm = pe.matmul(ps[par * DK:(par + 1) * DK, 4 * r + 3, j * P:(j + 1) * P],
                                           kbg[:, r, h * DK:(h + 1) * DK], Y[:, r, s, :], start=True, stop=True)
                        mm.then_inc(pe_done, PE.step("wT", t, r))
                    for sc in scan_after(t):
                        grp, n, r = sc
                        st, half = where(*sc)
                        d, lo = STORE[st], half * CHUNK
                        rr = slice(lo, lo + CHUNK)
                        if n == 0:
                            pe.wait_ge(act_done, A[("wT", t, r)])
                            pe.wait_ge(dve_done, V[("u", t, r)])
                            if grp == 0:
                                pe.wait_ge(pool_done, G["state0"])
                            else:
                                pe.wait_ge(s_state, 64)
                        else:
                            pe.wait_ge(dve_done, V[("o2", (grp, n - 1, r))])
                        for s, h, par, j in slots:
                            rows = slice(par * DK, (par + 1) * DK)
                            pe.matmul(ps[rr, 4 * r + par, j * DV:(j + 1) * DV], wT[rows, d, r, j, rr], S[rows, r, j, :],
                                      start=True, stop=True)
                            mm = pe.matmul(ps[rr, 4 * r + par, (H2 + j) * DV:(H2 + j + 1) * DV],
                                           g.qkv[rows, j, tok_at(st) + lo:tok_at(st) + lo + CHUNK], S[rows, r, j, :],
                                           start=True, stop=True)
                        mm.then_inc(pe_done, PE.step("RQ", sc))
                        pe.wait_ge(dve_done, V[("vn", sc)])
                        pe.wait_ge(pool_done, G[("kd", st, r)])
                        for s, h, par, j in slots:
                            pe.matmul(ps[par * DK:(par + 1) * DK, 4 * r + 3, j * DV:(j + 1) * DV],
                                      kd[rr, d, r, h * DK:(h + 1) * DK], vn[rr, r, s, :], start=True, stop=True)
                        for s, h, par, j in slots:
                            mm = pe.matmul(ps[rr, 4 * r + 2, s * DV:(s + 1) * DV], aT[rr, d, r, s, rr], vn[rr, r, s, :],
                                           start=True, stop=True)
                        mm.then_inc(pe_done, PE.step("OU", sc))

            @block.vector
            def _(dve):
                def norm(n):
                    i = "qk".index(n)
                    dve.wait_ge(pe_done, PE[("norm", n)])
                    if i:
                        dve.wait_ge(dve_done, V[("normed", "q")])
                    dve.tensor_scalar(rn, ps[:, 4 * i:4 * i + 4, 0:OUTW], EPS, None, ALU.add) \
                        .then_inc(dve_done, V.step("normeps", n))
                    dve.wait_ge(dve_done, V[("normeps", n)])
                    dve.reciprocal(rn, rn).then_inc(dve_done, V.step("normrec", n))
                    dve.wait_ge(act_done, A[("root", n)])
                    dve.tensor_tensor(g.qkv[:, 4 * i:4 * i + 4, :], g.qkv[:, 4 * i:4 * i + 4, :], rn, ALU.mult) \
                        .then_inc(dve_done, V.step("normed", n))

                norm("q")
                norm("k")
                dve.wait_ge(s_row, 48)
                dve.tensor_tensor(gw[:, 0], g.small[:, :, 32:48], over(arow[:, 1, :], TILES, 1), ALU.add) \
                    .then_inc(dve_done, V.step("xa"))
                dve.wait_ge(dve_done, V["xa"])
                dve.scalar_tensor_tensor(out=gw[:, 1], in0=gw[:, 0], scalar=-1.0, in1=gw[:, 0], op0=ALU.mult,
                                         op1=ALU.min).then_inc(dve_done, V.step("na"))
                dve.wait_ge(act_done, A["expb"])
                dve.scalar_tensor_tensor(out=gw[:, 2], in0=gw[:, 0], scalar=0.0, in1=gw[:, 2], op0=ALU.max,
                                         op1=ALU.add).then_inc(dve_done, V.step("sp"))
                dve.wait_ge(dve_done, V["sp"])
                dve.scalar_tensor_tensor(out=gg[:].rearrange("p t r h -> p t (r h)"), in0=gw[:, 2], scalar=-1.0,
                                         in1=over(arow[:, 0, :], TILES, 1), op0=ALU.mult, op1=ALU.mult) \
                    .then_inc(dve_done, V.step("gg"))
                dve.tensor_scalar(gw[:, 3], gw[:, 3], 1.0, None, ALU.add).then_inc(dve_done, V.step("b1"))
                dve.wait_ge(dve_done, V["b1"])
                dve.reciprocal(beta[:].rearrange("p t r h -> p t (r h)"), gw[:, 3]).then_inc(dve_done, V.step("beta"))
                dve.wait_ge(pe_done, PE["cums"])
                dve.tensor_copy(gc[:].rearrange("p n r t h -> p (n r t h)"), ps[:, 6, 0:4 * N48]) \
                    .then_inc(dve_done, V.step("gc"))
                dve.wait_ge(dve_done, V["gc"])
                dve.tensor_tensor(ex[:, 1], gc[:, 1], gc[:, 0], ALU.subtract).then_inc(dve_done, V.step("tdiff"))
                dve.wait_ge(act_done, A["ex"])
                for par in range(2):
                    rows = slice(par * DK, (par + 1) * DK)
                    i = dve.tensor_copy(glS[rows], ex[rows, 2:4, :, :, par::2].rearrange("p n r t j -> p n (r t) j"))
                i.then_inc(dve_done, V.step("glS"))
                for t in range(TILES):
                    d = STORE[t]
                    for r in DIRS:
                        if t == 0:
                            dve.wait_ge(act_done, A["ktok"])
                            dve.wait_ge(dve_done, V["glS"])
                        else:
                            dve.wait_ge(pool_done, G[("kbg", t - 1, r)])
                            dve.wait_ge(pe_done, PE[("wT", t - 1, 1)])
                            if t == 1:
                                dve.wait_ge(pe_done, PE[("OU", (0, 1, 1))])
                                dve.wait_ge(dve_done, V[("o2", (0, 1, 1))])
                        dve.tensor_tensor(heads(kb[:, r]), heads(ktok[:, t]), over(beta[:, t, r, :], DK, 2), ALU.mult) \
                            .then_inc(dve_done, V.step("kb", t, r))
                        for par in range(2):
                            i = dve.tensor_tensor(X[:, r, par * H2:(par + 1) * H2], over(c[f"incl{r}"], H2, 1),
                                                  over(gg[:, t, r, par::2], P, 2), ALU.mult)
                        i.then_inc(dve_done, V.step("gtri", t, r))
                    for r in DIRS:
                        dve.wait_ge(pe_done, PE[("D", t, r)])
                        for s, h, par, j in slots:
                            i = dve.tensor_scalar(PR[:, r, s, :], ps[:, 4 * r + par, j * P:(j + 1) * P],
                                                  gc[:, 0, r, t, h:h + 1], 0.0, ALU.subtract, ALU.min)
                        i.then_inc(dve_done, V.step("D", t, r))
                    for r in DIRS:
                        dve.wait_ge(pe_done, PE[("KK", t, r)])
                        dve.wait_ge(pool_done, G[("Es", t, r)])
                        dve.tensor_tensor(LT[:, r], banks(4 * r + 2), Y[:, r], ALU.mult) \
                            .then_inc(dve_done, V.step("LT", t, r))
                        dve.wait_ge(pe_done, PE[("QK", t, r)])
                        dve.wait_ge(pool_done, G[("Ei", t, r)])
                        if t == 2:
                            dve.wait_ge(pe_done, PE[("OU", (0, 1, 1))])
                        dve.tensor_tensor(aT[:, d, r], banks(4 * r), X[:, r], ALU.mult) \
                            .then_inc(dve_done, V.step("aT", t, r))
                    for r in DIRS:
                        dve.wait_ge(pe_done, PE[("L", t, r)])
                        dve.wait_ge(dve_done, V[("aT", t, r)])
                        dve.scalar_tensor_tensor(out=X[:, r], in0=banks(4 * r), scalar=-1.0,
                                                 in1=over(c[f"level{r}_1"], GH, 1), op0=ALU.mult, op1=ALU.mult) \
                            .then_inc(dve_done, V.step("X1", t, r))
                        dve.scalar_tensor_tensor(out=Y[:, r], in0=LT[:, r], scalar=-1.0,
                                                 in1=over(c[f"level{1 - r}_1"], GH, 1), op0=ALU.mult, op1=ALU.mult) \
                            .then_inc(dve_done, V.step("Y1", t, r))
                    for lv in LEVELS[1:]:
                        for r in DIRS:
                            dve.wait_ge(pe_done, PE[("P", t, r, lv)])
                            dve.tensor_tensor(PR[:, r], banks(4 * r), over(c[f"level{r}_{lv}"], GH, 1), ALU.mult) \
                                .then_inc(dve_done, V.step("P", t, r, lv))
                        for r in DIRS:
                            if lv != LAST:
                                dve.wait_ge(pe_done, PE[("Y", t, r, lv)])
                                dve.tensor_tensor(X[:, r], X[:, r], banks(4 * r + 2), ALU.subtract) \
                                    .then_inc(dve_done, V.step("X", t, r, lv))
                            dve.wait_ge(pe_done, PE[("Y", t, r, lv)])
                            dve.tensor_tensor(Y[:, r], Y[:, r], banks(4 * r), ALU.subtract) \
                                .then_inc(dve_done, V.step("Y", t, r, lv))
                    for r in DIRS:
                        dve.wait_ge(pe_done, PE[("u", t, r)])
                        dve.tensor_copy(u[:, d, r].rearrange("p s e -> p (s e)"), ps[:, 4 * r + 2, :]) \
                            .then_inc(dve_done, V.step("u", t, r))
                    for sc in scan_after(t):
                        grp, n, r = sc
                        st, half = where(*sc)
                        sd, rr = STORE[st], slice(half * CHUNK, (half + 1) * CHUNK)
                        pair = lambda lo: ps[rr, 4 * r:4 * r + 2, lo:lo + H2 * DV].rearrange(
                            "p b (j e) -> p b j e", j=H2)
                        sl = lambda x: x.rearrange("p (q j) e -> p q j e", q=2)
                        dve.wait_ge(pe_done, PE[("RQ", sc)])
                        dve.tensor_tensor(sl(vn[rr, r]), sl(u[rr, sd, r]), pair(0), ALU.subtract) \
                            .then_inc(dve_done, V.step("vn", sc))
                        for par in range(2):
                            i = dve.tensor_tensor(qs[rr, r, par * H2:(par + 1) * H2],
                                                  ps[rr, 4 * r + par, H2 * DV:2 * H2 * DV].rearrange(
                                                      "p (j e) -> p j e", j=H2),
                                                  over(ex[rr, 0, r, st, par::2], DV, 2), ALU.mult)
                        i.then_inc(dve_done, V.step("qs", sc))
                        dve.tensor_tensor(S[:, r], S[:, r], over(glS[:, half, r * TILES + st, :], DV, 2), ALU.mult) \
                            .then_inc(dve_done, V.step("Sg", sc))
                        dve.wait_ge(pe_done, PE[("OU", sc)])
                        dve.wait_ge(dve_done, V[("Sg", sc)])
                        dve.tensor_tensor(S[:, r], S[:, r], ps[:, 4 * r + 3, 0:H2 * DV].rearrange(
                            "p (j e) -> p j e", j=H2), ALU.add).then_inc(dve_done, V.step("S", sc))
                        dve.wait_ge(pool_done, G["og0"])
                        dve.tensor_tensor(qs[rr, r], qs[rr, r], ps[rr, 4 * r + 2, :].rearrange(
                            "p (s e) -> p s e", s=GH), ALU.add).then_inc(dve_done, V.step("o1", sc))
                        dve.wait_ge(dve_done, V[("o1", sc)])
                        dve.tensor_tensor(og[rr, st], og[rr, st], qs[rr, r], ALU.add) \
                            .then_inc(dve_done, V.step("o2", sc))
                flat = og.rearrange("p t s e -> p (t s) e")
                dve.wait_ge(act_done, A["osq"])
                dve.tensor_reduce(ostat[:, 0], sq_out.rearrange("p t s e -> p (t s) e"), AX, ALU.add) \
                    .then_inc(dve_done, V.step("oss"))
                dve.wait_ge(dve_done, V["oss"])
                dve.tensor_scalar(ostat[:, 1], ostat[:, 0], 1.0 / DV, EPS, ALU.mult, ALU.add) \
                    .then_inc(dve_done, V.step("oms"))
                dve.wait_ge(dve_done, V["oms"])
                dve.reciprocal(ostat[:, 2], ostat[:, 1]).then_inc(dve_done, V.step("orec"))
                dve.wait_ge(act_done, A["ors"])
                dve.tensor_tensor(flat, flat, over(ostat[:, 3], DV, 2), ALU.mult).then_inc(dve_done, V.step("on"))
                dve.wait_ge(dve_done, V["on"])
                dve.tensor_tensor(flat, flat, over(gnrow[:], TILES * GH, 1), ALU.mult).then_inc(dve_done, V.step("og1"))
                dve.wait_ge(dve_done, V["og1"])
                for t in range(TILES):
                    zt = g.z[:, t].rearrange("p (j q e) -> p q j e", j=H2, q=2)
                    i = dve.tensor_tensor(zt, zt, og[:, t].rearrange("p (q j) e -> p q j e", q=2), ALU.mult)
                i.then_inc(dve_done, V.step("out"))


def phase_merge(nc, g):
    a, ps, c = g.a, g.ps, g.c
    KO = GW // P
    with ExitStack() as ctx:
        def sb(name, shape):
            return ctx.enter_context(nc.sbuf_tensor(name, shape, F32))
        wo2 = sb("wo2", [P, 2, KO, D])
        wo = sb("wo", [P, KD, D])
        oT = sb("oT", [P, 2, KO, TOK])
        sg = sb("sg", [P, 2, 2, 512])
        merged = sb("merged", [P, TILES, D])
        gate = sb("gate", [P, 2, D])
        gpost = sb("gpost", [P, D])
        stat = sb("mstat", [P, 4, TILES])
        mT = g.hT
        s_wo2, s_wo, s_x, s_row = (g.sem(n) for n in ("wo2_loaded", "wo_loaded", "x_again_loaded", "gate1_loaded"))
        pe_done, dve_done, act_done, pool_done = (g.sem("merge_" + n) for n in ("pe", "dve", "act", "pool"))
        units = [(n, t) for n in range(2) for t in range(TILES)]
        PE = Count([("oT", w, t) for w in range(2) for t in range(TILES)]
                   + [(x, u) for u in units for x in ("y", "g")]
                   + [("mT", t) for t in range(TILES)] + [("o", t) for t in range(TILES)])
        A = Count([("oT", w, t) for w in range(2) for t in range(TILES)] + [("sig", u) for u in units]
                  + [("mT", t) for t in range(TILES)] + [("ss", t) for t in range(TILES)] + ["rs"])
        V = Count([(x, u) for u in units for x in ("a", "b")] + ["ms", "rec"]
                  + [(x, t) for t in range(TILES) for x in ("yn", "x1")])
        G = Count(["gate"] + [("sum", u) for u in units])
        with nc.Block() as block:
            @block.sync
            def _(sp):
                sp.dma_start(wo2[:, 0], a["w_oa"][0].rearrange("(p k) n -> p k n", k=KO)).then_inc(s_wo2, 16)
                sp.dma_start(wo2[:, 1], a["w_ob"][0].rearrange("(p k) n -> p k n", k=KO)).then_inc(s_wo2, 16)
                for v in range(2):
                    sp.dma_start(gate[:, v], g.mods_dram[v, 2].partition_broadcast(P)).then_inc(s_row, 16)
                sp.dma_start(gpost[:], a["g_post_mix"][0].partition_broadcast(P)).then_inc(s_row, 16)
                sp.dma_start(wo[:], a["w_o"][0].rearrange("(p k) n -> p k n", k=KD)).then_inc(s_wo, 16)
                sp.dma_start(g.x1[:, 0, :], a["x_prompt"][0]).then_inc(s_x, 16)
                sp.dma_start(g.x1[:, 1:3, :], a["x_sample"][0].rearrange("(t p) d -> p t d", p=P)).then_inc(s_x, 16)
                n = LOAD["gb1"]
                sp.wait_ge(pe_done, PE[("g", (0, TILES - 1))])
                sp.dma_start(g.ring[:, slot(n)], ring_source(g, n)).then_inc(g.s_slot[slot(n)], 16)

            @block.gpsimd
            def _(pool):
                pool.wait_ge(s_row, 48)
                pool.tensor_tensor(gate[:], gate[:], over(gpost[:], 2, 1), ALU.mult).then_inc(pool_done, G.step("gate"))
                for i, (n, t) in enumerate(units):
                    pool.wait_ge(dve_done, V[("b", (n, t))])
                    pool.tensor_tensor(merged[:, t, n * 512:(n + 1) * 512], sg[:, i % 2, 0, :], sg[:, i % 2, 1, :],
                                       ALU.add).then_inc(pool_done, G.step("sum", (n, t)))

            @block.scalar
            def _(act):
                for w in range(2):
                    for t in range(TILES):
                        act.wait_ge(pe_done, PE[("oT", w, t)])
                        act.activation(oT[:, w, :, t * P:(t + 1) * P],
                                       ps[:, 3 * w + t, :].rearrange("p (k n) -> p k n", k=KO), ACT.Copy) \
                            .then_inc(act_done, A.step("oT", w, t))
                for i, u in enumerate(units):
                    b = 4 * (i % 2)
                    act.wait_ge(pe_done, PE[("g", u)])
                    if i >= 2:
                        act.wait_ge(pool_done, G[("sum", units[i - 2])])
                    act.activation(sg[:, i % 2], ps[:, b + 2:b + 4, :], ACT.Sigmoid).then_inc(act_done, A.step("sig", u))
                for t in range(TILES):
                    act.wait_ge(pe_done, PE[("mT", t)])
                    act.activation(mT[:, :, t * P:(t + 1) * P],
                                   ps[:, 2 * t:2 * t + 2, :].rearrange("p b (k n) -> p (b k) n", k=4), ACT.Copy) \
                        .then_inc(act_done, A.step("mT", t))
                for t in range(TILES):
                    b = (6, 0, 2)[t]
                    act.wait_ge(pe_done, PE[("o", t)])
                    act.activation(merged[:, t, :].rearrange("p (b n) -> p b n", b=2), ps[:, b:b + 2, :], ACT.Square,
                                   accum_out=stat[:, 0, t:t + 1]).then_inc(act_done, A.step("ss", t))
                act.wait_ge(dve_done, V["rec"])
                act.activation(stat[:, 3], stat[:, 2], ACT.Sqrt).then_inc(act_done, A.step("rs"))

            @block.tensor
            def _(pe):
                for w, src in enumerate((g.omla, g.z)):
                    for t in range(TILES):
                        for k in range(KO):
                            mm = pe.transpose(ps[:, 3 * w + t, k * P:(k + 1) * P], src[:, t, k::KO], c["ident"])
                        mm.then_inc(pe_done, PE.step("oT", w, t))
                pe.wait_ge(s_wo2, 32)
                pe.wait_ge(act_done, A[("oT", 1, TILES - 1)])
                for i, (n, t) in enumerate(units):
                    b = 4 * (i % 2)
                    if i >= 2:
                        pe.wait_ge(dve_done, V[("b", units[i - 2])])
                    for w in range(2):
                        for k in range(KO):
                            mm = pe.matmul(ps[:, b + w, :], oT[:, w, k, t * P:(t + 1) * P],
                                           wo2[:, w, k, n * 512:(n + 1) * 512], start=(k == 0), stop=(k == KO - 1))
                    mm.then_inc(pe_done, PE.step("y", (n, t)))
                    for w, name in enumerate((f"ga{n}", f"gb{n}")):
                        m = LOAD[name]
                        pe.wait_ge(g.s_slot[slot(m)], loaded(m))
                        for k in range(KD):
                            mm = pe.matmul(ps[:, b + 2 + w, :], g.hT[:, k, t * P:(t + 1) * P], g.ring[:, slot(m), k, :],
                                           start=(k == 0), stop=(k == KD - 1))
                    mm.then_inc(pe_done, PE.step("g", (n, t)))
                for t in range(TILES):
                    pe.wait_ge(pool_done, G[("sum", (1, t))])
                    pe.wait_ge(dve_done, V[("b", (1, TILES - 1))])
                    for k in range(KD):
                        mm = pe.transpose(ps[:, 2 * t + k // 4, (k % 4) * P:(k % 4 + 1) * P], merged[:, t, k::KD],
                                          c["ident"])
                    mm.then_inc(pe_done, PE.step("mT", t))
                pe.wait_ge(s_wo, 16)
                for t in range(TILES):
                    b = (6, 0, 2)[t]
                    pe.wait_ge(act_done, A[("mT", t)])
                    for n in range(2):
                        for k in range(KD):
                            mm = pe.matmul(ps[:, b + n, :], mT[:, k, t * P:(t + 1) * P], wo[:, k, n * 512:(n + 1) * 512],
                                           start=(k == 0), stop=(k == KD - 1))
                    mm.then_inc(pe_done, PE.step("o", t))

            @block.vector
            def _(dve):
                for i, u in enumerate(units):
                    b = 4 * (i % 2)
                    dve.wait_ge(act_done, A[("sig", u)])
                    dve.tensor_tensor(sg[:, i % 2, 0, :], sg[:, i % 2, 0, :], ps[:, b, :], ALU.mult) \
                        .then_inc(dve_done, V.step("a", u))
                    dve.tensor_tensor(sg[:, i % 2, 1, :], sg[:, i % 2, 1, :], ps[:, b + 1, :], ALU.mult) \
                        .then_inc(dve_done, V.step("b", u))
                dve.wait_ge(act_done, A[("ss", TILES - 1)])
                dve.tensor_scalar(stat[:, 1], stat[:, 0], 1.0 / D, EPS, ALU.mult, ALU.add).then_inc(dve_done, V.step("ms"))
                dve.wait_ge(dve_done, V["ms"])
                dve.reciprocal(stat[:, 2], stat[:, 1]).then_inc(dve_done, V.step("rec"))
                dve.wait_ge(act_done, A["rs"])
                dve.wait_ge(pool_done, G["gate"])
                dve.wait_ge(s_x, 32)
                for t in range(TILES):
                    b = (6, 0, 2)[t]
                    mt = merged[:, t, :].rearrange("p (b n) -> p b n", b=2)
                    dve.scalar_tensor_tensor(out=mt, in0=ps[:, b:b + 2, :], scalar=stat[:, 3, t:t + 1],
                                             in1=gate[:, min(t, 1)].rearrange("p (b n) -> p b n", b=2),
                                             op0=ALU.mult, op1=ALU.mult).then_inc(dve_done, V.step("yn", t))
                    dve.wait_ge(dve_done, V[("yn", t)])
                    dve.tensor_tensor(g.x1[:, t, :], g.x1[:, t, :], merged[:, t, :], ALU.add) \
                        .then_inc(dve_done, V.step("x1", t))


def phase_route(nc, g):
    a, ps, c = g.a, g.ps, g.c
    E = EXPERTS
    with ExitStack() as ctx:
        def sb(name, shape, dt=F32):
            return ctx.enter_context(nc.sbuf_tensor(name, shape, dt))
        rows = sb("rows", [P, 2, 2, D])
        gpre = sb("gpre2", [P, D])
        wr = sb("wr", [P, KD, E])
        ebias = sb("ebias", [P, E])
        stat = sb("rstat", [P, 4, TILES])
        s = sb("score", [P, TILES, E])
        sel = sb("sel", [P, TILES, E])
        m8 = sb("m8", [P, TILES, GROUPS, 8])
        grp = sb("grp", [P, TILES, GROUPS])
        cmp = sb("cmp", [P, 2, TILES, GROUPS * GROUPS])
        rank = sb("rank", [P, 3, TILES, GROUPS])
        top = sb("top", [P, TILES, 8])
        rep = sb("rep", [P, TILES, E])
        gsum = sb("gsum", [P, 2, TILES])
        pmax = sb("pmax", [P, 1])
        nf = sb("nf", [1, 4])
        wsg = sb("wsg", [P, 2, KD, FE])
        wsd = sb("wsd", [P, KF, D])
        sact = sb("sact", [P, 2, FE])
        sactT = sb("sactT", [P, 2, KF, P])
        s_row, s_wr, s_ws = g.sem("ffn_rows_loaded"), g.sem("router_loaded"), g.sem("shared_loaded")
        pe_done, dve_done, act_done, pool_done = (g.sem("route_" + n) for n in ("pe", "dve", "act", "pool"))
        T = range(TILES)
        PE = Count([("hT", t) for t in T] + [("logit", t) for t in T] + [("gu", 0), ("gu", 1), ("pos", 0), ("pos", 1),
                   ("pos", 2), "pmaxT", ("actT", 0), ("y", 0), ("gu", 2), ("actT", 1), ("y", 1), ("actT", 2), ("y", 2)])
        A = Count([("ss", t) for t in T] + ["rs"] + [("hT", t) for t in T] + ["sig"]
                  + [x for t in T for x in (("silu", t), ("actT", t), ("y", t))])
        V = Count(["ms", "rec", "A"] + [x for t in T for x in (("h0", t), ("h", t))]
                  + ["sel", "m8", "grp", "gt", "eq", "eqe", "cmp", "rank", "gm", "pen", "selm0", "selm", "top",
                     "rep", "mask", "gs", "gsum", "grec", "gates", ("act", 0), "pos", "pmax", "nmax", "n1", "n2", "n3",
                     ("act", 1), ("act", 2)])
        with nc.Block() as block:
            @block.sync
            def _(sp):
                for v in range(2):
                    for m in range(2):
                        sp.dma_start(rows[:, v, m], g.mods_dram[v, 3 + m].partition_broadcast(P)).then_inc(s_row, 16)
                sp.dma_start(gpre[:], a["g_pre_ffn"][0].partition_broadcast(P)).then_inc(s_row, 16)
                sp.dma_start(wr[:], a["w_router"][0].rearrange("(p k) n -> p k n", k=KD)).then_inc(s_wr, 16)
                sp.dma_start(ebias[:], a["e_bias"][0].partition_broadcast(P)).then_inc(s_wr, 16)
                sp.dma_start(wsg[:, 0], a["ws_gate"][0].rearrange("(p k) n -> p k n", k=KD)).then_inc(s_ws, 16)
                sp.dma_start(wsg[:, 1], a["ws_up"][0].rearrange("(p k) n -> p k n", k=KD)).then_inc(s_ws, 16)
                sp.dma_start(wsd[:], a["ws_down"][0].rearrange("(p k) n -> p k n", k=KF)).then_inc(s_ws, 16)

            @block.scalar
            def _(act):
                for t in T:
                    act.activation(g.h2[:, t, :], g.x1[:, t, :], ACT.Square, accum_out=stat[:, 0, t:t + 1]) \
                        .then_inc(act_done, A.step("ss", t))
                act.wait_ge(dve_done, V["rec"])
                act.activation(stat[:, 3], stat[:, 2], ACT.Sqrt).then_inc(act_done, A.step("rs"))
                for t in T:
                    act.wait_ge(pe_done, PE[("hT", t)])
                    act.activation(g.hT[:, :, t * P:(t + 1) * P],
                                   ps[:, 2 * t:2 * t + 2, :].rearrange("p b (k n) -> p (b k) n", k=4), ACT.Copy) \
                        .then_inc(act_done, A.step("hT", t))
                act.wait_ge(pe_done, PE[("logit", 2)])
                act.activation(s[:].rearrange("p t e -> p (t e)"), ps[:, 6, 0:TILES * E], ACT.Sigmoid) \
                    .then_inc(act_done, A.step("sig"))
                for t in T:
                    act.wait_ge(pe_done, PE[("gu", t)])
                    if t == 2:
                        act.wait_ge(dve_done, V[("act", 0)])
                        act.wait_ge(pe_done, PE[("actT", 0)])
                    act.activation(sact[:, t % 2], ps[:, t % 2, 0:FE], ACT.Silu).then_inc(act_done, A.step("silu", t))
                    act.wait_ge(pe_done, PE[("actT", t)])
                    act.activation(sactT[:, t % 2].rearrange("p j n -> p (j n)"), ps[:, 3, 0:KF * P], ACT.Copy) \
                        .then_inc(act_done, A.step("actT", t))
                    act.wait_ge(pe_done, PE[("y", t)])
                    act.activation(g.y[:, t, :].rearrange("p (b n) -> p b n", b=2), ps[:, 4:6, :], ACT.Copy) \
                        .then_inc(act_done, A.step("y", t))

            @block.tensor
            def _(pe):
                for t in T:
                    pe.wait_ge(dve_done, V[("h", t)])
                    for k in range(KD):
                        mm = pe.transpose(ps[:, 2 * t + k // 4, (k % 4) * P:(k % 4 + 1) * P], g.h2[:, t, k::KD],
                                          c["ident"])
                    mm.then_inc(pe_done, PE.step("hT", t))
                pe.wait_ge(s_wr, 32)
                for t in T:
                    pe.wait_ge(act_done, A[("hT", t)])
                    for k in range(KD):
                        mm = pe.matmul(ps[:, 6, t * E:(t + 1) * E], g.hT[:, k, t * P:(t + 1) * P], wr[:, k, :],
                                       start=(k == 0), stop=(k == KD - 1))
                    mm.then_inc(pe_done, PE.step("logit", t))
                pe.wait_ge(s_ws, 48)

                def gate_up(t):
                    for k in range(KD):
                        mm = pe.matmul(ps[:, t % 2, :], g.hT[:, k, t * P:(t + 1) * P], wsg[:, :, k, :],
                                       start=(k == 0), stop=(k == KD - 1))
                    mm.then_inc(pe_done, PE.step("gu", t))

                def down(t):
                    pe.wait_ge(dve_done, V[("act", t)])
                    if t:
                        pe.wait_ge(act_done, A[("actT", t - 1)])
                    for j in range(KF):
                        mm = pe.transpose(ps[:, 3, j * P:(j + 1) * P], sact[:, t % 2, j::KF], c["ident"])
                    mm.then_inc(pe_done, PE.step("actT", t))
                    pe.wait_ge(act_done, A[("actT", t)])
                    if t:
                        pe.wait_ge(act_done, A[("y", t - 1)])
                    for n in range(2):
                        for j in range(KF):
                            mm = pe.matmul(ps[:, 4 + n, :], sactT[:, t % 2, j, :], wsd[:, j, n * 512:(n + 1) * 512],
                                           start=(j == 0), stop=(j == KF - 1))
                    mm.then_inc(pe_done, PE.step("y", t))

                gate_up(0)
                gate_up(1)
                pe.wait_ge(dve_done, V["mask"])
                for t in T:
                    for q in range(t + 1):
                        mm = pe.matmul(ps[:, 7, t * E:(t + 1) * E], c["before" if q == t else "ones"], rep[:, q, :],
                                       start=(q == 0), stop=(q == t))
                    mm.then_inc(pe_done, PE.step("pos", t))
                pe.wait_ge(dve_done, V["pmax"])
                pe.transpose(ps[0:1, 2, 0:P], pmax[:], c["ident"]).then_inc(pe_done, PE.step("pmaxT"))
                down(0)
                gate_up(2)
                down(1)
                down(2)

            @block.vector
            def _(dve):
                dve.wait_ge(act_done, A[("ss", 2)])
                dve.tensor_scalar(stat[:, 1], stat[:, 0], 1.0 / D, EPS, ALU.mult, ALU.add).then_inc(dve_done, V.step("ms"))
                dve.wait_ge(dve_done, V["ms"])
                dve.reciprocal(stat[:, 2], stat[:, 1]).then_inc(dve_done, V.step("rec"))
                dve.wait_ge(s_row, 80)
                dve.scalar_tensor_tensor(out=rows[:, :, 1, :], in0=rows[:, :, 1, :], scalar=1.0, in1=over(gpre[:], 2, 1),
                                         op0=ALU.add, op1=ALU.mult).then_inc(dve_done, V.step("A"))
                dve.wait_ge(act_done, A["rs"])
                dve.wait_ge(dve_done, V["A"])
                for t in T:
                    v = min(t, 1)
                    dve.scalar_tensor_tensor(out=g.h2[:, t, :], in0=g.x1[:, t, :], scalar=stat[:, 3, t:t + 1],
                                             in1=rows[:, v, 1, :], op0=ALU.mult, op1=ALU.mult) \
                        .then_inc(dve_done, V.step("h0", t))
                    dve.wait_ge(dve_done, V[("h0", t)])
                    dve.tensor_tensor(g.h2[:, t, :], g.h2[:, t, :], rows[:, v, 0, :], ALU.add) \
                        .then_inc(dve_done, V.step("h", t))
                dve.wait_ge(act_done, A["sig"])
                dve.tensor_tensor(sel[:], s[:], over(ebias[:], TILES, 1), ALU.add).then_inc(dve_done, V.step("sel"))
                dve.wait_ge(dve_done, V["sel"])
                for t in T:
                    for q in range(GROUPS):
                        i = dve.max(m8[:, t, q, :], sel[:, t, q * PER:(q + 1) * PER])
                i.then_inc(dve_done, V.step("m8"))
                dve.wait_ge(dve_done, V["m8"])
                dve.tensor_tensor(grp[:], m8[:, :, :, 0], m8[:, :, :, 1], ALU.add).then_inc(dve_done, V.step("grp"))
                dve.wait_ge(dve_done, V["grp"])
                sq = lambda x: x.rearrange("p t (i j) -> p t i j", i=GROUPS)
                dve.tensor_tensor(sq(cmp[:, 0]), over(grp[:], GROUPS, 2), over(grp[:], GROUPS, 3), ALU.is_gt) \
                    .then_inc(dve_done, V.step("gt"))
                dve.tensor_tensor(sq(cmp[:, 1]), over(grp[:], GROUPS, 2), over(grp[:], GROUPS, 3), ALU.is_equal) \
                    .then_inc(dve_done, V.step("eq"))
                dve.wait_ge(dve_done, V["eq"])
                dve.tensor_tensor(cmp[:, 1], cmp[:, 1], over(c["earlier"], TILES, 1), ALU.mult) \
                    .then_inc(dve_done, V.step("eqe"))
                dve.wait_ge(dve_done, V["eqe"])
                dve.tensor_tensor(cmp[:, 0], cmp[:, 0], cmp[:, 1], ALU.add).then_inc(dve_done, V.step("cmp"))
                dve.wait_ge(dve_done, V["cmp"])
                dve.tensor_reduce(rank[:, 0], sq(cmp[:, 0]), AX, ALU.add).then_inc(dve_done, V.step("rank"))
                dve.wait_ge(dve_done, V["rank"])
                dve.tensor_scalar(rank[:, 1], rank[:, 0], TOPG - 0.5, None, ALU.is_lt).then_inc(dve_done, V.step("gm"))
                dve.wait_ge(dve_done, V["gm"])
                dve.tensor_scalar(rank[:, 2], rank[:, 1], 1e30, -1e30, ALU.mult, ALU.add).then_inc(dve_done, V.step("pen"))
                per = lambda x: x.rearrange("p t (q e) -> p t q e", q=GROUPS)
                dve.tensor_tensor(per(sel[:]), per(sel[:]), over(rank[:, 1], PER, 3), ALU.mult) \
                    .then_inc(dve_done, V.step("selm0"))
                dve.wait_ge(dve_done, V["selm0"])
                dve.tensor_tensor(per(sel[:]), per(sel[:]), over(rank[:, 2], PER, 3), ALU.add) \
                    .then_inc(dve_done, V.step("selm"))
                dve.wait_ge(dve_done, V["selm"])
                for t in T:
                    i = dve.max(top[:, t, :], sel[:, t, :])
                i.then_inc(dve_done, V.step("top"))
                dve.wait_ge(dve_done, V["top"])
                for t in T:
                    i = dve.match_replace(rep[:, t, :], top[:, t, :], sel[:, t, :], -3e38)
                i.then_inc(dve_done, V.step("rep"))
                dve.wait_ge(dve_done, V["rep"])
                dve.tensor_tensor(rep[:], rep[:], sel[:], ALU.not_equal).then_inc(dve_done, V.step("mask"))
                dve.wait_ge(dve_done, V["mask"])
                dve.tensor_tensor(s[:], s[:], rep[:], ALU.mult).then_inc(dve_done, V.step("gs"))
                dve.wait_ge(dve_done, V["gs"])
                dve.tensor_reduce(gsum[:, 0], s[:], AX, ALU.add).then_inc(dve_done, V.step("gsum"))
                dve.wait_ge(dve_done, V["gsum"])
                dve.reciprocal(gsum[:, 1], gsum[:, 0]).then_inc(dve_done, V.step("grec"))
                dve.wait_ge(dve_done, V["grec"])
                for t in T:
                    i = dve.tensor_scalar(g.gates[:, t, :], s[:, t, :], gsum[:, 1, t:t + 1], ROUTED, ALU.mult, ALU.mult)
                i.then_inc(dve_done, V.step("gates"))

                def shared_act(t):
                    dve.wait_ge(act_done, A[("silu", t)])
                    dve.tensor_tensor(sact[:, t % 2], sact[:, t % 2], ps[:, t % 2, FE:2 * FE], ALU.mult) \
                        .then_inc(dve_done, V.step("act", t))

                shared_act(0)
                dve.wait_ge(pe_done, PE[("pos", 2)])
                flat = lambda x: x[:].rearrange("p t e -> p (t e)")
                dve.scalar_tensor_tensor(out=flat(g.pos), in0=ps[:, 7, 0:TILES * E], scalar=1.0, in1=flat(rep),
                                         op0=ALU.add, op1=ALU.mult).then_inc(dve_done, V.step("pos"))
                dve.wait_ge(dve_done, V["pos"])
                dve.tensor_reduce(pmax[:], flat(g.pos), AX, ALU.max).then_inc(dve_done, V.step("pmax"))
                dve.wait_ge(pe_done, PE["pmaxT"])
                dve.tensor_reduce(nf[:, 0:1], ps[0:1, 2, 0:P], AX, ALU.max).then_inc(dve_done, V.step("nmax"))
                dve.wait_ge(dve_done, V["nmax"])
                dve.tensor_scalar(nf[:, 1:2], nf[:, 0:1], P + 0.5, None, ALU.is_gt).then_inc(dve_done, V.step("n1"))
                dve.tensor_scalar(nf[:, 2:3], nf[:, 0:1], 2 * P + 0.5, 1.0, ALU.is_gt, ALU.add) \
                    .then_inc(dve_done, V.step("n2"))
                dve.wait_ge(dve_done, V["n2"])
                dve.tensor_tensor(g.passes[:], nf[:, 1:2], nf[:, 2:3], ALU.add).then_inc(dve_done, V.step("n3"))
                shared_act(1)
                shared_act(2)


class Each:

    def __init__(self, names):
        self.at = {n: i + 1 for i, n in enumerate(names)}
        self.n = len(names)

    def now(self, it, name):
        return (it + 1) * self.n + self.at[name]

    def before(self, it, name):
        return it * self.n + self.at[name]


def phase_experts(nc, g):
    a, ps, c = g.a, g.ps, g.c
    T = range(TILES)
    PAIRS = EXPERTS // 2
    B = range(2)
    with ExitStack() as ctx:
        def sb(name, shape, dt=F32):
            return ctx.enter_context(nc.sbuf_tensor(name, shape, dt))
        wgu = [g.ring[:, b].rearrange("p k n -> p (k n)").rearrange("p (m k n) -> p m k n", m=2, k=KD) for b in B]
        wd = [g.ring[:, 2].rearrange("p k n -> p (k n)")[:, b * 2048:(b + 1) * 2048].rearrange(
            "p (j n) -> p j n", j=KF) for b in B]
        hot = sb("hot", [P, 2, TILES, P])
        hotT = sb("hotT", [P, 2, TOK])
        gcol = sb("gcol", [P, 2, TILES])
        gslot = sb("gslot", [P, 2])
        hgT = sb("hgT", [P, 2, KD, P])
        sil = sb("sil", [P, 2, FE])
        actT = sb("actT", [P, 2, KF, P])
        ye = sb("ye", [P, 2, D])
        s_gu = [g.sem(f"gate_up_loaded{b}") for b in B]
        s_dn = [g.sem(f"down_loaded{b}") for b in B]
        pe_done, dve_done, act_done = (g.sem("moe_" + n) for n in ("pe", "dve", "act"))
        units = [(t, n) for t in T for n in range(2)]
        YB = (7, 5, 6)
        PE = Each([(x, b) for b in B for x in ("hg", "hotT", "gate", "gu", "actT", "ye")] + [("y", u) for u in units])
        A = Each([(x, b) for b in B for x in ("hgT", "silu", "actT", "ye")])
        V = Each([("hot", 0), ("hot", 1)] + [(x, b) for b in B for x in ("hotT", "gslot", "act")]
                 + [("y", u) for u in units])
        with nc.Block() as block:
            def loop(eng, body):
                n = eng.value_load(g.passes[0:1, 0:1], min_val=1, max_val=TILES)
                with eng.Fori(0, n) as turn:
                    with eng.Fori(0, PAIRS) as pair:
                        body(turn * PAIRS + pair, pair)

            @block.sync
            def _(sp):
                def body(it, pair):
                    for b in B:
                        e = pair * 2 + b
                        sp.wait_ge(pe_done, PE.before(it, ("gu", b)))
                        for m, w in enumerate((a["w_gate"], a["w_up"])):
                            sp.dma_start(wgu[b][:, m], w[0, bass.ds(e, 1)].rearrange("e (p k) n -> p (e k) n", k=KD)) \
                                .then_inc(s_gu[b], 16)
                        sp.wait_ge(pe_done, PE.before(it, ("ye", b)))
                        sp.dma_start(wd[b], a["w_down"][0, bass.ds(e, 1)].rearrange("e (p j) n -> p (e j) n", j=KF)) \
                            .then_inc(s_dn[b], 16)
                loop(sp, body)

            @block.scalar
            def _(act):
                act.sem_inc(act_done, A.n)

                def body(it, pair):
                    for b in B:
                        act.wait_ge(pe_done, PE.now(it, ("hg", b)))
                        act.activation(hgT[:, b], ps[:, 0:2, :].rearrange("p b (k n) -> p (b k) n", k=4), ACT.Copy) \
                            .then_inc(act_done, 1)
                        act.wait_ge(pe_done, PE.now(it, ("gu", b)))
                        act.wait_ge(pe_done, PE.before(it, ("actT", b)))
                        act.activation(sil[:, b], ps[:, 4, 0:FE], ACT.Silu).then_inc(act_done, 1)
                        act.wait_ge(pe_done, PE.now(it, ("actT", b)))
                        act.activation(actT[:, b].rearrange("p j n -> p (j n)"), ps[:, 3, 0:KF * P], ACT.Copy) \
                            .then_inc(act_done, 1)
                        act.wait_ge(pe_done, PE.now(it, ("ye", b)))
                        act.activation(ye[:, b].rearrange("p (b n) -> p b n", b=2), ps[:, 5:7, :], ACT.Copy) \
                            .then_inc(act_done, 1)
                loop(act, body)

            @block.tensor
            def _(pe):
                pe.sem_inc(pe_done, PE.n)

                def body(it, pair):
                    for b in B:
                        pe.wait_ge(dve_done, V.now(it, ("hot", b)))
                        if b:
                            pe.wait_ge(act_done, A.now(it, ("hgT", 0)))
                        else:
                            pe.wait_ge(act_done, A.before(it, ("hgT", 1)))
                        for k in range(KD):
                            for t in T:
                                mm = pe.matmul(ps[:, k // 4, (k % 4) * P:(k % 4 + 1) * P], g.h2[:, t, k::KD],
                                               hot[:, b, t, :], start=(t == 0), stop=(t == TILES - 1))
                        mm.then_inc(pe_done, 1)
                        pe.wait_ge(dve_done, V.now(it, ("gslot", 0)) if b else V.before(it, ("gslot", 1)))
                        for t in T:
                            mm = pe.transpose(ps[:, 2, t * P:(t + 1) * P], hot[:, b, t, :], c["ident"])
                        mm.then_inc(pe_done, 1)
                        for t in T:
                            mm = pe.matmul(ps[:, 2, TOK:TOK + 1], hot[:, b, t, :], gcol[:, b, t:t + 1],
                                           start=(t == 0), stop=(t == TILES - 1))
                        mm.then_inc(pe_done, 1)
                        pe.wait_ge(act_done, A.now(it, ("hgT", b)))
                        pe.wait_ge(s_gu[b], it * 32 + 32)
                        pe.wait_ge(dve_done, V.now(it, ("act", 0)) if b else V.before(it, ("act", 1)))
                        for k in range(KD):
                            mm = pe.matmul(ps[:, 4, :], hgT[:, b, k, :], wgu[b][:, :, k, :], start=(k == 0),
                                           stop=(k == KD - 1))
                        mm.then_inc(pe_done, 1)
                        pe.wait_ge(dve_done, V.now(it, ("act", b)))
                        for j in range(KF):
                            mm = pe.transpose(ps[:, 3, j * P:(j + 1) * P], sil[:, b, j::KF], c["ident"])
                        mm.then_inc(pe_done, 1)
                        pe.wait_ge(act_done, A.now(it, ("actT", b)))
                        pe.wait_ge(s_dn[b], it * 16 + 16)
                        if b:
                            pe.wait_ge(act_done, A.now(it, ("ye", 0)))
                        else:
                            pe.wait_ge(dve_done, V.before(it, ("y", units[-1])))
                        for n in range(2):
                            for j in range(KF):
                                mm = pe.matmul(ps[:, 5 + n, :], actT[:, b, j, :], wd[b][:, j, n * 512:(n + 1) * 512],
                                               start=(j == 0), stop=(j == KF - 1))
                        mm.then_inc(pe_done, 1)
                    pe.wait_ge(act_done, A.now(it, ("ye", 1)))
                    for i, (t, n) in enumerate(units):
                        if i >= 3:
                            pe.wait_ge(dve_done, V.now(it, ("y", units[i - 3])))
                        for b in B:
                            mm = pe.matmul(ps[:, YB[i % 3], :], hotT[:, b, t * P:(t + 1) * P],
                                           ye[:, b, n * 512:(n + 1) * 512], start=(b == 0), stop=(b == 1))
                        mm.then_inc(pe_done, 1)
                loop(pe, body)

            @block.vector
            def _(dve):
                dve.sem_inc(dve_done, V.n)
                n = dve.value_load(g.passes[0:1, 0:1], min_val=1, max_val=TILES)
                with dve.Fori(0, n) as turn:
                    with dve.Fori(0, PAIRS) as pair:
                        it = turn * PAIRS + pair
                        for b in B:
                            e = pair * 2 + b
                            dve.wait_ge(pe_done, PE.before(it, ("gate", b)))
                            for t in T:
                                dve.tensor_scalar(hot[:, b, t, :], c["iota"], g.pos[:, t, bass.ds(e, 1)], None,
                                                  ALU.is_equal)
                            dve.tensor_copy(gcol[:, b, :], g.gates[:, :, bass.ds(e, 1)].rearrange("p t e -> p (t e)")) \
                                .then_inc(dve_done, 1)
                        for b in B:
                            dve.wait_ge(pe_done, PE.now(it, ("gate", b)))
                            dve.tensor_copy(hotT[:, b, :], ps[:, 2, 0:TOK]).then_inc(dve_done, 1)
                            dve.tensor_copy(gslot[:, b:b + 1], ps[:, 2, TOK:TOK + 1]).then_inc(dve_done, 1)
                            dve.wait_ge(act_done, A.now(it, ("silu", b)))
                            dve.wait_ge(dve_done, V.now(it, ("gslot", b)))
                            dve.scalar_tensor_tensor(out=sil[:, b], in0=ps[:, 4, FE:2 * FE], scalar=gslot[:, b:b + 1],
                                                     in1=sil[:, b], op0=ALU.mult, op1=ALU.mult).then_inc(dve_done, 1)
                        for i, (t, m) in enumerate(units):
                            yt = g.y[:, t, m * 512:(m + 1) * 512]
                            dve.wait_ge(pe_done, PE.now(it, ("y", (t, m))))
                            dve.wait_ge(dve_done, V.before(it, ("y", (t, m))))
                            dve.tensor_tensor(yt, yt, ps[:, YB[i % 3], :], ALU.add).then_inc(dve_done, 1)
                    dve.wait_ge(pe_done, (turn * PAIRS + PAIRS - 1 + 1) * PE.n + PE.at[("gate", 1)])
                    dve.tensor_scalar(g.pos[:], g.pos[:], -float(P), None, ALU.add).then_inc(g.s_pos, 1)
                    dve.wait_ge(g.s_pos, turn + 1)


def phase_output(nc, g):
    a = g.a
    with ExitStack() as ctx:
        def sb(name, shape):
            return ctx.enter_context(nc.sbuf_tensor(name, shape, F32))
        gate = sb("gate2", [P, 2, D])
        gpost = sb("gpost2", [P, D])
        tmp = sb("tmp", [P, TILES, D])
        stat = sb("ostat2", [P, 4, TILES])
        s_row, s_out = g.sem("gate2_loaded"), g.sem("y_stored")
        dve_done, act_done = g.sem("out_dve"), g.sem("out_act")
        T = range(TILES)
        V = Count(["gate", "ms", "rec"] + [(x, t) for t in T for x in ("yn", "x2")])
        A = Count([("ss", t) for t in T] + ["rs"])
        with nc.Block() as block:
            @block.sync
            def _(sp):
                for v in range(2):
                    sp.dma_start(gate[:, v], g.mods_dram[v, 5].partition_broadcast(P)).then_inc(s_row, 16)
                sp.dma_start(gpost[:], a["g_post_ffn"][0].partition_broadcast(P)).then_inc(s_row, 16)
                for t in T:
                    sp.wait_ge(dve_done, V[("x2", t)])
                    dst = g.o["y_prompt"][0] if t == 0 else g.o["y_sample"][0, (t - 1) * P:t * P]
                    sp.dma_start(dst, g.x1[:, t, :]).then_inc(s_out, 16)
                sp.wait_ge(s_out, 16 * TILES)

            @block.scalar
            def _(act):
                for t in T:
                    act.activation(tmp[:, t, :], g.y[:, t, :], ACT.Square, accum_out=stat[:, 0, t:t + 1]) \
                        .then_inc(act_done, A.step("ss", t))
                act.wait_ge(dve_done, V["rec"])
                act.activation(stat[:, 3], stat[:, 2], ACT.Sqrt).then_inc(act_done, A.step("rs"))

            @block.vector
            def _(dve):
                dve.wait_ge(s_row, 48)
                dve.tensor_tensor(gate[:], gate[:], over(gpost[:], 2, 1), ALU.mult).then_inc(dve_done, V.step("gate"))
                dve.wait_ge(act_done, A[("ss", 2)])
                dve.tensor_scalar(stat[:, 1], stat[:, 0], 1.0 / D, EPS, ALU.mult, ALU.add).then_inc(dve_done, V.step("ms"))
                dve.wait_ge(dve_done, V["ms"])
                dve.reciprocal(stat[:, 2], stat[:, 1]).then_inc(dve_done, V.step("rec"))
                dve.wait_ge(act_done, A["rs"])
                dve.wait_ge(dve_done, V["gate"])
                for t in T:
                    dve.scalar_tensor_tensor(out=tmp[:, t, :], in0=g.y[:, t, :], scalar=stat[:, 3, t:t + 1],
                                             in1=gate[:, min(t, 1)], op0=ALU.mult, op1=ALU.mult) \
                        .then_inc(dve_done, V.step("yn", t))
                    dve.wait_ge(dve_done, V[("yn", t)])
                    dve.tensor_tensor(g.x1[:, t, :], g.x1[:, t, :], tmp[:, t, :], ALU.add) \
                        .then_inc(dve_done, V.step("x2", t))


def phases(nc, g, sb, sem):
    with ExitStack() as early:
        def eb(name, shape):
            return early.enter_context(nc.sbuf_tensor(name, shape, F32))
        g.small = eb("small", [P, TILES, 64])
        g.z = eb("z", [P, TILES, GW])
        g.omla = eb("omla", [P, TILES, GW])
        with nc.sbuf_tensor("wconv", [P, CONV, 12], F32) as g.wconv, nc.sbuf_tensor("qkv", [P, 12, OUTW], F32) as g.qkv:
            phase_condition(nc, g)
            with nc.sbuf_tensor("cqkv", [P, TILES, 2 * LORA], F32) as g.cqkv:
                phase_project(nc, g)
                phase_attention(nc, g)
            phase_delta(nc, g)
        g.x1 = sb("x1", [P, TILES, D], side="right")
        phase_merge(nc, g)
    g.h2 = sb("h2", [P, TILES, D])
    g.y = sb("y", [P, TILES, D])
    g.gates = sb("gates", [P, TILES, EXPERTS])
    g.pos = sb("pos", [P, TILES, EXPERTS])
    g.passes = sb("passes", [1, 1], mybir.dt.int32)
    g.s_pos = sem("pos_shifted")
    phase_route(nc, g)
    phase_experts(nc, g)
    phase_output(nc, g)


_INS = ["x_prompt", "x_sample", "cache_ckv", "cache_krope", "state_delta", "c", "c_ctx", "w_ada", "b_ada",
        "g_pre_mix", "g_post_mix", "g_pre_ffn", "g_post_ffn", "w_in", "q_norm_g", "kv_norm_g", "w_uq", "w_ukv",
        "conv_w", "a_log", "dt_bias", "gdn_norm_g", "w_oa", "w_ob", "w_o", "w_router", "e_bias", "w_gate", "w_up",
        "w_down", "ws_gate", "ws_up", "ws_down"]
_OUTS = [("y_prompt", (1, CTX, D)), ("y_sample", (1, LAT, D)), ("ckv", (1, 1, CTX, LORA)),
         ("krope", (1, 1, CTX, ROPE)), ("state", (1, 1, 2, GH, DK, DV))]


def kernel(**inputs):
    from concourse import bacc
    from concourse.bass_utils import run_bass_kernel_spmd

    nc = bacc.Bacc("TRN2", target_bir_lowering=False, num_devices=1)
    arrays = {f"in_{n}": np.ascontiguousarray(inputs[n]) for n in _INS}
    arrays["in_table"] = constant_columns()[0]
    a = {n[3:]: nc.dram_tensor(n, v.shape, F32, kind="ExternalInput").ap() for n, v in arrays.items()}
    o = {n: nc.dram_tensor(f"out_{n}", s, F32, kind="ExternalOutput").ap() for n, s in _OUTS}
    build(nc, a, o)
    r = run_bass_kernel_spmd(nc, [arrays], core_ids=[0])
    return tuple(r.results[0][f"out_{n}"] for n, _ in _OUTS)
```

```python
from contextlib import ExitStack

import numpy as np

import concourse.bass as bass
from concourse import mybir

F32 = mybir.dt.float32
ALU = mybir.AluOpType
ACT = mybir.ActivationFunctionType
AX = mybir.AxisListType.X

P = 128
D = 1024
KD = D // P
CTX, LAT, PAST = 128, 256, 128
TILES = (CTX + LAT) // P
TOK = TILES * P
MH, NOPE, ROPE, VH = 8, 64, 32, 64
QK = NOPE + ROPE
LORA = 256
KL = LORA // P
GH, DK, DV = 8, 64, 64
GW = GH * DV
CONV, CHUNK = 5, 64
EXPERTS, GROUPS, TOPG, TOPK = 64, 8, 4, 8
PER = EXPERTS // GROUPS
FE = 256
KF = FE // P
ROUTED = 2.5
EPS = 1e-6
GRID_W, THETA = 64, 10000.0
GAP = CONV // 2
PADW = TOK + 3 * GAP
OUTW = TOK + GAP
LEVELS = (1, 2, 4, 8, 16, 32)

C_CQ, C_CKV, C_KR, C_QKV, C_Z, C_AB, C_GA, C_GB = 0, 256, 512, 544, 2080, 2592, 2624, 3648


def tok_at(t):
    return t * P + (GAP if t else 0)


def constant_columns():
    i = np.arange(P)[:, None]
    j = np.arange(P)[None, :]
    same = (i // CHUNK) == (j // CHUNK)
    parts = {"ident": i == j, "incl0": same & (i <= j), "incl1": same & (i >= j),
             "strict0": same & (i < j), "strict1": same & (i > j), "block": same,
             "half0": (i < CHUNK) & (j >= 0), "half1": (i >= CHUNK) & (j >= 0),
             "before": i < j, "ones": (i >= 0) & (j >= 0), "iota": j + 1 + 0 * i}
    for s in LEVELS:
        low = ((i // s) == (j // s) + 1) & ((j // s) % 2 == 0)
        parts[f"level0_{s}"] = low
        parts[f"level1_{s}"] = low.T
    inv = THETA ** (-np.arange(ROPE // 4) / (ROPE // 4))
    n = np.arange(LAT)
    ang = np.stack([(n // GRID_W)[:, None] * inv, (n % GRID_W)[:, None] * inv], axis=1).reshape(LAT, ROPE // 2)
    parts["cos"] = np.cos(ang).reshape(LAT // P, P, ROPE // 2).transpose(1, 0, 2).reshape(P, -1)
    parts["sin"] = np.sin(ang).reshape(LAT // P, P, ROPE // 2).transpose(1, 0, 2).reshape(P, -1)
    g = np.arange(GROUPS)
    parts["earlier"] = np.broadcast_to((g[None, :] < g[:, None]).reshape(1, -1), (P, GROUPS * GROUPS))
    at, n = {}, 0
    for name, a in parts.items():
        at[name] = (n, n + a.shape[1])
        n += a.shape[1]
    return np.concatenate([np.asarray(a, np.float32) for a in parts.values()], axis=1), at


class Names:
    pass


class Count:

    def __init__(self, names):
        self.at = {n: i + 1 for i, n in enumerate(names)}
        self.done = 0
        assert len(self.at) == len(names)

    def __getitem__(self, name):
        return self.at[name]

    def step(self, *name):
        name = name if len(name) > 1 else name[0]
        self.done += 1
        assert self.at[name] == self.done, (name, self.at[name], self.done)
        return 1


def over(ap, n, axis):
    a = ap.unsqueeze(axis)
    shape = list(a.shape)
    shape[axis] = n
    return a.broadcast_to(shape)


RING = 3


def build(nc, a, o):
    g = Names()
    with ExitStack() as ctx:
        def sb(name, shape, dt=F32, **kw):
            return ctx.enter_context(nc.sbuf_tensor(name, shape, dt, **kw))

        def sem(name):
            return ctx.enter_context(nc.semaphore(name))

        cols, at = constant_columns()
        g.cst = sb("cst", [P, cols.shape[1]])
        g.c = {n: g.cst[:, lo:hi] for n, (lo, hi) in at.items()}
        g.sem, g.a, g.o, g.ctx = sem, a, o, ctx
        g.ps = ctx.enter_context(nc.psum_tensor("ps", [P, 8, 512], F32))
        g.mods_dram = nc.dram_tensor("mods_scratch", [2, 6, D], F32, kind="Internal").ap()
        g.ring = sb("ring", [P, RING, KD, 512])
        g.s_slot = [sem(f"slot_loaded{i}") for i in range(RING)]
        g.loads = 0
        phases(nc, g, sb, sem)


def slot(i):
    return i % RING


def loaded(i):
    return 16 * (i // RING + 1)


N_ADA = 6 * D // 512
IN_CHUNKS = [("cqkv", C_CQ), ("q", C_QKV), ("k", C_QKV + GW), ("v", C_QKV + 2 * GW), ("z", C_Z)]
GATE_CHUNKS = [("ga0", C_GA), ("gb0", C_GB), ("ga1", C_GA + 512), ("gb1", C_GB + 512)]
RING_LOADS = [("ada", n) for n in range(N_ADA)] + [c[0] for c in IN_CHUNKS] + [c[0] for c in GATE_CHUNKS]
LOAD = {n: i for i, n in enumerate(RING_LOADS)}


def ring_source(g, i):
    name = RING_LOADS[i]
    if isinstance(name, tuple):
        w, c0 = g.a["w_ada"][0], name[1] * 512
    else:
        w, c0 = g.a["w_in"][0], dict(IN_CHUNKS + GATE_CHUNKS)[name]
    return w.rearrange("(p k) n -> p k n", k=KD)[:, :, c0:c0 + 512]


def phase_condition(nc, g):
    a, ps, c = g.a, g.ps, g.c
    with ExitStack() as ctx:
        def sb(name, shape):
            return ctx.enter_context(nc.sbuf_tensor(name, shape, F32))
        cond = sb("cond", [P, 2, KD])
        scond = sb("scond", [P, 2, KD])
        bias = sb("bias", [2, 6 * D])
        mods = sb("mods", [2, 6 * D])
        x = sb("x", [P, TILES, D])
        xn = sb("xn", [P, TILES, D])
        stat = sb("stat", [P, 4, TILES])
        modT = sb("modT", [P, 2, 2, KD])
        gpre = sb("gpre", [P, KD])
        scaleT = sb("scaleT", [P, 2, KD])
        convrow = sb("convrow", [CONV * 12, P])
        s_c, s_cst, s_b, s_x, s_conv, s_g = (g.sem(n) for n in
            ("cond_loaded", "const_loaded", "bias_loaded", "x_loaded", "convw_loaded", "gpre_loaded"))
        g.s_cst = s_cst
        s_modst, s_modT, s_mods = g.sem("mods_head_stored"), g.sem("modT_loaded"), g.sem("mods_stored")
        pe_done, dve_done, act_done = g.sem("cond_pe"), g.sem("cond_dve"), g.sem("cond_act")
        pe_order = []
        for n in range(N_ADA):
            pe_order.append(("ada", n))
            if n == 5:
                pe_order += ["convT", ("xT", 0), ("xT", 1)]
            if n == 8:
                pe_order.append(("xT", 2))
        PE = Count(pe_order)
        dve_order = ["ms", "rms"] + [("xn", t) for t in range(TILES)] + [("mods", n) for n in range(4)] \
            + ["A1", "A"] + [("mods", 4), ("mods", 5), "convT", ("hT", 0), ("hT", 1)] \
            + [("mods", n) for n in range(6, 9)] + [("hT", 2)] + [("mods", n) for n in range(9, N_ADA)]
        V = Count(dve_order)
        A = Count(["scond"] + [("ss", t) for t in range(TILES)] + ["rs"])
        with nc.Block() as block:
            @block.sync
            def _(sp):
                for v, src in ((0, a["c_ctx"]), (1, a["c"][0])):
                    sp.dma_start(cond[:, v, :], src.rearrange("(p k) -> p k", k=KD)).then_inc(s_c, 16)
                for n in range(RING):
                    sp.dma_start(g.ring[:, slot(n)], ring_source(g, n)).then_inc(g.s_slot[slot(n)], 16)
                sp.dma_start(bias[:], a["b_ada"][0].partition_broadcast(2)).then_inc(s_b, 16)
                sp.dma_start(g.cst[:], a["table"]).then_inc(s_cst, 16)
                for n in range(RING, LOAD["v"]):
                    last = PE[("ada", n - RING)]
                    sp.wait_ge(pe_done, last)
                    sp.dma_start(g.ring[:, slot(n)], ring_source(g, n)).then_inc(g.s_slot[slot(n)], 16)
                    if n == RING + 4:
                        sp.wait_ge(dve_done, V[("mods", 3)])
                        sp.dma_start(g.mods_dram[:, 0:2, :].rearrange("v m d -> v (m d)"),
                                     mods[:, 0:2 * D]).then_inc(s_modst, 16)
                        sp.wait_ge(s_modst, 16)
                        for v in range(2):
                            sp.dma_start(modT[:, v], g.mods_dram[v, 0:2].rearrange("m (p k) -> p m k", k=KD)) \
                                .then_inc(s_modT, 16)
                sp.wait_ge(dve_done, V[("mods", N_ADA - 1)])
                sp.dma_start(g.mods_dram[:, 2:6, :].rearrange("v m d -> v (m d)"),
                             mods[:, 2 * D:6 * D]).then_inc(s_mods, 16)
                sp.wait_ge(s_mods, 16)

            @block.scalar
            def _(act):
                act.dma_start(x[:, 0, :], a["x_prompt"][0]).then_inc(s_x, 16)
                act.dma_start(x[:, 1:3, :], a["x_sample"][0].rearrange("(t p) d -> p t d", p=P)).then_inc(s_x, 16)
                act.dma_start(convrow[:], a["conv_w"][0].rearrange("j (m p) -> (j m) p", p=P)).then_inc(s_conv, 16)
                act.dma_start(gpre[:], a["g_pre_mix"][0].rearrange("(p k) -> p k", k=KD)).then_inc(s_g, 16)
                act.wait_ge(s_c, 32)
                act.activation(scond[:], cond[:], ACT.Silu).then_inc(act_done, A.step("scond"))
                act.wait_ge(s_x, 32)
                for t in range(TILES):
                    act.activation(xn[:, t, :], x[:, t, :], ACT.Square, accum_out=stat[:, 0, t:t + 1]) \
                        .then_inc(act_done, A.step("ss", t))
                act.wait_ge(dve_done, V["rms"])
                act.activation(stat[:, 3, :], stat[:, 2, :], ACT.Sqrt).then_inc(act_done, A.step("rs"))

            @block.tensor
            def _(pe):
                def transposes(t):
                    for k in range(KD):
                        mm = pe.transpose(ps[:, 4 + 2 * (t % 2) + k // 4, (k % 4) * P:(k % 4 + 1) * P],
                                          xn[:, t, k::KD], c["ident"])
                    mm.then_inc(pe_done, PE.step("xT", t))

                pe.wait_ge(act_done, A["scond"])
                for n in range(N_ADA):
                    pe.wait_ge(g.s_slot[slot(n)], loaded(n))
                    if n >= 4:
                        pe.wait_ge(dve_done, V[("mods", n - 4)])
                    for k in range(KD):
                        mm = pe.matmul(ps[0:2, n % 4, :], scond[:, :, k], g.ring[:, slot(n), k, :],
                                       start=(k == 0), stop=(k == KD - 1))
                    mm.then_inc(pe_done, PE.step("ada", n))
                    if n == 5:
                        pe.wait_ge(s_cst, 16)
                        pe.wait_ge(s_conv, 16)
                        pe.transpose(ps[:, 4, 0:CONV * 12], convrow[:], c["ident"][0:CONV * 12, 0:CONV * 12]) \
                            .then_inc(pe_done, PE.step("convT"))
                        pe.wait_ge(dve_done, V["convT"])
                        transposes(0)
                        transposes(1)
                    if n == 8:
                        pe.wait_ge(dve_done, V[("hT", 0)])
                        transposes(2)

            @block.vector
            def _(dve):
                dve.wait_ge(act_done, A[("ss", TILES - 1)])
                dve.tensor_scalar(stat[:, 1, :], stat[:, 0, :], 1.0 / D, EPS, ALU.mult, ALU.add) \
                    .then_inc(dve_done, V.step("ms"))
                dve.wait_ge(dve_done, V["ms"])
                dve.reciprocal(stat[:, 2, :], stat[:, 1, :]).then_inc(dve_done, V.step("rms"))
                dve.wait_ge(act_done, A["rs"])
                for t in range(TILES):
                    dve.tensor_scalar(xn[:, t, :], x[:, t, :], stat[:, 3, t:t + 1], None, ALU.mult) \
                        .then_inc(dve_done, V.step("xn", t))
                dve.wait_ge(s_b, 16)

                def take_mods(n):
                    dve.wait_ge(pe_done, PE[("ada", n)])
                    dve.tensor_tensor(mods[:, n * 512:(n + 1) * 512], ps[0:2, n % 4, :],
                                      bias[:, n * 512:(n + 1) * 512], ALU.add).then_inc(dve_done, V.step("mods", n))

                def take_hT(t):
                    dve.wait_ge(pe_done, PE[("xT", t)])
                    v = min(t, 1)
                    for k in range(KD):
                        i = dve.tensor_scalar(g.hT[:, k, t * P:(t + 1) * P],
                                              ps[:, 4 + 2 * (t % 2) + k // 4, (k % 4) * P:(k % 4 + 1) * P],
                                              scaleT[:, v, k:k + 1], modT[:, v, 0, k:k + 1], ALU.mult, ALU.add)
                    i.then_inc(dve_done, V.step("hT", t))

                for n in range(4):
                    take_mods(n)
                dve.wait_ge(s_modT, 32)
                dve.wait_ge(s_g, 16)
                dve.tensor_scalar(scaleT[:], modT[:, :, 1, :], 1.0, None, ALU.add).then_inc(dve_done, V.step("A1"))
                dve.wait_ge(dve_done, V["A1"])
                dve.tensor_tensor(scaleT[:], scaleT[:], over(gpre[:], 2, 1), ALU.mult).then_inc(dve_done, V.step("A"))
                dve.wait_ge(dve_done, V["A"])
                take_mods(4)
                take_mods(5)
                dve.wait_ge(pe_done, PE["convT"])
                dve.tensor_copy(g.wconv[:], ps[:, 4, 0:CONV * 12].rearrange("p (j m) -> p j m", j=CONV)) \
                    .then_inc(dve_done, V.step("convT"))
                take_hT(0)
                take_hT(1)
                for n in range(6, 9):
                    take_mods(n)
                take_hT(2)
                for n in range(9, N_ADA):
                    take_mods(n)


def phase_project(nc, g):
    a, ps = g.a, g.ps
    with ExitStack() as ctx:
        def sb(name, shape):
            return ctx.enter_context(nc.sbuf_tensor(name, shape, F32))
        wsmall = sb("wsmall", [P, KD, 64])
        acc = sb("acc", [P, 2, OUTW])
        pad = sb("pad", [P, 2, PADW])
        s_small = g.sem("wsmall_loaded")
        pe_done, dve_done, act_done = g.sem("proj_pe"), g.sem("proj_dve"), g.sem("proj_act")
        units = [("cqkv", t) for t in range(TILES)] + [("small", t) for t in range(TILES)] \
            + [(n, m) for n in "qkv" for m in range(4)] + [("z", t) for t in range(TILES)]
        PE = Count(units)
        A = Count(["gaps"] + [("cqkv", t) for t in range(TILES)] + [("small", t) for t in range(TILES)]
                  + [x for i in range(12) for x in ((("pad", i),) + ((("silu", i - 1),) if i else ()))]
                  + [("silu", 11)] + [("z", t) for t in range(TILES)])
        V = Count([(s, i) for i in range(12) for s in [f"tap{j}" for j in range(CONV)]])
        with nc.Block() as block:
            @block.sync
            def _(sp):
                w = a["w_in"][0].rearrange("(p k) n -> p k n", k=KD)
                sp.dma_start(wsmall[:, :, 0:32], w[:, :, C_KR:C_KR + 32]).then_inc(s_small, 16)
                sp.dma_start(wsmall[:, :, 32:64], w[:, :, C_AB:C_AB + 32]).then_inc(s_small, 16)
                for name, last in (("v", ("cqkv", TILES - 1)), ("z", ("q", 3)), ("ga0", ("k", 3)), ("gb0", ("v", 3)),
                                   ("ga1", ("z", TILES - 1))):
                    n = LOAD[name]
                    sp.wait_ge(pe_done, PE[last])
                    sp.dma_start(g.ring[:, slot(n)], ring_source(g, n)).then_inc(g.s_slot[slot(n)], 16)

            @block.tensor
            def _(pe):
                for i, (name, m) in enumerate(units):
                    b = i % 8
                    if name == "small":
                        pe.wait_ge(s_small, 32)
                    else:
                        n = LOAD[name]
                        pe.wait_ge(g.s_slot[slot(n)], loaded(n))
                    if i >= 8:
                        was = units[i - 8]
                        pe.wait_ge(act_done, A[("pad", "qkv".index(was[0]) * 4 + was[1])
                                               if was[0] in "qkv" else was])
                    for k in range(KD):
                        if name in ("cqkv", "z"):
                            mm = pe.matmul(ps[:, b, :], g.hT[:, k, m * P:(m + 1) * P], g.ring[:, slot(n), k, :],
                                           start=(k == 0), stop=(k == KD - 1))
                        elif name == "small":
                            mm = pe.matmul(ps[:, b, 0:64], g.hT[:, k, m * P:(m + 1) * P], wsmall[:, k, :],
                                           start=(k == 0), stop=(k == KD - 1))
                        else:
                            mm = pe.matmul(ps[:, b, 0:TOK], g.ring[:, slot(n), k, m * P:(m + 1) * P], g.hT[:, k, :],
                                           start=(k == 0), stop=(k == KD - 1))
                    mm.then_inc(pe_done, PE.step(name, m))

            @block.scalar
            def _(act):
                for b in range(2):
                    for z in (0, GAP + CTX, PADW - GAP):
                        i = act.activation(pad[:, b, z:z + GAP], g.c["ident"][:, 0:GAP], ACT.Copy, scale=0.0)
                i.then_inc(act_done, A.step("gaps"))
                at = 0

                def take(dst, width, name, m):
                    nonlocal at
                    act.wait_ge(pe_done, PE[(name, m)])
                    act.activation(dst, ps[:, at % 8, 0:width], ACT.Copy).then_inc(act_done, A.step(name, m))
                    at += 1

                def silu(i):
                    act.wait_ge(dve_done, V[("tap4", i)])
                    act.activation(g.qkv[:, i, :], acc[:, i % 2, :], ACT.Silu).then_inc(act_done, A.step("silu", i))

                for t in range(TILES):
                    take(g.cqkv[:, t, :], 512, "cqkv", t)
                for t in range(TILES):
                    take(g.small[:, t, :], 64, "small", t)
                for i in range(12):
                    act.wait_ge(pe_done, PE[("qkv"[i // 4], i % 4)])
                    if i >= 2:
                        act.wait_ge(dve_done, V[("tap4", i - 2)])
                    act.activation(pad[:, i % 2, GAP:GAP + CTX], ps[:, at % 8, 0:CTX], ACT.Copy)
                    act.activation(pad[:, i % 2, 2 * GAP + CTX:2 * GAP + TOK], ps[:, at % 8, CTX:TOK], ACT.Copy) \
                        .then_inc(act_done, A.step("pad", i))
                    at += 1
                    if i:
                        silu(i - 1)
                silu(11)
                for t in range(TILES):
                    take(g.z[:, t, :], 512, "z", t)

            @block.vector
            def _(dve):
                for i in range(12):
                    dve.wait_ge(act_done, A[("pad", i)])
                    if i >= 2:
                        dve.wait_ge(act_done, A[("silu", i - 2)])
                    for j in range(CONV):
                        src = pad[:, i % 2, j:j + OUTW]
                        w = g.wconv[:, j, i:i + 1]
                        if j == 0:
                            ins = dve.tensor_scalar(acc[:, i % 2, :], src, w, None, ALU.mult)
                        else:
                            dve.wait_ge(dve_done, V[(f"tap{j - 1}", i)])
                            ins = dve.scalar_tensor_tensor(out=acc[:, i % 2, :], in0=src, scalar=w,
                                                           in1=acc[:, i % 2, :], op0=ALU.mult, op1=ALU.add)
                        ins.then_inc(dve_done, V.step(f"tap{j}", i))


def phase_attention(nc, g):
    a, ps, c, o = g.a, g.ps, g.c, g.o
    KT = TILES + 1
    SCALE = float(QK) ** -0.5
    with ExitStack() as ctx:
        def sb(name, shape):
            return ctx.enter_context(nc.sbuf_tensor(name, shape, F32))
        wuq = sb("wuq", [P, KL, MH * QK])
        wukv = sb("wukv", [P, KL, MH * (NOPE + VH)])
        grow = sb("grow", [P, 2, LORA])
        kr = sb("kr", [P, KT, ROPE])
        ckv = sb("ckv", [P, KT, LORA])
        cqn = sb("cqn", [P, TILES, LORA])
        stat = sb("astat", [P, 4, 6])
        cqT = sb("cqT", [P, KL, TOK])
        ckvT = sb("ckvT", [P, KL, KT * P])
        q = sb("q", [P, TILES, MH, QK])
        k = sb("k", [P, KT, MH, QK])
        v = sb("v", [P, KT, MH, VH])
        qT = sb("qT", [QK, MH, TOK])
        kT = sb("kT", [QK, MH, KT * P])
        prob = sb("prob", [P, 2, 3 * P])
        probT = sb("probT", [P, 2, 3, P])
        nmax = sb("nmax", [P, TILES, MH])
        rsum = sb("rsum", [P, TILES, MH])
        rinv = sb("rinv", [P, TILES, MH])
        rope = sb("ropetmp", [P, 4, MH, 2, 8])
        s_w, s_g, s_cache, s_out = (g.sem(n) for n in ("attw_loaded", "gains_loaded", "cache_loaded", "ckv_stored"))
        pe_done, dve_done, act_done = g.sem("att_pe"), g.sem("att_dve"), g.sem("att_act")
        units = [(t, h) for t in range(TILES) for h in range(MH)]
        nk = lambda t: 1 if t == 0 else 3
        k0 = lambda t: 0 if t == 0 else 1
        loop = []
        for i in range(len(units) + 2):
            if i < len(units):
                loop.append(("score", i))
            if 1 <= i <= len(units):
                loop.append(("probT", i - 1))
            if i >= 2:
                loop.append(("pv", i - 2))
        PE = Count(["cqT", "ckvT"] + [("q", t) for t in range(TILES)] + [("kv", t) for t in range(KT)]
                   + [("qT", t) for t in range(TILES)] + [("kT", t) for t in range(KT)] + loop)
        rope_steps = lambda n: [(n, s) for s in ("ac", "bs", "bc", "as", "a", "b")]
        V = Count(["ms", "rms", "cqn0", "cqn", "ckv0", "ckv"] + rope_steps("kr1") + rope_steps("kr2")
                  + ["cqT"]
                  + [x for t in range(TILES) for x in (["q", t],)] * 0
                  + [("q", t) for t in range(TILES)] + rope_steps("q1") + rope_steps("q2")
                  + [("kr", t) for t in range(KT)] + [("qT", t) for t in range(TILES)]
                  + [x for i in range(len(units) + 2) for x in
                     ([("max", i)] if i < len(units) else []) + ([("probT", i - 1)] if 1 <= i <= len(units) else [])]
                  + ["rinv", "o"])
        A = Count([("ss", i) for i in range(6)] + ["rs", "ckvT"] + [("kv", t) for t in range(KT)]
                  + [("kT", t) for t in range(KT)] + [("exp", i) for i in range(len(units))])
        with nc.Block() as block:
            @block.sync
            def _(sp):
                sp.dma_start(grow[:, 0, :], a["q_norm_g"][0].partition_broadcast(P)).then_inc(s_g, 16)
                sp.dma_start(grow[:, 1, :], a["kv_norm_g"][0].partition_broadcast(P)).then_inc(s_g, 16)
                sp.dma_start(ckv[:, 1, :], a["cache_ckv"][0, 0]).then_inc(s_cache, 16)
                sp.dma_start(kr[:, 1, :], a["cache_krope"][0, 0]).then_inc(s_cache, 16)
                sp.dma_start(wuq[:], a["w_uq"][0].rearrange("(p j) n -> p j n", j=KL)).then_inc(s_w, 16)
                sp.dma_start(wukv[:], a["w_ukv"][0].rearrange("(p j) n -> p j n", j=KL)).then_inc(s_w, 16)
                sp.dma_start(o["krope"][0, 0], g.small[:, 0, 0:ROPE]).then_inc(s_out, 16)
                sp.wait_ge(dve_done, V["ckv"])
                sp.dma_start(o["ckv"][0, 0], ckv[:, 0, :]).then_inc(s_out, 16)
                sp.wait_ge(s_out, 32)

            @block.scalar
            def _(act):
                for i in range(6):
                    t, part = i % 3, i // 3
                    junk = cqn[:, t, :] if part == 0 else ckv[:, (0, 2, 3)[t], :]
                    act.activation(junk, g.cqkv[:, t, part * LORA:(part + 1) * LORA], ACT.Square,
                                   accum_out=stat[:, 0, i:i + 1]).then_inc(act_done, A.step("ss", i))
                act.wait_ge(dve_done, V["rms"])
                act.activation(stat[:, 3, :], stat[:, 2, :], ACT.Sqrt).then_inc(act_done, A.step("rs"))
                act.wait_ge(pe_done, PE["ckvT"])
                act.activation(ckvT[:], ps[:, 2:4, :], ACT.Copy).then_inc(act_done, A.step("ckvT"))
                for t in range(KT):
                    b = 2 * (t % 2)
                    act.wait_ge(pe_done, PE[("kv", t)])
                    src = ps[:, b:b + 2, :].rearrange("p b (h e) -> p (b h) e", e=P)
                    act.activation(k[:, t, :, 0:NOPE], src[:, :, 0:NOPE], ACT.Copy)
                    act.activation(v[:, t], src[:, :, NOPE:P], ACT.Copy).then_inc(act_done, A.step("kv", t))
                for t in range(KT):
                    b = 2 * (t % 2)
                    act.wait_ge(pe_done, PE[("kT", t)])
                    act.activation(kT[:, :, t * P:(t + 1) * P],
                                   ps[0:QK, b:b + 2, :].rearrange("p b (h e) -> p (b h) e", e=P), ACT.Copy) \
                        .then_inc(act_done, A.step("kT", t))
                for i, (t, h) in enumerate(units):
                    w = nk(t) * P
                    act.wait_ge(dve_done, V[("max", i)])
                    if i >= 2:
                        act.wait_ge(pe_done, PE[("probT", i - 2)])
                    act.activation(prob[:, i % 2, 0:w], ps[:, i % 2, 0:w], ACT.Exp, bias=nmax[:, t, h:h + 1],
                                   accum_out=rsum[:, t, h:h + 1]).then_inc(act_done, A.step("exp", i))

            @block.tensor
            def _(pe):
                pe.wait_ge(dve_done, V["cqn"])
                for j in range(KL):
                    for t in range(TILES):
                        mm = pe.transpose(ps[:, j, t * P:(t + 1) * P], cqn[:, t, j::KL], c["ident"])
                mm.then_inc(pe_done, PE.step("cqT"))
                pe.wait_ge(dve_done, V["ckv"])
                pe.wait_ge(s_cache, 32)
                for j in range(KL):
                    for t in range(KT):
                        mm = pe.transpose(ps[:, 2 + j, t * P:(t + 1) * P], ckv[:, t, j::KL], c["ident"])
                mm.then_inc(pe_done, PE.step("ckvT"))
                pe.wait_ge(s_w, 32)
                pe.wait_ge(dve_done, V["cqT"])
                for t in range(TILES):
                    b = 4 + 2 * (t % 2)
                    if t >= 2:
                        pe.wait_ge(dve_done, V[("q", t - 2)])
                    for lo, hi in ((0, 512), (512, MH * QK)):
                        for j in range(KL):
                            mm = pe.matmul(ps[:, b + lo // 512, 0:hi - lo], cqT[:, j, t * P:(t + 1) * P],
                                           wuq[:, j, lo:hi], start=(j == 0), stop=(j == KL - 1))
                    mm.then_inc(pe_done, PE.step("q", t))
                pe.wait_ge(act_done, A["ckvT"])
                for t in range(KT):
                    b = 2 * (t % 2)
                    if t >= 2:
                        pe.wait_ge(act_done, A[("kv", t - 2)])
                    for n in range(2):
                        for j in range(KL):
                            mm = pe.matmul(ps[:, b + n, :], ckvT[:, j, t * P:(t + 1) * P],
                                           wukv[:, j, n * 512:(n + 1) * 512], start=(j == 0), stop=(j == KL - 1))
                    mm.then_inc(pe_done, PE.step("kv", t))
                for t in range(TILES):
                    b = 4 + 2 * (t % 2)
                    pe.wait_ge(dve_done, V[("q2", "b")])
                    if t >= 2:
                        pe.wait_ge(dve_done, V[("qT", t - 2)])
                    for h in range(MH):
                        mm = pe.transpose(ps[0:QK, b + h // 4, (h % 4) * P:(h % 4 + 1) * P], q[:, t, h, :], c["ident"])
                    mm.then_inc(pe_done, PE.step("qT", t))
                for t in range(KT):
                    b = 2 * (t % 2)
                    pe.wait_ge(act_done, A[("kv", KT - 1)])
                    pe.wait_ge(dve_done, V[("kr", t)])
                    if t >= 2:
                        pe.wait_ge(act_done, A[("kT", t - 2)])
                    for h in range(MH):
                        mm = pe.transpose(ps[0:QK, b + h // 4, (h % 4) * P:(h % 4 + 1) * P], k[:, t, h, :], c["ident"])
                    mm.then_inc(pe_done, PE.step("kT", t))
                pe.wait_ge(act_done, A[("kT", KT - 1)])
                pe.wait_ge(dve_done, V[("qT", TILES - 1)])
                for i in range(len(units) + 2):
                    if i < len(units):
                        t, h = units[i]
                        if i >= 2:
                            pe.wait_ge(act_done, A[("exp", i - 2)])
                        pe.matmul(ps[:, i % 2, 0:nk(t) * P], qT[:, h, t * P:(t + 1) * P],
                                  kT[:, h, k0(t) * P:(k0(t) + nk(t)) * P], start=True, stop=True) \
                            .then_inc(pe_done, PE.step("score", i))
                    if 1 <= i <= len(units):
                        u = i - 1
                        t, h = units[u]
                        pe.wait_ge(act_done, A[("exp", u)])
                        if u >= 2:
                            pe.wait_ge(dve_done, V[("probT", u - 2)])
                        for n in range(nk(t)):
                            mm = pe.transpose(ps[:, 2 + u % 2, n * P:(n + 1) * P],
                                              prob[:, u % 2, n * P:(n + 1) * P], c["ident"])
                        mm.then_inc(pe_done, PE.step("probT", u))
                    if i >= 2:
                        u = i - 2
                        t, h = units[u]
                        pe.wait_ge(dve_done, V[("probT", u)])
                        for n in range(nk(t)):
                            mm = pe.matmul(ps[:, 4 + t, h * VH:(h + 1) * VH], probT[:, u % 2, n, :],
                                           v[:, k0(t) + n, h, :], start=(n == 0), stop=(n == nk(t) - 1))
                        mm.then_inc(pe_done, PE.step("pv", u))

            @block.vector
            def _(dve):
                dve.wait_ge(act_done, A[("ss", 5)])
                dve.tensor_scalar(stat[:, 1, :], stat[:, 0, :], 1.0 / LORA, EPS, ALU.mult, ALU.add) \
                    .then_inc(dve_done, V.step("ms"))
                dve.wait_ge(dve_done, V["ms"])
                dve.reciprocal(stat[:, 2, :], stat[:, 1, :]).then_inc(dve_done, V.step("rms"))
                dve.wait_ge(act_done, A["rs"])
                dve.wait_ge(s_g, 32)
                for t in range(TILES):
                    i = dve.tensor_scalar(cqn[:, t, :], g.cqkv[:, t, 0:LORA], stat[:, 3, t:t + 1], None, ALU.mult)
                i.then_inc(dve_done, V.step("cqn0"))
                dve.wait_ge(dve_done, V["cqn0"])
                dve.tensor_tensor(cqn[:], cqn[:], over(grow[:, 0, :], TILES, 1), ALU.mult) \
                    .then_inc(dve_done, V.step("cqn"))
                key = (0, 2, 3)
                for t in range(TILES):
                    i = dve.tensor_scalar(ckv[:, key[t], :], g.cqkv[:, t, LORA:2 * LORA], stat[:, 3, 3 + t:4 + t],
                                          None, ALU.mult)
                i.then_inc(dve_done, V.step("ckv0"))
                dve.wait_ge(dve_done, V["ckv0"])
                for t in range(TILES):
                    i = dve.tensor_tensor(ckv[:, key[t], :], ckv[:, key[t], :], grow[:, 1, :], ALU.mult)
                i.then_inc(dve_done, V.step("ckv"))

                def rotate(name, dst, src, heads, t):
                    r = lambda n: rope[:, n, 0:heads]
                    x = src.rearrange("p h (x s f) -> p h x s f", x=2, s=2)
                    y = dst.rearrange("p h (x s f) -> p h x s f", x=2, s=2)
                    tab = lambda n: over(c[n][:, (t - 1) * 16:t * 16].rearrange("p (x f) -> p x f", x=2), heads, 1)
                    dve.tensor_tensor(r(0), x[:, :, :, 0], tab("cos"), ALU.mult).then_inc(dve_done, V.step(name, "ac"))
                    dve.tensor_tensor(r(1), x[:, :, :, 1], tab("sin"), ALU.mult).then_inc(dve_done, V.step(name, "bs"))
                    dve.tensor_tensor(r(2), x[:, :, :, 1], tab("cos"), ALU.mult).then_inc(dve_done, V.step(name, "bc"))
                    dve.tensor_tensor(r(3), x[:, :, :, 0], tab("sin"), ALU.mult).then_inc(dve_done, V.step(name, "as"))
                    dve.wait_ge(dve_done, V[(name, "as")])
                    dve.tensor_tensor(y[:, :, :, 0], r(0), r(1), ALU.subtract).then_inc(dve_done, V.step(name, "a"))
                    dve.tensor_tensor(y[:, :, :, 1], r(2), r(3), ALU.add).then_inc(dve_done, V.step(name, "b"))
                    dve.wait_ge(dve_done, V[(name, "b")])

                for t in (1, 2):
                    rotate(f"kr{t}", kr[:, t + 1:t + 2, :], g.small[:, t:t + 1, 0:ROPE], 1, t)
                dve.wait_ge(pe_done, PE["cqT"])
                dve.tensor_copy(cqT[:], ps[:, 0:2, 0:TOK]).then_inc(dve_done, V.step("cqT"))
                for t in range(TILES):
                    b = 4 + 2 * (t % 2)
                    dve.wait_ge(pe_done, PE[("q", t)])
                    flat = q[:, t].rearrange("p h e -> p (h e)")
                    dve.tensor_scalar(flat[:, 0:512], ps[:, b, :], SCALE, None, ALU.mult)
                    dve.tensor_scalar(flat[:, 512:MH * QK], ps[:, b + 1, 0:MH * QK - 512], SCALE, None, ALU.mult) \
                        .then_inc(dve_done, V.step("q", t))
                dve.wait_ge(dve_done, V[("q", TILES - 1)])
                for t in (1, 2):
                    rotate(f"q{t}", q[:, t, :, NOPE:QK], q[:, t, :, NOPE:QK], MH, t)
                dve.wait_ge(s_cache, 32)
                for t in range(KT):
                    src = g.small[:, 0, 0:ROPE] if t == 0 else kr[:, t, :]
                    dve.tensor_copy(k[:, t, :, NOPE:QK], over(src, MH, 1)).then_inc(dve_done, V.step("kr", t))
                for t in range(TILES):
                    b = 4 + 2 * (t % 2)
                    dve.wait_ge(pe_done, PE[("qT", t)])
                    dve.tensor_copy(qT[:, :, t * P:(t + 1) * P],
                                    ps[0:QK, b:b + 2, :].rearrange("p b (h e) -> p (b h) e", e=P)) \
                        .then_inc(dve_done, V.step("qT", t))
                for i in range(len(units) + 2):
                    if i < len(units):
                        t, h = units[i]
                        dve.wait_ge(pe_done, PE[("score", i)])
                        dve.tensor_reduce(nmax[:, t, h:h + 1], ps[:, i % 2, 0:nk(t) * P], AX, ALU.max, negate=True) \
                            .then_inc(dve_done, V.step("max", i))
                    if 1 <= i <= len(units):
                        u = i - 1
                        t, h = units[u]
                        dve.wait_ge(pe_done, PE[("probT", u)])
                        if u >= 2:
                            dve.wait_ge(pe_done, PE[("pv", u - 2)])
                        dve.tensor_copy(probT[:, u % 2, 0:nk(t), :].rearrange("p n q -> p (n q)"),
                                        ps[:, 2 + u % 2, 0:nk(t) * P]).then_inc(dve_done, V.step("probT", u))
                dve.wait_ge(act_done, A[("exp", len(units) - 1)])
                dve.reciprocal(rinv[:], rsum[:]).then_inc(dve_done, V.step("rinv"))
                dve.wait_ge(dve_done, V["rinv"])
                dve.wait_ge(pe_done, PE[("pv", len(units) - 1)])
                for t in range(TILES):
                    i = dve.tensor_tensor(g.omla[:, t, :].rearrange("p (h e) -> p h e", h=MH),
                                          ps[:, 4 + t, :].rearrange("p (h e) -> p h e", h=MH),
                                          over(rinv[:, t, :], VH, 2), ALU.mult)
                i.then_inc(dve_done, V.step("o"))


def phase_delta(nc, g):
    a, ps, c, o = g.a, g.ps, g.c, g.o
    H2 = GH // 2
    N48 = 2 * TILES * GH
    DIRS = (0, 1)
    STORE = {0: 1, 1: 0, 2: 1}
    TR = [(t, r) for t in range(TILES) for r in DIRS]
    GROUPS_ = {0: [(0, 0), (0, 1)], 1: [(1, 0), (1, 1), (2, 0), (2, 1)]}
    SCANS = [(grp, n, r) for grp in (0, 1) for n in range(len(GROUPS_[grp])) for r in DIRS]

    def where(grp, n, r):
        seq = GROUPS_[grp]
        return seq[n] if r == 0 else seq[len(seq) - 1 - n]

    with ExitStack() as ctx:
        def sb(name, shape):
            return ctx.enter_context(nc.sbuf_tensor(name, shape, F32))
        ktok = sb("ktok", [P, TILES, GW])
        vtok = sb("vtok", [P, TILES, GW])
        LT = sb("LT", [P, 2, GH, P])
        X = sb("X", [P, 2, GH, P])
        Y = sb("Y", [P, 2, GH, P])
        PR = sb("PR", [P, 2, GH, P])
        kb = sb("kb", [P, 2, GW])
        kbg = sb("kbg", [P, 2, GW])
        vb = sb("vb", [P, 2, GW])
        kbT = LT[:, :, 0:H2, :]
        u = sb("u", [P, 2, 2, GH, DV])
        wT = sb("wT", [P, 2, 2, H2, P])
        aT = sb("aT", [P, 2, 2, GH, P])
        kd = sb("kd", [P, 2, 2, GW])
        S = sb("S", [P, 2, H2, DV])
        flatX = X[:].rearrange("p r h n -> p r (h n)")
        vn = flatX[:, :, 0:GW].rearrange("p r (s e) -> p r s e", s=GH)
        qs = flatX[:, :, GW:2 * GW].rearrange("p r (s e) -> p r s e", s=GH)
        og = g.qkv[:, 8:12, :].rearrange("p m n -> p (m n)")[:, 0:TILES * GW].rearrange(
            "p (t s e) -> p t s e", t=TILES, s=GH)
        sq = X[:].rearrange("p r h n -> p (r h n)")[:, 0:4 * OUTW].rearrange("p (m n) -> p m n", m=4)
        rn = Y[:].rearrange("p r h n -> p (r h n)")[:, 0:4 * OUTW].rearrange("p (m n) -> p m n", m=4)
        sq_out = LT[:].rearrange("p r h n -> p (r h n)")[:, 0:TILES * GW].rearrange(
            "p (t s e) -> p t s e", t=TILES, s=GH)
        arow = sb("arow", [P, 2, 2 * GH])
        gw = sb("gw", [P, 4, TILES, 2 * GH])
        gg = sb("gg", [P, TILES, 2, GH])
        beta = sb("beta", [P, TILES, 2, GH])
        gc = sb("gc", [P, 4, 2, TILES, GH])
        ex = sb("ex", [P, 4, 2, TILES, GH])
        glS = sb("glS", [P, 2, 2 * TILES, H2])
        gnrow = sb("gnrow", [P, DV])
        ostat = sb("ostat", [P, 4, TILES * GH])
        s_row, s_state, s_fin = g.sem("gdn_rows_loaded"), g.sem("state_loaded"), g.sem("state_stored")
        pe_done, dve_done, act_done, pool_done = (g.sem("gdn_" + n) for n in ("pe", "dve", "act", "pool"))

        def scan_after(t):
            return [s for s in SCANS if (s[0] == 0 and t == 0) or (s[0] == 1 and t == 2)]

        pe_o, dve_o, act_o, pool_o = [], [], [], ["state0", "og0"]
        for n in "qk":
            act_o += [("sq", n), ("root", n)]
            pe_o += [("norm", n)]
            dve_o += [("normeps", n), ("normrec", n), ("normed", n)]
        pe_o += ["vtok", "ktok"]
        act_o += ["vtok", "ktok"]
        dve_o += ["xa", "na"]
        act_o += ["expna", "ln", "expa", "expb"]
        dve_o += ["sp", "gg", "b1", "beta"]
        pe_o += ["cums"]
        dve_o += ["gc", "tdiff"]
        act_o += ["ex"]
        dve_o += ["glS"]
        for t in range(TILES):
            for r in DIRS:
                dve_o += [("kb", t, r), ("gtri", t, r)]
                pool_o += [("kbg", t, r), ("vb", t, r), ("kd", t, r)]
                pe_o += [("kbT", t, r), ("D", t, r)]
                act_o += [("kbT", t, r), ("E", t, r)]
            for r in DIRS:
                dve_o += [("D", t, r)]
                pool_o += [("Es", t, r), ("Ei", t, r)]
                pe_o += [("KK", t, r), ("QK", t, r)]
            for r in DIRS:
                dve_o += [("LT", t, r), ("aT", t, r)]
                pe_o += [("L", t, r)]
            for r in DIRS:
                dve_o += [("X1", t, r), ("Y1", t, r)]
                pool_o += [("X1", t, r), ("Y1", t, r)]
            for s in LEVELS[1:]:
                for r in DIRS:
                    pe_o += [("P", t, r, s)]
                    dve_o += [("P", t, r, s)]
                for r in DIRS:
                    if s != LEVELS[-1]:
                        pe_o += [("X", t, r, s)]
                    pe_o += [("Y", t, r, s)]
                for r in DIRS:
                    if s != LEVELS[-1]:
                        dve_o += [("X", t, r, s)]
                    dve_o += [("Y", t, r, s)]
            for r in DIRS:
                pe_o += [("u", t, r), ("wT", t, r)]
                dve_o += [("u", t, r)]
                act_o += [("wT", t, r)]
            for sc in scan_after(t):
                pe_o += [("RQ", sc), ("OU", sc)]
                dve_o += [("vn", sc), ("qs", sc), ("Sg", sc), ("S", sc), ("o1", sc), ("o2", sc)]
        act_o += ["silu", "osq", "ors"]
        dve_o += ["oss", "oms", "orec", "on", "og1", "out"]
        PE, V, A, G = Count(pe_o), Count(dve_o), Count(act_o), Count(pool_o)
        LAST = LEVELS[-1]
        slots = [(par * H2 + j, 2 * j + par, par, j) for par in range(2) for j in range(H2)]
        ctx_done = ("S", (0, 1, 1))

        def by_slot(x):
            return x.rearrange("p (j q) -> p q j", q=2)

        def heads(x):
            return x.rearrange("p (h d) -> p h d", h=GH)

        def banks(b):
            return ps[:, b:b + 2, :].rearrange("p b (j n) -> p (b j) n", j=H2)

        with nc.Block() as block:
            @block.sync
            def _(sp):
                sp.dma_start(arow[:, 0, :], a["a_log"][0].rearrange("r h -> (r h)").partition_broadcast(P)).then_inc(s_row, 16)
                sp.dma_start(arow[:, 1, :], a["dt_bias"][0].rearrange("r h -> (r h)").partition_broadcast(P)) \
                    .then_inc(s_row, 16)
                sp.dma_start(gnrow[:], a["gdn_norm_g"][0].partition_broadcast(P)).then_inc(s_row, 16)

                def state(x, r, par):
                    return x[0, 0, r].rearrange("(j q) k v -> q k j v", q=2)[par]

                sp.wait_ge(dve_done, V[ctx_done])
                for r in DIRS:
                    for par in range(2):
                        sp.dma_start(state(o["state"], r, par), S[par * DK:(par + 1) * DK, r]).then_inc(s_fin, 16)
                sp.wait_ge(s_fin, 64)
                for r in DIRS:
                    for par in range(2):
                        sp.dma_start(S[par * DK:(par + 1) * DK, r], state(a["state_delta"], r, par)).then_inc(s_state, 16)
                sp.wait_ge(s_state, 64)

            @block.gpsimd
            def _(pool):
                pool.memset(S[:], 0.0).then_inc(pool_done, G.step("state0"))
                pool.wait_ge(pe_done, PE["vtok"])
                pool.memset(og, 0.0).then_inc(pool_done, G.step("og0"))
                for t in range(TILES):
                    for r in DIRS:
                        d = STORE[t]
                        if t == 0 and r == 0:
                            pool.wait_ge(act_done, A["ktok"])
                            pool.wait_ge(dve_done, V["glS"])
                        if t:
                            pool.wait_ge(pe_done, PE[("wT", t - 1, 1)])
                        pool.wait_ge(dve_done, V[("kb", t, r)])
                        e = lambda n: over(ex[:, n, r, t, :], DK, 2)
                        pool.tensor_tensor(heads(kbg[:, r]), heads(kb[:, r]), e(0), ALU.mult) \
                            .then_inc(pool_done, G.step("kbg", t, r))
                        pool.tensor_tensor(heads(vb[:, r]), heads(vtok[:, t]), over(beta[:, t, r, :], DV, 2), ALU.mult) \
                            .then_inc(pool_done, G.step("vb", t, r))
                        if t == 2:
                            pool.wait_ge(pe_done, PE[("OU", (0, 1, 1))])
                        pool.tensor_tensor(heads(kd[:, d, r]), heads(ktok[:, t]), e(1), ALU.mult) \
                            .then_inc(pool_done, G.step("kd", t, r))
                    for r in DIRS:
                        pool.wait_ge(act_done, A[("E", t, r)])
                        pool.tensor_tensor(Y[:, r], PR[:, r], over(c[f"strict{r}"], GH, 1), ALU.mult) \
                            .then_inc(pool_done, G.step("Es", t, r))
                        pool.wait_ge(pe_done, PE[("D", t, r)])
                        pool.tensor_tensor(X[:, r], PR[:, r], over(c[f"incl{r}"], GH, 1), ALU.mult) \
                            .then_inc(pool_done, G.step("Ei", t, r))
                    for r in DIRS:
                        for n, Z in (("X1", X), ("Y1", Y)):
                            pool.wait_ge(dve_done, V[(n, t, r)])
                            pool.tensor_tensor(Z[:, r], Z[:, r], over(c["ident"], GH, 1), ALU.add) \
                                .then_inc(pool_done, G.step(n, t, r))

            @block.scalar
            def _(act):
                for i, n in enumerate("qk"):
                    if i:
                        act.wait_ge(pe_done, PE[("norm", "q")])
                    act.activation(sq, g.qkv[:, 4 * i:4 * i + 4, :], ACT.Square).then_inc(act_done, A.step("sq", n))
                    act.wait_ge(dve_done, V[("normrec", n)])
                    act.activation(rn, rn, ACT.Sqrt, scale=1.0 / DK if n == "q" else 1.0) \
                        .then_inc(act_done, A.step("root", n))
                act.wait_ge(pe_done, PE["vtok"])
                act.activation(vtok[:], ps[:, 0:TILES, :], ACT.Copy).then_inc(act_done, A.step("vtok"))
                act.wait_ge(pe_done, PE["ktok"])
                act.activation(ktok[:], ps[:, 3:3 + TILES, :], ACT.Copy).then_inc(act_done, A.step("ktok"))
                act.wait_ge(dve_done, V["na"])
                act.activation(gw[:, 1], gw[:, 1], ACT.Exp).then_inc(act_done, A.step("expna"))
                act.wait_ge(act_done, A["expna"])
                act.activation(gw[:, 2], gw[:, 1], ACT.Ln, bias=1.0).then_inc(act_done, A.step("ln"))
                act.wait_ge(s_row, 48)
                act.activation(arow[:, 0, :], arow[:, 0, :], ACT.Exp).then_inc(act_done, A.step("expa"))
                act.activation(gw[:, 3], g.small[:, :, 48:64], ACT.Exp, scale=-1.0).then_inc(act_done, A.step("expb"))
                act.wait_ge(dve_done, V["tdiff"])
                act.activation(ex[:, 0], gc[:, 0], ACT.Exp)
                act.activation(ex[:, 2:4], gc[:, 2:4], ACT.Exp)
                act.activation(ex[:, 1], ex[:, 1], ACT.Exp).then_inc(act_done, A.step("ex"))
                for t in range(TILES):
                    for r in DIRS:
                        act.wait_ge(pe_done, PE[("kbT", t, r)])
                        act.activation(kbT[:, r].rearrange("p j n -> p (j n)"), ps[:, 4 * r + 2, :], ACT.Copy) \
                            .then_inc(act_done, A.step("kbT", t, r))
                        act.wait_ge(dve_done, V[("D", t, r)])
                        act.activation(PR[:, r], PR[:, r], ACT.Exp).then_inc(act_done, A.step("E", t, r))
                    for r in DIRS:
                        act.wait_ge(pe_done, PE[("wT", t, r)])
                        if t == 2:
                            act.wait_ge(pe_done, PE[("OU", (0, 1, 1))])
                        act.activation(wT[:, STORE[t], r].rearrange("p j n -> p (j n)"), ps[:, 4 * r + 3, :],
                                       ACT.Copy).then_inc(act_done, A.step("wT", t, r))
                act.activation(g.z[:], g.z[:], ACT.Silu).then_inc(act_done, A.step("silu"))
                act.wait_ge(dve_done, V[("o2", SCANS[-1])])
                act.activation(sq_out, og, ACT.Square).then_inc(act_done, A.step("osq"))
                act.wait_ge(dve_done, V["orec"])
                act.activation(ostat[:, 3], ostat[:, 2], ACT.Sqrt).then_inc(act_done, A.step("ors"))

            @block.tensor
            def _(pe):
                for i, n in enumerate("qk"):
                    pe.wait_ge(act_done, A[("sq", n)])
                    for m in range(4):
                        mm = pe.matmul(ps[:, 4 * i + m, 0:OUTW], c["block"], sq[:, m, :], start=True, stop=True)
                    mm.then_inc(pe_done, PE.step("norm", n))
                pe.wait_ge(dve_done, V[("normeps", "q")])
                for t in range(TILES):
                    for m in range(4):
                        mm = pe.transpose(ps[:, t, m * P:(m + 1) * P], g.qkv[:, 8 + m, tok_at(t):tok_at(t) + P],
                                          c["ident"])
                mm.then_inc(pe_done, PE.step("vtok"))
                pe.wait_ge(dve_done, V[("normed", "k")])
                for t in range(TILES):
                    for m in range(4):
                        mm = pe.transpose(ps[:, 3 + t, m * P:(m + 1) * P], g.qkv[:, 4 + m, tok_at(t):tok_at(t) + P],
                                          c["ident"])
                mm.then_inc(pe_done, PE.step("ktok"))
                pe.wait_ge(dve_done, V["gg"])
                gv = gg[:].rearrange("p t r h -> p r t h")
                for r in DIRS:
                    pe.matmul(ps[:, 6, r * 24:(r + 1) * 24], c[f"incl{r}"], gv[:, r], start=True, stop=True)
                for n, m in enumerate(("block", "half0", "half1")):
                    mm = pe.matmul(ps[:, 6, (n + 1) * N48:(n + 2) * N48], c[m], gv, start=True, stop=True)
                mm.then_inc(pe_done, PE.step("cums"))
                for t in range(TILES):
                    tc = slice(tok_at(t), tok_at(t) + P)
                    for r in DIRS:
                        pe.wait_ge(dve_done, V[("kb", t, r)])
                        if t == 0:
                            pe.wait_ge(act_done, A["ktok"])
                            pe.wait_ge(dve_done, V["gc"])
                        else:
                            pe.wait_ge(dve_done, V[("u", t - 1, r)])
                            pe.wait_ge(act_done, A[("wT", t - 1, r)])
                            if t == 1:
                                pe.wait_ge(dve_done, V[("o2", (0, 1, r))])
                        for m in range(H2):
                            mm = pe.transpose(ps[:, 4 * r + 2, m * P:(m + 1) * P], kb[:, r, m * P:(m + 1) * P], c["ident"])
                        mm.then_inc(pe_done, PE.step("kbT", t, r))
                        pe.wait_ge(dve_done, V[("gtri", t, r)])
                        for b in range(2):
                            mm = pe.matmul(ps[:, 4 * r + b, :], c["ones"],
                                           X[:, r, 4 * b:4 * b + 4].rearrange("p h n -> p (h n)"), start=True, stop=True)
                        mm.then_inc(pe_done, PE.step("D", t, r))
                    for r in DIRS:
                        pe.wait_ge(act_done, A[("kbT", t, r)])
                        for s, h, par, j in slots:
                            rows = slice(par * DK, (par + 1) * DK)
                            mm = pe.matmul(ps[:, 4 * r + 2 + par, j * P:(j + 1) * P], g.qkv[rows, 4 + j, tc],
                                           kbT[rows, r, j, :], start=True, stop=True)
                        mm.then_inc(pe_done, PE.step("KK", t, r))
                        pe.wait_ge(dve_done, V[("D", t, r)])
                        for s, h, par, j in slots:
                            rows = slice(par * DK, (par + 1) * DK)
                            mm = pe.matmul(ps[:, 4 * r + par, j * P:(j + 1) * P], g.qkv[rows, 4 + j, tc],
                                           g.qkv[rows, j, tc], start=True, stop=True)
                        mm.then_inc(pe_done, PE.step("QK", t, r))
                    for r in DIRS:
                        pe.wait_ge(dve_done, V[("aT", t, r)])
                        for s, h, par, j in slots:
                            mm = pe.transpose(ps[:, 4 * r + par, j * P:(j + 1) * P], LT[:, r, s, :], c["ident"])
                        mm.then_inc(pe_done, PE.step("L", t, r))
                    for lv in LEVELS[1:]:
                        for r in DIRS:
                            if lv == 2:
                                pe.wait_ge(pool_done, G[("Y1", t, r)])
                            else:
                                pe.wait_ge(dve_done, V[("Y", t, r, lv // 2)])
                            for s, h, par, j in slots:
                                mm = pe.matmul(ps[:, 4 * r + par, j * P:(j + 1) * P], LT[:, r, s, :], X[:, r, s, :],
                                               start=True, stop=True)
                            mm.then_inc(pe_done, PE.step("P", t, r, lv))
                        for r in DIRS:
                            pe.wait_ge(dve_done, V[("P", t, r, lv)])
                            if lv != LAST:
                                for s, h, par, j in slots:
                                    mm = pe.matmul(ps[:, 4 * r + 2 + par, j * P:(j + 1) * P], Y[:, r, s, :],
                                                   PR[:, r, s, :], start=True, stop=True)
                                mm.then_inc(pe_done, PE.step("X", t, r, lv))
                            for s, h, par, j in slots:
                                mm = pe.matmul(ps[:, 4 * r + par, j * P:(j + 1) * P], PR[:, r, s, :], Y[:, r, s, :],
                                               start=True, stop=True)
                            mm.then_inc(pe_done, PE.step("Y", t, r, lv))
                    for r in DIRS:
                        pe.wait_ge(dve_done, V[("Y", t, r, LAST)])
                        pe.wait_ge(pool_done, G[("vb", t, r)])
                        for s, h, par, j in slots:
                            mm = pe.matmul(ps[:, 4 * r + 2, s * DV:(s + 1) * DV], Y[:, r, s, :],
                                           vb[:, r, h * DV:(h + 1) * DV], start=True, stop=True)
                        mm.then_inc(pe_done, PE.step("u", t, r))
                        for s, h, par, j in slots:
                            mm = pe.matmul(ps[par * DK:(par + 1) * DK, 4 * r + 3, j * P:(j + 1) * P],
                                           kbg[:, r, h * DK:(h + 1) * DK], Y[:, r, s, :], start=True, stop=True)
                        mm.then_inc(pe_done, PE.step("wT", t, r))
                    for sc in scan_after(t):
                        grp, n, r = sc
                        st, half = where(*sc)
                        d, lo = STORE[st], half * CHUNK
                        rr = slice(lo, lo + CHUNK)
                        if n == 0:
                            pe.wait_ge(act_done, A[("wT", t, r)])
                            pe.wait_ge(dve_done, V[("u", t, r)])
                            if grp == 0:
                                pe.wait_ge(pool_done, G["state0"])
                            else:
                                pe.wait_ge(s_state, 64)
                        else:
                            pe.wait_ge(dve_done, V[("o2", (grp, n - 1, r))])
                        for s, h, par, j in slots:
                            rows = slice(par * DK, (par + 1) * DK)
                            pe.matmul(ps[rr, 4 * r + par, j * DV:(j + 1) * DV], wT[rows, d, r, j, rr], S[rows, r, j, :],
                                      start=True, stop=True)
                            mm = pe.matmul(ps[rr, 4 * r + par, (H2 + j) * DV:(H2 + j + 1) * DV],
                                           g.qkv[rows, j, tok_at(st) + lo:tok_at(st) + lo + CHUNK], S[rows, r, j, :],
                                           start=True, stop=True)
                        mm.then_inc(pe_done, PE.step("RQ", sc))
                        pe.wait_ge(dve_done, V[("vn", sc)])
                        pe.wait_ge(pool_done, G[("kd", st, r)])
                        for s, h, par, j in slots:
                            pe.matmul(ps[par * DK:(par + 1) * DK, 4 * r + 3, j * DV:(j + 1) * DV],
                                      kd[rr, d, r, h * DK:(h + 1) * DK], vn[rr, r, s, :], start=True, stop=True)
                        for s, h, par, j in slots:
                            mm = pe.matmul(ps[rr, 4 * r + 2, s * DV:(s + 1) * DV], aT[rr, d, r, s, rr], vn[rr, r, s, :],
                                           start=True, stop=True)
                        mm.then_inc(pe_done, PE.step("OU", sc))

            @block.vector
            def _(dve):
                def norm(n):
                    i = "qk".index(n)
                    dve.wait_ge(pe_done, PE[("norm", n)])
                    if i:
                        dve.wait_ge(dve_done, V[("normed", "q")])
                    dve.tensor_scalar(rn, ps[:, 4 * i:4 * i + 4, 0:OUTW], EPS, None, ALU.add) \
                        .then_inc(dve_done, V.step("normeps", n))
                    dve.wait_ge(dve_done, V[("normeps", n)])
                    dve.reciprocal(rn, rn).then_inc(dve_done, V.step("normrec", n))
                    dve.wait_ge(act_done, A[("root", n)])
                    dve.tensor_tensor(g.qkv[:, 4 * i:4 * i + 4, :], g.qkv[:, 4 * i:4 * i + 4, :], rn, ALU.mult) \
                        .then_inc(dve_done, V.step("normed", n))

                norm("q")
                norm("k")
                dve.wait_ge(s_row, 48)
                dve.tensor_tensor(gw[:, 0], g.small[:, :, 32:48], over(arow[:, 1, :], TILES, 1), ALU.add) \
                    .then_inc(dve_done, V.step("xa"))
                dve.wait_ge(dve_done, V["xa"])
                dve.scalar_tensor_tensor(out=gw[:, 1], in0=gw[:, 0], scalar=-1.0, in1=gw[:, 0], op0=ALU.mult,
                                         op1=ALU.min).then_inc(dve_done, V.step("na"))
                dve.wait_ge(act_done, A["expb"])
                dve.scalar_tensor_tensor(out=gw[:, 2], in0=gw[:, 0], scalar=0.0, in1=gw[:, 2], op0=ALU.max,
                                         op1=ALU.add).then_inc(dve_done, V.step("sp"))
                dve.wait_ge(dve_done, V["sp"])
                dve.scalar_tensor_tensor(out=gg[:].rearrange("p t r h -> p t (r h)"), in0=gw[:, 2], scalar=-1.0,
                                         in1=over(arow[:, 0, :], TILES, 1), op0=ALU.mult, op1=ALU.mult) \
                    .then_inc(dve_done, V.step("gg"))
                dve.tensor_scalar(gw[:, 3], gw[:, 3], 1.0, None, ALU.add).then_inc(dve_done, V.step("b1"))
                dve.wait_ge(dve_done, V["b1"])
                dve.reciprocal(beta[:].rearrange("p t r h -> p t (r h)"), gw[:, 3]).then_inc(dve_done, V.step("beta"))
                dve.wait_ge(pe_done, PE["cums"])
                dve.tensor_copy(gc[:].rearrange("p n r t h -> p (n r t h)"), ps[:, 6, 0:4 * N48]) \
                    .then_inc(dve_done, V.step("gc"))
                dve.wait_ge(dve_done, V["gc"])
                dve.tensor_tensor(ex[:, 1], gc[:, 1], gc[:, 0], ALU.subtract).then_inc(dve_done, V.step("tdiff"))
                dve.wait_ge(act_done, A["ex"])
                for par in range(2):
                    rows = slice(par * DK, (par + 1) * DK)
                    i = dve.tensor_copy(glS[rows], ex[rows, 2:4, :, :, par::2].rearrange("p n r t j -> p n (r t) j"))
                i.then_inc(dve_done, V.step("glS"))
                for t in range(TILES):
                    d = STORE[t]
                    for r in DIRS:
                        if t == 0:
                            dve.wait_ge(act_done, A["ktok"])
                            dve.wait_ge(dve_done, V["glS"])
                        else:
                            dve.wait_ge(pool_done, G[("kbg", t - 1, r)])
                            dve.wait_ge(pe_done, PE[("wT", t - 1, 1)])
                            if t == 1:
                                dve.wait_ge(pe_done, PE[("OU", (0, 1, 1))])
                                dve.wait_ge(dve_done, V[("o2", (0, 1, 1))])
                        dve.tensor_tensor(heads(kb[:, r]), heads(ktok[:, t]), over(beta[:, t, r, :], DK, 2), ALU.mult) \
                            .then_inc(dve_done, V.step("kb", t, r))
                        for par in range(2):
                            i = dve.tensor_tensor(X[:, r, par * H2:(par + 1) * H2], over(c[f"incl{r}"], H2, 1),
                                                  over(gg[:, t, r, par::2], P, 2), ALU.mult)
                        i.then_inc(dve_done, V.step("gtri", t, r))
                    for r in DIRS:
                        dve.wait_ge(pe_done, PE[("D", t, r)])
                        for s, h, par, j in slots:
                            i = dve.tensor_scalar(PR[:, r, s, :], ps[:, 4 * r + par, j * P:(j + 1) * P],
                                                  gc[:, 0, r, t, h:h + 1], 0.0, ALU.subtract, ALU.min)
                        i.then_inc(dve_done, V.step("D", t, r))
                    for r in DIRS:
                        dve.wait_ge(pe_done, PE[("KK", t, r)])
                        dve.wait_ge(pool_done, G[("Es", t, r)])
                        dve.tensor_tensor(LT[:, r], banks(4 * r + 2), Y[:, r], ALU.mult) \
                            .then_inc(dve_done, V.step("LT", t, r))
                        dve.wait_ge(pe_done, PE[("QK", t, r)])
                        dve.wait_ge(pool_done, G[("Ei", t, r)])
                        if t == 2:
                            dve.wait_ge(pe_done, PE[("OU", (0, 1, 1))])
                        dve.tensor_tensor(aT[:, d, r], banks(4 * r), X[:, r], ALU.mult) \
                            .then_inc(dve_done, V.step("aT", t, r))
                    for r in DIRS:
                        dve.wait_ge(pe_done, PE[("L", t, r)])
                        dve.wait_ge(dve_done, V[("aT", t, r)])
                        dve.scalar_tensor_tensor(out=X[:, r], in0=banks(4 * r), scalar=-1.0,
                                                 in1=over(c[f"level{r}_1"], GH, 1), op0=ALU.mult, op1=ALU.mult) \
                            .then_inc(dve_done, V.step("X1", t, r))
                        dve.scalar_tensor_tensor(out=Y[:, r], in0=LT[:, r], scalar=-1.0,
                                                 in1=over(c[f"level{1 - r}_1"], GH, 1), op0=ALU.mult, op1=ALU.mult) \
                            .then_inc(dve_done, V.step("Y1", t, r))
                    for lv in LEVELS[1:]:
                        for r in DIRS:
                            dve.wait_ge(pe_done, PE[("P", t, r, lv)])
                            dve.tensor_tensor(PR[:, r], banks(4 * r), over(c[f"level{r}_{lv}"], GH, 1), ALU.mult) \
                                .then_inc(dve_done, V.step("P", t, r, lv))
                        for r in DIRS:
                            if lv != LAST:
                                dve.wait_ge(pe_done, PE[("Y", t, r, lv)])
                                dve.tensor_tensor(X[:, r], X[:, r], banks(4 * r + 2), ALU.subtract) \
                                    .then_inc(dve_done, V.step("X", t, r, lv))
                            dve.wait_ge(pe_done, PE[("Y", t, r, lv)])
                            dve.tensor_tensor(Y[:, r], Y[:, r], banks(4 * r), ALU.subtract) \
                                .then_inc(dve_done, V.step("Y", t, r, lv))
                    for r in DIRS:
                        dve.wait_ge(pe_done, PE[("u", t, r)])
                        dve.tensor_copy(u[:, d, r].rearrange("p s e -> p (s e)"), ps[:, 4 * r + 2, :]) \
                            .then_inc(dve_done, V.step("u", t, r))
                    for sc in scan_after(t):
                        grp, n, r = sc
                        st, half = where(*sc)
                        sd, rr = STORE[st], slice(half * CHUNK, (half + 1) * CHUNK)
                        pair = lambda lo: ps[rr, 4 * r:4 * r + 2, lo:lo + H2 * DV].rearrange(
                            "p b (j e) -> p b j e", j=H2)
                        sl = lambda x: x.rearrange("p (q j) e -> p q j e", q=2)
                        dve.wait_ge(pe_done, PE[("RQ", sc)])
                        dve.tensor_tensor(sl(vn[rr, r]), sl(u[rr, sd, r]), pair(0), ALU.subtract) \
                            .then_inc(dve_done, V.step("vn", sc))
                        for par in range(2):
                            i = dve.tensor_tensor(qs[rr, r, par * H2:(par + 1) * H2],
                                                  ps[rr, 4 * r + par, H2 * DV:2 * H2 * DV].rearrange(
                                                      "p (j e) -> p j e", j=H2),
                                                  over(ex[rr, 0, r, st, par::2], DV, 2), ALU.mult)
                        i.then_inc(dve_done, V.step("qs", sc))
                        dve.tensor_tensor(S[:, r], S[:, r], over(glS[:, half, r * TILES + st, :], DV, 2), ALU.mult) \
                            .then_inc(dve_done, V.step("Sg", sc))
                        dve.wait_ge(pe_done, PE[("OU", sc)])
                        dve.wait_ge(dve_done, V[("Sg", sc)])
                        dve.tensor_tensor(S[:, r], S[:, r], ps[:, 4 * r + 3, 0:H2 * DV].rearrange(
                            "p (j e) -> p j e", j=H2), ALU.add).then_inc(dve_done, V.step("S", sc))
                        dve.wait_ge(pool_done, G["og0"])
                        dve.tensor_tensor(qs[rr, r], qs[rr, r], ps[rr, 4 * r + 2, :].rearrange(
                            "p (s e) -> p s e", s=GH), ALU.add).then_inc(dve_done, V.step("o1", sc))
                        dve.wait_ge(dve_done, V[("o1", sc)])
                        dve.tensor_tensor(og[rr, st], og[rr, st], qs[rr, r], ALU.add) \
                            .then_inc(dve_done, V.step("o2", sc))
                flat = og.rearrange("p t s e -> p (t s) e")
                dve.wait_ge(act_done, A["osq"])
                dve.tensor_reduce(ostat[:, 0], sq_out.rearrange("p t s e -> p (t s) e"), AX, ALU.add) \
                    .then_inc(dve_done, V.step("oss"))
                dve.wait_ge(dve_done, V["oss"])
                dve.tensor_scalar(ostat[:, 1], ostat[:, 0], 1.0 / DV, EPS, ALU.mult, ALU.add) \
                    .then_inc(dve_done, V.step("oms"))
                dve.wait_ge(dve_done, V["oms"])
                dve.reciprocal(ostat[:, 2], ostat[:, 1]).then_inc(dve_done, V.step("orec"))
                dve.wait_ge(act_done, A["ors"])
                dve.tensor_tensor(flat, flat, over(ostat[:, 3], DV, 2), ALU.mult).then_inc(dve_done, V.step("on"))
                dve.wait_ge(dve_done, V["on"])
                dve.tensor_tensor(flat, flat, over(gnrow[:], TILES * GH, 1), ALU.mult).then_inc(dve_done, V.step("og1"))
                dve.wait_ge(dve_done, V["og1"])
                for t in range(TILES):
                    zt = g.z[:, t].rearrange("p (j q e) -> p q j e", j=H2, q=2)
                    i = dve.tensor_tensor(zt, zt, og[:, t].rearrange("p (q j) e -> p q j e", q=2), ALU.mult)
                i.then_inc(dve_done, V.step("out"))


def phase_merge(nc, g):
    a, ps, c = g.a, g.ps, g.c
    KO = GW // P
    with ExitStack() as ctx:
        def sb(name, shape):
            return ctx.enter_context(nc.sbuf_tensor(name, shape, F32))
        wo2 = sb("wo2", [P, 2, KO, D])
        wo = sb("wo", [P, KD, D])
        oT = sb("oT", [P, 2, KO, TOK])
        sg = sb("sg", [P, 2, 2, 512])
        merged = sb("merged", [P, TILES, D])
        gate = sb("gate", [P, 2, D])
        gpost = sb("gpost", [P, D])
        stat = sb("mstat", [P, 4, TILES])
        mT = g.hT
        s_wo2, s_wo, s_x, s_row = (g.sem(n) for n in ("wo2_loaded", "wo_loaded", "x_again_loaded", "gate1_loaded"))
        pe_done, dve_done, act_done, pool_done = (g.sem("merge_" + n) for n in ("pe", "dve", "act", "pool"))
        units = [(n, t) for n in range(2) for t in range(TILES)]
        PE = Count([("oT", w, t) for w in range(2) for t in range(TILES)]
                   + [(x, u) for u in units for x in ("y", "g")]
                   + [("mT", t) for t in range(TILES)] + [("o", t) for t in range(TILES)])
        A = Count([("oT", w, t) for w in range(2) for t in range(TILES)] + [("sig", u) for u in units]
                  + [("mT", t) for t in range(TILES)] + [("ss", t) for t in range(TILES)] + ["rs"])
        V = Count([(x, u) for u in units for x in ("a", "b")] + ["ms", "rec"]
                  + [(x, t) for t in range(TILES) for x in ("yn", "x1")])
        G = Count(["gate"] + [("sum", u) for u in units])
        with nc.Block() as block:
            @block.sync
            def _(sp):
                sp.dma_start(wo2[:, 0], a["w_oa"][0].rearrange("(p k) n -> p k n", k=KO)).then_inc(s_wo2, 16)
                sp.dma_start(wo2[:, 1], a["w_ob"][0].rearrange("(p k) n -> p k n", k=KO)).then_inc(s_wo2, 16)
                for v in range(2):
                    sp.dma_start(gate[:, v], g.mods_dram[v, 2].partition_broadcast(P)).then_inc(s_row, 16)
                sp.dma_start(gpost[:], a["g_post_mix"][0].partition_broadcast(P)).then_inc(s_row, 16)
                sp.dma_start(wo[:], a["w_o"][0].rearrange("(p k) n -> p k n", k=KD)).then_inc(s_wo, 16)
                sp.dma_start(g.x1[:, 0, :], a["x_prompt"][0]).then_inc(s_x, 16)
                sp.dma_start(g.x1[:, 1:3, :], a["x_sample"][0].rearrange("(t p) d -> p t d", p=P)).then_inc(s_x, 16)
                n = LOAD["gb1"]
                sp.wait_ge(pe_done, PE[("g", (0, TILES - 1))])
                sp.dma_start(g.ring[:, slot(n)], ring_source(g, n)).then_inc(g.s_slot[slot(n)], 16)

            @block.gpsimd
            def _(pool):
                pool.wait_ge(s_row, 48)
                pool.tensor_tensor(gate[:], gate[:], over(gpost[:], 2, 1), ALU.mult).then_inc(pool_done, G.step("gate"))
                for i, (n, t) in enumerate(units):
                    pool.wait_ge(dve_done, V[("b", (n, t))])
                    pool.tensor_tensor(merged[:, t, n * 512:(n + 1) * 512], sg[:, i % 2, 0, :], sg[:, i % 2, 1, :],
                                       ALU.add).then_inc(pool_done, G.step("sum", (n, t)))

            @block.scalar
            def _(act):
                for w in range(2):
                    for t in range(TILES):
                        act.wait_ge(pe_done, PE[("oT", w, t)])
                        act.activation(oT[:, w, :, t * P:(t + 1) * P],
                                       ps[:, 3 * w + t, :].rearrange("p (k n) -> p k n", k=KO), ACT.Copy) \
                            .then_inc(act_done, A.step("oT", w, t))
                for i, u in enumerate(units):
                    b = 4 * (i % 2)
                    act.wait_ge(pe_done, PE[("g", u)])
                    if i >= 2:
                        act.wait_ge(pool_done, G[("sum", units[i - 2])])
                    act.activation(sg[:, i % 2], ps[:, b + 2:b + 4, :], ACT.Sigmoid).then_inc(act_done, A.step("sig", u))
                for t in range(TILES):
                    act.wait_ge(pe_done, PE[("mT", t)])
                    act.activation(mT[:, :, t * P:(t + 1) * P],
                                   ps[:, 2 * t:2 * t + 2, :].rearrange("p b (k n) -> p (b k) n", k=4), ACT.Copy) \
                        .then_inc(act_done, A.step("mT", t))
                for t in range(TILES):
                    b = (6, 0, 2)[t]
                    act.wait_ge(pe_done, PE[("o", t)])
                    act.activation(merged[:, t, :].rearrange("p (b n) -> p b n", b=2), ps[:, b:b + 2, :], ACT.Square,
                                   accum_out=stat[:, 0, t:t + 1]).then_inc(act_done, A.step("ss", t))
                act.wait_ge(dve_done, V["rec"])
                act.activation(stat[:, 3], stat[:, 2], ACT.Sqrt).then_inc(act_done, A.step("rs"))

            @block.tensor
            def _(pe):
                for w, src in enumerate((g.omla, g.z)):
                    for t in range(TILES):
                        for k in range(KO):
                            mm = pe.transpose(ps[:, 3 * w + t, k * P:(k + 1) * P], src[:, t, k::KO], c["ident"])
                        mm.then_inc(pe_done, PE.step("oT", w, t))
                pe.wait_ge(s_wo2, 32)
                pe.wait_ge(act_done, A[("oT", 1, TILES - 1)])
                for i, (n, t) in enumerate(units):
                    b = 4 * (i % 2)
                    if i >= 2:
                        pe.wait_ge(dve_done, V[("b", units[i - 2])])
                    for w in range(2):
                        for k in range(KO):
                            mm = pe.matmul(ps[:, b + w, :], oT[:, w, k, t * P:(t + 1) * P],
                                           wo2[:, w, k, n * 512:(n + 1) * 512], start=(k == 0), stop=(k == KO - 1))
                    mm.then_inc(pe_done, PE.step("y", (n, t)))
                    for w, name in enumerate((f"ga{n}", f"gb{n}")):
                        m = LOAD[name]
                        pe.wait_ge(g.s_slot[slot(m)], loaded(m))
                        for k in range(KD):
                            mm = pe.matmul(ps[:, b + 2 + w, :], g.hT[:, k, t * P:(t + 1) * P], g.ring[:, slot(m), k, :],
                                           start=(k == 0), stop=(k == KD - 1))
                    mm.then_inc(pe_done, PE.step("g", (n, t)))
                for t in range(TILES):
                    pe.wait_ge(pool_done, G[("sum", (1, t))])
                    pe.wait_ge(dve_done, V[("b", (1, TILES - 1))])
                    for k in range(KD):
                        mm = pe.transpose(ps[:, 2 * t + k // 4, (k % 4) * P:(k % 4 + 1) * P], merged[:, t, k::KD],
                                          c["ident"])
                    mm.then_inc(pe_done, PE.step("mT", t))
                pe.wait_ge(s_wo, 16)
                for t in range(TILES):
                    b = (6, 0, 2)[t]
                    pe.wait_ge(act_done, A[("mT", t)])
                    for n in range(2):
                        for k in range(KD):
                            mm = pe.matmul(ps[:, b + n, :], mT[:, k, t * P:(t + 1) * P], wo[:, k, n * 512:(n + 1) * 512],
                                           start=(k == 0), stop=(k == KD - 1))
                    mm.then_inc(pe_done, PE.step("o", t))

            @block.vector
            def _(dve):
                for i, u in enumerate(units):
                    b = 4 * (i % 2)
                    dve.wait_ge(act_done, A[("sig", u)])
                    dve.tensor_tensor(sg[:, i % 2, 0, :], sg[:, i % 2, 0, :], ps[:, b, :], ALU.mult) \
                        .then_inc(dve_done, V.step("a", u))
                    dve.tensor_tensor(sg[:, i % 2, 1, :], sg[:, i % 2, 1, :], ps[:, b + 1, :], ALU.mult) \
                        .then_inc(dve_done, V.step("b", u))
                dve.wait_ge(act_done, A[("ss", TILES - 1)])
                dve.tensor_scalar(stat[:, 1], stat[:, 0], 1.0 / D, EPS, ALU.mult, ALU.add).then_inc(dve_done, V.step("ms"))
                dve.wait_ge(dve_done, V["ms"])
                dve.reciprocal(stat[:, 2], stat[:, 1]).then_inc(dve_done, V.step("rec"))
                dve.wait_ge(act_done, A["rs"])
                dve.wait_ge(pool_done, G["gate"])
                dve.wait_ge(s_x, 32)
                for t in range(TILES):
                    b = (6, 0, 2)[t]
                    mt = merged[:, t, :].rearrange("p (b n) -> p b n", b=2)
                    dve.scalar_tensor_tensor(out=mt, in0=ps[:, b:b + 2, :], scalar=stat[:, 3, t:t + 1],
                                             in1=gate[:, min(t, 1)].rearrange("p (b n) -> p b n", b=2),
                                             op0=ALU.mult, op1=ALU.mult).then_inc(dve_done, V.step("yn", t))
                    dve.wait_ge(dve_done, V[("yn", t)])
                    dve.tensor_tensor(g.x1[:, t, :], g.x1[:, t, :], merged[:, t, :], ALU.add) \
                        .then_inc(dve_done, V.step("x1", t))


def phase_route(nc, g):
    a, ps, c = g.a, g.ps, g.c
    E = EXPERTS
    with ExitStack() as ctx:
        def sb(name, shape, dt=F32):
            return ctx.enter_context(nc.sbuf_tensor(name, shape, dt))
        rows = sb("rows", [P, 2, 2, D])
        gpre = sb("gpre2", [P, D])
        wr = sb("wr", [P, KD, E])
        ebias = sb("ebias", [P, E])
        stat = sb("rstat", [P, 4, TILES])
        s = sb("score", [P, TILES, E])
        sel = sb("sel", [P, TILES, E])
        m8 = sb("m8", [P, TILES, GROUPS, 8])
        grp = sb("grp", [P, TILES, GROUPS])
        cmp = sb("cmp", [P, 2, TILES, GROUPS * GROUPS])
        rank = sb("rank", [P, 3, TILES, GROUPS])
        top = sb("top", [P, TILES, 8])
        rep = sb("rep", [P, TILES, E])
        gates = sb("gates", [P, TILES, E])
        gsum = sb("gsum", [P, 2, TILES])
        pmax = sb("pmax", [P, 1])
        nf = sb("nf", [1, 4])
        wsg = sb("wsg", [P, 2, KD, FE])
        wsd = sb("wsd", [P, KF, D])
        sact = sb("sact", [P, 2, FE])
        sactT = sb("sactT", [P, 2, KF, P])
        s_row, s_wr, s_ws = g.sem("ffn_rows_loaded"), g.sem("router_loaded"), g.sem("shared_loaded")
        pe_done, dve_done, act_done, pool_done = (g.sem("route_" + n) for n in ("pe", "dve", "act", "pool"))
        T = range(TILES)
        PE = Count([("hT", t) for t in T] + [("logit", t) for t in T] + [("gu", 0), ("gu", 1), ("pos", 0), ("pos", 1),
                   ("pos", 2), "pmaxT", ("actT", 0), ("y", 0), ("gu", 2), ("actT", 1), ("y", 1), ("actT", 2), ("y", 2)])
        A = Count([("ss", t) for t in T] + ["rs"] + [("hT", t) for t in T] + ["sig"] + [("h2_hi", t) for t in T]
                  + [x for t in T for x in (("silu", t), ("actT", t), ("y", t))])
        V = Count(["ms", "rec", "A"] + [x for t in T for x in (("h0", t), ("h", t))]
                  + ["sel", "m8", "grp", "gt", "eq", "eqe", "cmp", "rank", "gm", "pen", "selm0", "selm", "top",
                     "rep", "mask", "gs", "gsum", "grec", "gates", "gate_hi", "gate_lo", ("h2_lo", 0), ("h2_lo", 1), ("h2_lo", 2), ("act", 0), "pos", "pmax", "nmax", "n1", "n2", "n3",
                     ("act", 1), ("act", 2)])
        with nc.Block() as block:
            @block.sync
            def _(sp):
                for v in range(2):
                    for m in range(2):
                        sp.dma_start(rows[:, v, m], g.mods_dram[v, 3 + m].partition_broadcast(P)).then_inc(s_row, 16)
                sp.dma_start(gpre[:], a["g_pre_ffn"][0].partition_broadcast(P)).then_inc(s_row, 16)
                sp.dma_start(wr[:], a["w_router"][0].rearrange("(p k) n -> p k n", k=KD)).then_inc(s_wr, 16)
                sp.dma_start(ebias[:], a["e_bias"][0].partition_broadcast(P)).then_inc(s_wr, 16)
                sp.dma_start(wsg[:, 0], a["ws_gate"][0].rearrange("(p k) n -> p k n", k=KD)).then_inc(s_ws, 16)
                sp.dma_start(wsg[:, 1], a["ws_up"][0].rearrange("(p k) n -> p k n", k=KD)).then_inc(s_ws, 16)
                sp.dma_start(wsd[:], a["ws_down"][0].rearrange("(p k) n -> p k n", k=KF)).then_inc(s_ws, 16)

            @block.scalar
            def _(act):
                for t in T:
                    act.activation(g.h2[:, t, :], g.x1[:, t, :], ACT.Square, accum_out=stat[:, 0, t:t + 1]) \
                        .then_inc(act_done, A.step("ss", t))
                act.wait_ge(dve_done, V["rec"])
                act.activation(stat[:, 3], stat[:, 2], ACT.Sqrt).then_inc(act_done, A.step("rs"))
                for t in T:
                    act.wait_ge(pe_done, PE[("hT", t)])
                    act.activation(g.hT[:, :, t * P:(t + 1) * P],
                                   ps[:, 2 * t:2 * t + 2, :].rearrange("p b (k n) -> p (b k) n", k=4), ACT.Copy) \
                        .then_inc(act_done, A.step("hT", t))
                act.wait_ge(pe_done, PE[("logit", 2)])
                act.activation(s[:].rearrange("p t e -> p (t e)"), ps[:, 6, 0:TILES * E], ACT.Sigmoid) \
                    .then_inc(act_done, A.step("sig"))
                for t in T:
                    act.activation(g.h2s[:, 0, t, :], g.h2[:, t, :], ACT.Copy).then_inc(act_done, A.step("h2_hi", t))
                for t in T:
                    act.wait_ge(pe_done, PE[("gu", t)])
                    if t == 2:
                        act.wait_ge(dve_done, V[("act", 0)])
                        act.wait_ge(pe_done, PE[("actT", 0)])
                    act.activation(sact[:, t % 2], ps[:, t % 2, 0:FE], ACT.Silu).then_inc(act_done, A.step("silu", t))
                    act.wait_ge(pe_done, PE[("actT", t)])
                    act.activation(sactT[:, t % 2].rearrange("p j n -> p (j n)"), ps[:, 3, 0:KF * P], ACT.Copy) \
                        .then_inc(act_done, A.step("actT", t))
                    act.wait_ge(pe_done, PE[("y", t)])
                    act.activation(g.y[:, t, :].rearrange("p (b n) -> p b n", b=2), ps[:, 4:6, :], ACT.Copy) \
                        .then_inc(act_done, A.step("y", t))

            @block.tensor
            def _(pe):
                for t in T:
                    pe.wait_ge(dve_done, V[("h", t)])
                    for k in range(KD):
                        mm = pe.transpose(ps[:, 2 * t + k // 4, (k % 4) * P:(k % 4 + 1) * P], g.h2[:, t, k::KD],
                                          c["ident"])
                    mm.then_inc(pe_done, PE.step("hT", t))
                pe.wait_ge(s_wr, 32)
                for t in T:
                    pe.wait_ge(act_done, A[("hT", t)])
                    for k in range(KD):
                        mm = pe.matmul(ps[:, 6, t * E:(t + 1) * E], g.hT[:, k, t * P:(t + 1) * P], wr[:, k, :],
                                       start=(k == 0), stop=(k == KD - 1))
                    mm.then_inc(pe_done, PE.step("logit", t))
                pe.wait_ge(s_ws, 48)

                def gate_up(t):
                    for k in range(KD):
                        mm = pe.matmul(ps[:, t % 2, :], g.hT[:, k, t * P:(t + 1) * P], wsg[:, :, k, :],
                                       start=(k == 0), stop=(k == KD - 1))
                    mm.then_inc(pe_done, PE.step("gu", t))

                def down(t):
                    pe.wait_ge(dve_done, V[("act", t)])
                    if t:
                        pe.wait_ge(act_done, A[("actT", t - 1)])
                    for j in range(KF):
                        mm = pe.transpose(ps[:, 3, j * P:(j + 1) * P], sact[:, t % 2, j::KF], c["ident"])
                    mm.then_inc(pe_done, PE.step("actT", t))
                    pe.wait_ge(act_done, A[("actT", t)])
                    if t:
                        pe.wait_ge(act_done, A[("y", t - 1)])
                    for n in range(2):
                        for j in range(KF):
                            mm = pe.matmul(ps[:, 4 + n, :], sactT[:, t % 2, j, :], wsd[:, j, n * 512:(n + 1) * 512],
                                           start=(j == 0), stop=(j == KF - 1))
                    mm.then_inc(pe_done, PE.step("y", t))

                gate_up(0)
                gate_up(1)
                pe.wait_ge(dve_done, V["mask"])
                for t in T:
                    for q in range(t + 1):
                        mm = pe.matmul(ps[:, 7, t * E:(t + 1) * E], c["before" if q == t else "ones"], rep[:, q, :],
                                       start=(q == 0), stop=(q == t))
                    mm.then_inc(pe_done, PE.step("pos", t))
                pe.wait_ge(dve_done, V["pmax"])
                pe.transpose(ps[0:1, 2, 0:P], pmax[:], c["ident"]).then_inc(pe_done, PE.step("pmaxT"))
                down(0)
                gate_up(2)
                down(1)
                down(2)

            @block.vector
            def _(dve):
                dve.wait_ge(act_done, A[("ss", 2)])
                dve.tensor_scalar(stat[:, 1], stat[:, 0], 1.0 / D, EPS, ALU.mult, ALU.add).then_inc(dve_done, V.step("ms"))
                dve.wait_ge(dve_done, V["ms"])
                dve.reciprocal(stat[:, 2], stat[:, 1]).then_inc(dve_done, V.step("rec"))
                dve.wait_ge(s_row, 80)
                dve.scalar_tensor_tensor(out=rows[:, :, 1, :], in0=rows[:, :, 1, :], scalar=1.0, in1=over(gpre[:], 2, 1),
                                         op0=ALU.add, op1=ALU.mult).then_inc(dve_done, V.step("A"))
                dve.wait_ge(act_done, A["rs"])
                dve.wait_ge(dve_done, V["A"])
                for t in T:
                    v = min(t, 1)
                    dve.scalar_tensor_tensor(out=g.h2[:, t, :], in0=g.x1[:, t, :], scalar=stat[:, 3, t:t + 1],
                                             in1=rows[:, v, 1, :], op0=ALU.mult, op1=ALU.mult) \
                        .then_inc(dve_done, V.step("h0", t))
                    dve.wait_ge(dve_done, V[("h0", t)])
                    dve.tensor_tensor(g.h2[:, t, :], g.h2[:, t, :], rows[:, v, 0, :], ALU.add) \
                        .then_inc(dve_done, V.step("h", t))
                dve.wait_ge(act_done, A["sig"])
                dve.tensor_tensor(sel[:], s[:], over(ebias[:], TILES, 1), ALU.add).then_inc(dve_done, V.step("sel"))
                dve.wait_ge(dve_done, V["sel"])
                for t in T:
                    for q in range(GROUPS):
                        i = dve.max(m8[:, t, q, :], sel[:, t, q * PER:(q + 1) * PER])
                i.then_inc(dve_done, V.step("m8"))
                dve.wait_ge(dve_done, V["m8"])
                dve.tensor_tensor(grp[:], m8[:, :, :, 0], m8[:, :, :, 1], ALU.add).then_inc(dve_done, V.step("grp"))
                dve.wait_ge(dve_done, V["grp"])
                sq = lambda x: x.rearrange("p t (i j) -> p t i j", i=GROUPS)
                dve.tensor_tensor(sq(cmp[:, 0]), over(grp[:], GROUPS, 2), over(grp[:], GROUPS, 3), ALU.is_gt) \
                    .then_inc(dve_done, V.step("gt"))
                dve.tensor_tensor(sq(cmp[:, 1]), over(grp[:], GROUPS, 2), over(grp[:], GROUPS, 3), ALU.is_equal) \
                    .then_inc(dve_done, V.step("eq"))
                dve.wait_ge(dve_done, V["eq"])
                dve.tensor_tensor(cmp[:, 1], cmp[:, 1], over(c["earlier"], TILES, 1), ALU.mult) \
                    .then_inc(dve_done, V.step("eqe"))
                dve.wait_ge(dve_done, V["eqe"])
                dve.tensor_tensor(cmp[:, 0], cmp[:, 0], cmp[:, 1], ALU.add).then_inc(dve_done, V.step("cmp"))
                dve.wait_ge(dve_done, V["cmp"])
                dve.tensor_reduce(rank[:, 0], sq(cmp[:, 0]), AX, ALU.add).then_inc(dve_done, V.step("rank"))
                dve.wait_ge(dve_done, V["rank"])
                dve.tensor_scalar(rank[:, 1], rank[:, 0], TOPG - 0.5, None, ALU.is_lt).then_inc(dve_done, V.step("gm"))
                dve.wait_ge(dve_done, V["gm"])
                dve.tensor_scalar(rank[:, 2], rank[:, 1], 1e30, -1e30, ALU.mult, ALU.add).then_inc(dve_done, V.step("pen"))
                per = lambda x: x.rearrange("p t (q e) -> p t q e", q=GROUPS)
                dve.tensor_tensor(per(sel[:]), per(sel[:]), over(rank[:, 1], PER, 3), ALU.mult) \
                    .then_inc(dve_done, V.step("selm0"))
                dve.wait_ge(dve_done, V["selm0"])
                dve.tensor_tensor(per(sel[:]), per(sel[:]), over(rank[:, 2], PER, 3), ALU.add) \
                    .then_inc(dve_done, V.step("selm"))
                dve.wait_ge(dve_done, V["selm"])
                for t in T:
                    i = dve.max(top[:, t, :], sel[:, t, :])
                i.then_inc(dve_done, V.step("top"))
                dve.wait_ge(dve_done, V["top"])
                for t in T:
                    i = dve.match_replace(rep[:, t, :], top[:, t, :], sel[:, t, :], -3e38)
                i.then_inc(dve_done, V.step("rep"))
                dve.wait_ge(dve_done, V["rep"])
                dve.tensor_tensor(rep[:], rep[:], sel[:], ALU.not_equal).then_inc(dve_done, V.step("mask"))
                dve.wait_ge(dve_done, V["mask"])
                dve.tensor_tensor(s[:], s[:], rep[:], ALU.mult).then_inc(dve_done, V.step("gs"))
                dve.wait_ge(dve_done, V["gs"])
                dve.tensor_reduce(gsum[:, 0], s[:], AX, ALU.add).then_inc(dve_done, V.step("gsum"))
                dve.wait_ge(dve_done, V["gsum"])
                dve.reciprocal(gsum[:, 1], gsum[:, 0]).then_inc(dve_done, V.step("grec"))
                dve.wait_ge(dve_done, V["grec"])
                for t in T:
                    i = dve.tensor_scalar(gates[:, t, :], s[:, t, :], gsum[:, 1, t:t + 1], ROUTED, ALU.mult, ALU.mult)
                i.then_inc(dve_done, V.step("gates"))

                dve.wait_ge(dve_done, V["gates"])
                dve.tensor_copy(g.gate2[:, :, :, 0], gates[:]).then_inc(dve_done, V.step("gate_hi"))
                dve.wait_ge(dve_done, V["gate_hi"])
                dve.tensor_tensor(g.gate2[:, :, :, 1], gates[:], g.gate2[:, :, :, 0].bitcast(F32), ALU.subtract) \
                    .then_inc(dve_done, V.step("gate_lo"))
                for t in T:
                    dve.wait_ge(act_done, A[("h2_hi", t)])
                    dve.tensor_tensor(g.h2s[:, 1, t, :], g.h2[:, t, :], g.h2s[:, 0, t, :].bitcast(F32), ALU.subtract) \
                        .then_inc(dve_done, V.step("h2_lo", t))

                def shared_act(t):
                    dve.wait_ge(act_done, A[("silu", t)])
                    dve.tensor_tensor(sact[:, t % 2], sact[:, t % 2], ps[:, t % 2, FE:2 * FE], ALU.mult) \
                        .then_inc(dve_done, V.step("act", t))

                shared_act(0)
                dve.wait_ge(pe_done, PE[("pos", 2)])
                flat = lambda x: x[:].rearrange("p t e -> p (t e)")
                dve.scalar_tensor_tensor(out=flat(g.pos), in0=ps[:, 7, 0:TILES * E], scalar=1.0, in1=flat(rep),
                                         op0=ALU.add, op1=ALU.mult).then_inc(dve_done, V.step("pos"))
                dve.wait_ge(dve_done, V["pos"])
                dve.tensor_reduce(pmax[:], flat(g.pos), AX, ALU.max).then_inc(dve_done, V.step("pmax"))
                dve.wait_ge(pe_done, PE["pmaxT"])
                dve.tensor_reduce(nf[:, 0:1], ps[0:1, 2, 0:P], AX, ALU.max).then_inc(dve_done, V.step("nmax"))
                dve.wait_ge(dve_done, V["nmax"])
                dve.tensor_scalar(nf[:, 1:2], nf[:, 0:1], P + 0.5, None, ALU.is_gt).then_inc(dve_done, V.step("n1"))
                dve.tensor_scalar(nf[:, 2:3], nf[:, 0:1], 2 * P + 0.5, 1.0, ALU.is_gt, ALU.add) \
                    .then_inc(dve_done, V.step("n2"))
                dve.wait_ge(dve_done, V["n2"])
                dve.tensor_tensor(g.passes[:], nf[:, 1:2], nf[:, 2:3], ALU.add).then_inc(dve_done, V.step("n3"))
                shared_act(1)
                shared_act(2)


class Event:

    def __init__(self, sem, ahead=0):
        self.sem, self.ahead = sem, ahead

    def value(self, i):
        return i + 1 + self.ahead


def phase_experts(nc, g):
    a, ps, c = g.a, g.ps, g.c
    T = range(TILES)
    PAIRS = EXPERTS // 2
    B = range(2)
    KP = 2
    GP = KD // KP
    NP = GP + KF
    PW = KP * 2 * FE
    assert PW == D
    F32R = mybir.dt.float32r
    with ExitStack() as ctx:
        def sb(name, shape, dt=F32R):
            return ctx.enter_context(nc.sbuf_tensor(name, shape, dt))
        flat = lambda i: g.ring[:, i].rearrange("p k n -> p (k n)")
        wgu = [flat(b).rearrange("p (m k n) -> p m k n", m=2, k=KD) for b in B]
        wd = [flat(2)[:, b * KF * D:(b + 1) * KF * D].rearrange("p (j n) -> p j n", j=KF) for b in B]
        hi = sb("w_hi", [P, NP, PW])
        lo = sb("w_lo", [P, NP, PW])
        hot = sb("hot", [P, TILES, 2, P])
        hotT = sb("hotT", [P, 2, TOK])
        gcol = sb("gcol", [P, 2, TILES, 2])
        gslot = sb("gslot", [P, 2], F32)
        hgT = sb("hgT", [P, 2, KD, 2, P])
        sil = sb("sil", [P, 2, FE], F32)
        actT = sb("actT", [P, 2, 2, KF, P])
        ye = sb("ye", [P, 2, 2, D])
        s_gu = [g.sem(f"gate_up_loaded{b}") for b in B]
        s_dn = [g.sem(f"down_loaded{b}") for b in B]

        def event(name, ahead):
            return Event(g.sem(name), ahead)

        hot_made, gate_ps, gslot_sb = (event(n, 1) for n in ("hot_made", "slot_gates", "gslot_copied"))
        hg_ps, hgT_hi, hgT_lo = (event(n, 2) for n in ("gathered", "hgT_hi", "hgT_lo"))
        actT_ps, hotT_ps, silu, actT_hi, hotT_sb, ye_hi, act_done, actT_lo, ye_lo = (
            event(n, 2) for n in ("act_turned", "hot_turned", "silu_done", "actT_hi", "hotT_copied", "ye_hi",
                                  "act_done", "actT_lo", "ye_lo"))
        used, hi_made = event("pieces_used", NP), event("hi_made", NP)
        lo_gu, lo_dn = event("lo_gate_up_made", 2 * GP), event("lo_down_made", 2 * KF)
        units = [(t, n) for t in T for n in range(2)]
        U = len(units)
        y_ps, y_added = event("y_summed", U), event("y_added", 2 * U)
        YB = (6, 7, 5)
        GU, AT, HT, DN = 2, 3, 4, 6
        HG = (slice(0, 2), slice(4, 6))
        HK = KD // 2

        def wait(eng, ev, i):
            eng.wait_ge(ev.sem, ev.value(i))

        def turns(eng, own, prologue, body, epilogue):
            for ev in own:
                eng.sem_inc(ev.sem, ev.ahead)
            passes = eng.value_load(g.passes[0:1, 0:1], min_val=1, max_val=TILES)
            with eng.Fori(0, passes) as turn:
                first = turn * PAIRS
                prologue(first, 0)
                body(first, 0, True, False)
                with eng.Fori(1, PAIRS - 1) as pair:
                    body(first + pair, pair * 2, False, False)
                body(first + (PAIRS - 1), EXPERTS - 2, False, True)
                if epilogue:
                    epilogue(first + (PAIRS - 1), turn)

        with nc.Block() as block:
            @block.sync
            def _(sp):
                def load(q, e, b):
                    n = 2 * q + b
                    for half, (ev, per) in enumerate(((lo_gu, GP), (lo_dn, KF))):
                        wait(sp, ev, (n - 2) * per + per - 1)
                        if half == 0:
                            for m, w in enumerate((a["w_gate"], a["w_up"])):
                                sp.dma_start(wgu[b][:, m], w[0, bass.ds(e, 1)].rearrange(
                                    "e (p k) n -> p (e k) n", k=KD)).then_inc(s_gu[b], 16)
                        else:
                            sp.dma_start(wd[b], a["w_down"][0, bass.ds(e, 1)].rearrange(
                                "e (p j) n -> p (e j) n", j=KF)).then_inc(s_dn[b], 16)

                def body(q, e, first, last):
                    load(q, e + 1, 1)
                    if not last:
                        load(q + 1, e + 2, 0)
                turns(sp, (), lambda q, e: load(q, e, 0), body, None)

            @block.scalar
            def _(act):
                def split(q, b, i):
                    n = 2 * q + b
                    if i == 0:
                        act.wait_ge(s_gu[b], q * 32 + 32)
                    if i == GP:
                        act.wait_ge(s_dn[b], q * 16 + 16)
                    wait(act, used, (n - 1) * NP + i)
                    if i < GP:
                        act.activation(hi[:, i].rearrange("p (m k n) -> p m k n", m=2, k=KP),
                                       wgu[b][:, :, i * KP:(i + 1) * KP, :], ACT.Copy).then_inc(hi_made.sem, 1)
                    else:
                        act.activation(hi[:, i], wd[b][:, i - GP, :], ACT.Copy).then_inc(hi_made.sem, 1)

                def take_hg(q, h):
                    wait(act, hg_ps, 2 * q + h)
                    wait(act, used, (2 * q - 1) * NP + GP - 1)
                    act.activation(hgT[:, 0, h * HK:(h + 1) * HK].rearrange("p (b k) e n -> p b (k e n)", b=2),
                                   ps[:, HG[h], :], ACT.Copy).then_inc(hgT_hi.sem, 1)

                def take_silu(q, b):
                    n = 2 * q + b
                    wait(act, used, n * NP + GP - 1)
                    wait(act, actT_ps, n - 2)
                    act.activation(sil[:, b], ps[:, GU, 0:FE], ACT.Silu).then_inc(silu.sem, 1)

                def take_actT(q, b):
                    n = 2 * q + b
                    wait(act, actT_ps, n)
                    wait(act, used, (n - 2) * NP + NP - 1)
                    act.activation(actT[:, b, 0].rearrange("p j n -> p (j n)"), ps[:, AT, 0:KF * P], ACT.Copy) \
                        .then_inc(actT_hi.sem, 1)

                def take_hotT(q, b):
                    n = 2 * q + b
                    wait(act, hotT_ps, n)
                    act.activation(hotT[:, b, :], ps[:, (HT, GU)[b], 0:TOK], ACT.Copy).then_inc(hotT_sb.sem, 1)

                def take_ye(q, b):
                    n = 2 * q + b
                    wait(act, used, n * NP + NP - 1)
                    act.activation(ye[:, b, 0].rearrange("p (b n) -> p b n", b=2), ps[:, DN:DN + 2, :], ACT.Copy) \
                        .then_inc(ye_hi.sem, 1)

                def prologue(q, e):
                    take_hg(q, 0)
                    take_hg(q, 1)
                    for i in range(NP):
                        split(q, 0, i)

                def body(q, e, first, last):
                    split(q, 1, 0)
                    split(q, 1, 1)
                    take_silu(q, 0)
                    split(q, 1, 2)
                    take_actT(q, 0)
                    split(q, 1, 3)
                    take_hotT(q, 0)
                    take_hotT(q, 1)
                    split(q, 1, 4)
                    take_ye(q, 0)
                    split(q, 1, 5)
                    if not last:
                        split(q + 1, 0, 0)
                        split(q + 1, 0, 1)
                    take_silu(q, 1)
                    if not last:
                        split(q + 1, 0, 2)
                        take_hg(q + 1, 0)
                    take_actT(q, 1)
                    if not last:
                        split(q + 1, 0, 3)
                        take_hg(q + 1, 1)
                        split(q + 1, 0, 4)
                    take_ye(q, 1)
                    if not last:
                        split(q + 1, 0, 5)
                turns(act, (hgT_hi, silu, actT_hi, hotT_sb, ye_hi, hi_made), prologue, body, None)

            @block.gpsimd
            def _(pool):
                def split(q, b):
                    n = 2 * q + b
                    for j in range(KF):
                        wait(pool, hi_made, n * NP + GP + j)
                        pool.tensor_tensor(lo[:, GP + j], wd[b][:, j, :], hi[:, GP + j].bitcast(F32), ALU.subtract) \
                            .then_inc(lo_dn.sem, 1)

                def body(q, e, first, last):
                    split(q, 1)
                    if not last:
                        split(q + 1, 0)
                turns(pool, (lo_dn,), lambda q, e: split(q, 0), body, None)

            @block.tensor
            def _(pe):
                def gather(q, h):
                    if h == 0:
                        wait(pe, hot_made, q)
                        wait(pe, hgT_hi, 2 * q - 2)
                        wait(pe, hgT_lo, 2 * q - 2)
                    else:
                        wait(pe, hotT_sb, 2 * q - 2)
                        wait(pe, y_added, (q - 2) * U + 5)
                    for k in range(HK):
                        for i, (part, t) in enumerate([(x, t) for x in range(2) for t in T]):
                            mm = pe.matmul(ps[:, HG[h].start + k // 2, (k % 2) * 2 * P:(k % 2 + 1) * 2 * P],
                                           g.h2s[:, part, t, h * HK + k::KD], hot[:, t],
                                           start=(i == 0), stop=(i == 2 * TILES - 1))
                    mm.then_inc(hg_ps.sem, 1)
                    if h == 0:
                        wait(pe, actT_hi, 2 * q - 2)
                        wait(pe, actT_lo, 2 * q - 2)
                        for b in B:
                            for t in T:
                                mm = pe.matmul(ps[:, AT, KF * P + 2 * b:KF * P + 2 * b + 2], hot[:, t, b, :],
                                               gcol[:, b, t, :], start=(t == 0), stop=(t == TILES - 1))
                        mm.then_inc(gate_ps.sem, 1)

                def gate_up(q, b):
                    n = 2 * q + b
                    wait(pe, act_done, n - 1)
                    if b:
                        wait(pe, hotT_sb, n)
                    for i in range(GP):
                        if b == 0 and i in (0, GP // 2):
                            wait(pe, hgT_hi, n + i // (GP // 2))
                            wait(pe, hgT_lo, n + i // (GP // 2))
                        wait(pe, hi_made, n * NP + i)
                        wait(pe, lo_gu, n * GP + i)
                        w = [x[:, i].rearrange("p (m k n) -> p m k n", m=2, k=KP) for x in (hi, lo)]
                        for k in range(KP):
                            kk = i * KP + k
                            for x, y in ((0, 0), (0, 1), (1, 0)):
                                mm = pe.matmul(ps[:, GU, :], hgT[:, x, kk, b, :], w[y][:, :, k, :],
                                               start=(kk == 0 and (x, y) == (0, 0)),
                                               stop=(kk == KD - 1 and (x, y) == (1, 0)))
                        mm.then_inc(used.sem, 1)

                def turn_act(q, b, last):
                    wait(pe, act_done, 2 * q + b)
                    wait(pe, gslot_sb, q + (b and not last))
                    for j in range(KF):
                        mm = pe.transpose(ps[:, AT, j * P:(j + 1) * P], sil[:, b, j::KF], c["ident"])
                    mm.then_inc(actT_ps.sem, 1)

                def down(q, b):
                    n = 2 * q + b
                    wait(pe, actT_hi, n)
                    wait(pe, actT_lo, n)
                    if b:
                        wait(pe, ye_hi, n - 1)
                        wait(pe, ye_lo, n - 1)
                    for j in range(KF):
                        wait(pe, hi_made, n * NP + GP + j)
                        wait(pe, lo_dn, n * KF + j)
                        for m in range(2):
                            if not b and j == 0:
                                wait(pe, y_added, q * U - 3 + m)
                            for x, y in ((0, 0), (0, 1), (1, 0)):
                                mm = pe.matmul(ps[:, DN + m, :], actT[:, b, x, j, :],
                                               (hi, lo)[y][:, GP + j, m * 512:(m + 1) * 512],
                                               start=(j == 0 and (x, y) == (0, 0)),
                                               stop=(j == KF - 1 and (x, y) == (1, 0)))
                        mm.then_inc(used.sem, 1)

                def scatter(q, turn=None, part=range(U)):
                    if part[0] == 0:
                        for ev in (ye_hi, ye_lo, hotT_sb):
                            wait(pe, ev, 2 * q + 1)
                    for i in part:
                        t, m = units[i]
                        wait(pe, y_added, q * U + (i - 3))
                        for j, (b, x) in enumerate([(b, x) for b in B for x in range(2)]):
                            mm = pe.matmul(ps[:, YB[i % 3], :], hotT[:, b, t * P:(t + 1) * P],
                                           ye[:, b, x, m * 512:(m + 1) * 512], start=(j == 0), stop=(j == 3))
                        mm.then_inc(y_ps.sem, 1)

                def turn_hot(q, b):
                    n = 2 * q + b
                    if b == 0:
                        wait(pe, hotT_sb, n - 2)
                    for t in T:
                        mm = pe.transpose(ps[:, (HT, GU)[b], t * P:(t + 1) * P], hot[:, t, b, :].bitcast(F32), c["ident"])
                    mm.then_inc(hotT_ps.sem, 1)

                def prologue(q, e):
                    gather(q, 0)
                    gather(q, 1)

                def body(q, e, first, last):
                    gate_up(q, 0)
                    if not first:
                        scatter(q - 1, part=range(0, 2))
                    turn_act(q, 0, last)
                    if not first:
                        scatter(q - 1, part=range(2, U))
                    turn_hot(q, 0)
                    turn_hot(q, 1)
                    down(q, 0)
                    gate_up(q, 1)
                    if not last:
                        gather(q + 1, 0)
                    turn_act(q, 1, last)
                    if not last:
                        gather(q + 1, 1)
                    down(q, 1)
                turns(pe, (hg_ps, gate_ps, actT_ps, hotT_ps, used, y_ps), prologue, body, scatter)

            @block.vector
            def _(dve):
                def make_hot(q, e):
                    wait(dve, hotT_ps, 2 * q - 1)
                    for b in B:
                        for t in T:
                            dve.tensor_scalar(hot[:, t, b, :], c["iota"], g.pos[:, t, bass.ds(e + b, 1)], None,
                                              ALU.is_equal)
                        i = dve.tensor_copy(gcol[:, b],
                                            g.gate2[:, :, bass.ds(e + b, 1), :].rearrange("p t e x -> p (t e) x"))
                    i.then_inc(hot_made.sem, 1)

                def take_gate(q):
                    wait(dve, gate_ps, q)
                    wait(dve, act_done, 2 * q - 1)
                    dve.tensor_reduce(gslot[:], ps[:, AT, KF * P:KF * P + 4].rearrange("p (b x) -> p b x", b=2),
                                      AX, ALU.add).then_inc(gslot_sb.sem, 1)

                def take_hg(q, h):
                    wait(dve, hgT_hi, 2 * q + h)
                    two = lambda x: x[:, h * HK:(h + 1) * HK].rearrange("p (b k) e n -> p b (k e n)", b=2)
                    dve.tensor_tensor(two(hgT[:, 1]), ps[:, HG[h], :], two(hgT[:, 0].bitcast(F32)),
                                      ALU.subtract).then_inc(hgT_lo.sem, 1)

                def split(q, b, i):
                    n = 2 * q + b
                    wait(dve, hi_made, n * NP + i)
                    dve.tensor_tensor(lo[:, i].rearrange("p (m k n) -> p m k n", m=2, k=KP),
                                      wgu[b][:, :, i * KP:(i + 1) * KP, :],
                                      hi[:, i].bitcast(F32).rearrange("p (m k n) -> p m k n", m=2, k=KP),
                                      ALU.subtract).then_inc(lo_gu.sem, 1)

                def take_act(q, b):
                    n = 2 * q + b
                    wait(dve, silu, n)
                    wait(dve, gslot_sb, q)
                    dve.scalar_tensor_tensor(out=sil[:, b], in0=ps[:, GU, FE:2 * FE], scalar=gslot[:, b:b + 1],
                                             in1=sil[:, b], op0=ALU.mult, op1=ALU.mult).then_inc(act_done.sem, 1)

                def take_actT(q, b):
                    n = 2 * q + b
                    wait(dve, actT_hi, n)
                    dve.tensor_tensor(actT[:, b, 1].rearrange("p j n -> p (j n)"), ps[:, AT, 0:KF * P],
                                      actT[:, b, 0].bitcast(F32).rearrange("p j n -> p (j n)"), ALU.subtract) \
                        .then_inc(actT_lo.sem, 1)

                def take_ye(q, b):
                    n = 2 * q + b
                    wait(dve, ye_hi, n)
                    dve.tensor_tensor(ye[:, b, 1].rearrange("p (b n) -> p b n", b=2), ps[:, DN:DN + 2, :],
                                      ye[:, b, 0].bitcast(F32).rearrange("p (b n) -> p b n", b=2), ALU.subtract) \
                        .then_inc(ye_lo.sem, 1)

                def add_y(q, part=range(U)):
                    for i in part:
                        t, m = units[i]
                        yt = g.y[:, t, m * 512:(m + 1) * 512]
                        wait(dve, y_ps, q * U + i)
                        wait(dve, y_added, q * U + (i - U))
                        dve.tensor_tensor(yt, yt, ps[:, YB[i % 3], :], ALU.add).then_inc(y_added.sem, 1)

                def prologue(q, e):
                    make_hot(q, e)
                    take_gate(q)
                    take_hg(q, 0)
                    take_hg(q, 1)
                    for i in range(GP):
                        split(q, 0, i)

                def body(q, e, first, last):
                    split(q, 1, 0)
                    split(q, 1, 1)
                    take_act(q, 0)
                    split(q, 1, 2)
                    if not first:
                        add_y(q - 1, range(0, 2))
                    take_actT(q, 0)
                    if not first:
                        add_y(q - 1, range(2, 4))
                    split(q, 1, 3)
                    if not first:
                        add_y(q - 1, range(4, U))
                    if not last:
                        make_hot(q + 1, e + 2)
                    take_ye(q, 0)
                    if not last:
                        split(q + 1, 0, 0)
                        split(q + 1, 0, 1)
                    take_act(q, 1)
                    if not last:
                        split(q + 1, 0, 2)
                        take_gate(q + 1)
                        take_hg(q + 1, 0)
                    take_actT(q, 1)
                    if not last:
                        split(q + 1, 0, 3)
                        take_hg(q + 1, 1)
                    take_ye(q, 1)

                def epilogue(q, turn):
                    add_y(q)
                    wait(dve, hot_made, q)
                    dve.tensor_scalar(g.pos[:], g.pos[:], -float(P), None, ALU.add).then_inc(g.s_pos, 1)
                    dve.wait_ge(g.s_pos, turn + 1)
                turns(dve, (hot_made, gslot_sb, act_done, hgT_lo, actT_lo, ye_lo, lo_gu, y_added), prologue, body, epilogue)


def phase_output(nc, g):
    a = g.a
    with ExitStack() as ctx:
        def sb(name, shape):
            return ctx.enter_context(nc.sbuf_tensor(name, shape, F32))
        gate = sb("gate_out", [P, 2, D])
        gpost = sb("gpost2", [P, D])
        tmp = sb("tmp", [P, TILES, D])
        stat = sb("ostat2", [P, 4, TILES])
        s_row, s_out = g.sem("gate2_loaded"), g.sem("y_stored")
        dve_done, act_done = g.sem("out_dve"), g.sem("out_act")
        T = range(TILES)
        V = Count(["gate", "ms", "rec"] + [(x, t) for t in T for x in ("yn", "x2")])
        A = Count([("ss", t) for t in T] + ["rs"])
        with nc.Block() as block:
            @block.sync
            def _(sp):
                for v in range(2):
                    sp.dma_start(gate[:, v], g.mods_dram[v, 5].partition_broadcast(P)).then_inc(s_row, 16)
                sp.dma_start(gpost[:], a["g_post_ffn"][0].partition_broadcast(P)).then_inc(s_row, 16)
                for t in T:
                    sp.wait_ge(dve_done, V[("x2", t)])
                    dst = g.o["y_prompt"][0] if t == 0 else g.o["y_sample"][0, (t - 1) * P:t * P]
                    sp.dma_start(dst, g.x1[:, t, :]).then_inc(s_out, 16)
                sp.wait_ge(s_out, 16 * TILES)

            @block.scalar
            def _(act):
                for t in T:
                    act.activation(tmp[:, t, :], g.y[:, t, :], ACT.Square, accum_out=stat[:, 0, t:t + 1]) \
                        .then_inc(act_done, A.step("ss", t))
                act.wait_ge(dve_done, V["rec"])
                act.activation(stat[:, 3], stat[:, 2], ACT.Sqrt).then_inc(act_done, A.step("rs"))

            @block.vector
            def _(dve):
                dve.wait_ge(s_row, 48)
                dve.tensor_tensor(gate[:], gate[:], over(gpost[:], 2, 1), ALU.mult).then_inc(dve_done, V.step("gate"))
                dve.wait_ge(act_done, A[("ss", 2)])
                dve.tensor_scalar(stat[:, 1], stat[:, 0], 1.0 / D, EPS, ALU.mult, ALU.add).then_inc(dve_done, V.step("ms"))
                dve.wait_ge(dve_done, V["ms"])
                dve.reciprocal(stat[:, 2], stat[:, 1]).then_inc(dve_done, V.step("rec"))
                dve.wait_ge(act_done, A["rs"])
                dve.wait_ge(dve_done, V["gate"])
                for t in T:
                    dve.scalar_tensor_tensor(out=tmp[:, t, :], in0=g.y[:, t, :], scalar=stat[:, 3, t:t + 1],
                                             in1=gate[:, min(t, 1)], op0=ALU.mult, op1=ALU.mult) \
                        .then_inc(dve_done, V.step("yn", t))
                    dve.wait_ge(dve_done, V[("yn", t)])
                    dve.tensor_tensor(g.x1[:, t, :], g.x1[:, t, :], tmp[:, t, :], ALU.add) \
                        .then_inc(dve_done, V.step("x2", t))


def phases(nc, g, sb, sem):
    with ExitStack() as early:
        def eb(name, shape):
            return early.enter_context(nc.sbuf_tensor(name, shape, F32))
        g.hT = eb("hT", [P, KD, TOK])
        g.small = eb("small", [P, TILES, 64])
        g.z = eb("z", [P, TILES, GW])
        g.omla = eb("omla", [P, TILES, GW])
        with nc.sbuf_tensor("wconv", [P, CONV, 12], F32) as g.wconv, nc.sbuf_tensor("qkv", [P, 12, OUTW], F32) as g.qkv:
            phase_condition(nc, g)
            with nc.sbuf_tensor("cqkv", [P, TILES, 2 * LORA], F32) as g.cqkv:
                phase_project(nc, g)
                phase_attention(nc, g)
            phase_delta(nc, g)
        g.x1 = sb("x1", [P, TILES, D], side="right")
        phase_merge(nc, g)
    F32R = mybir.dt.float32r
    g.y = sb("y", [P, TILES, D])
    g.h2s = sb("h2s", [P, 2, TILES, D], F32R)
    g.gate2 = sb("gate2", [P, TILES, EXPERTS, 2], F32R)
    g.pos = sb("pos", [P, TILES, EXPERTS])
    g.passes = sb("passes", [1, 1], mybir.dt.int32)
    g.s_pos = sem("pos_shifted")
    with nc.sbuf_tensor("h2", [P, TILES, D], F32) as g.h2, nc.sbuf_tensor("h2T", [P, KD, TOK], F32) as g.hT:
        phase_route(nc, g)
    phase_experts(nc, g)
    phase_output(nc, g)


_INS = ["x_prompt", "x_sample", "cache_ckv", "cache_krope", "state_delta", "c", "c_ctx", "w_ada", "b_ada",
        "g_pre_mix", "g_post_mix", "g_pre_ffn", "g_post_ffn", "w_in", "q_norm_g", "kv_norm_g", "w_uq", "w_ukv",
        "conv_w", "a_log", "dt_bias", "gdn_norm_g", "w_oa", "w_ob", "w_o", "w_router", "e_bias", "w_gate", "w_up",
        "w_down", "ws_gate", "ws_up", "ws_down"]
_OUTS = [("y_prompt", (1, CTX, D)), ("y_sample", (1, LAT, D)), ("ckv", (1, 1, CTX, LORA)),
         ("krope", (1, 1, CTX, ROPE)), ("state", (1, 1, 2, GH, DK, DV))]


def kernel(**inputs):
    from concourse import bacc
    from concourse.bass_utils import run_bass_kernel_spmd

    nc = bacc.Bacc("TRN2", target_bir_lowering=False, num_devices=1)
    arrays = {f"in_{n}": np.ascontiguousarray(inputs[n]) for n in _INS}
    arrays["in_table"] = constant_columns()[0]
    a = {n[3:]: nc.dram_tensor(n, v.shape, F32, kind="ExternalInput").ap() for n, v in arrays.items()}
    o = {n: nc.dram_tensor(f"out_{n}", s, F32, kind="ExternalOutput").ap() for n, s in _OUTS}
    build(nc, a, o)
    r = run_bass_kernel_spmd(nc, [arrays], core_ids=[0])
    return tuple(r.results[0][f"out_{n}"] for n, _ in _OUTS)
```

```python
from contextlib import ExitStack

import numpy as np

import concourse.bass as bass
from concourse import mybir

F32 = mybir.dt.float32
ALU = mybir.AluOpType
ACT = mybir.ActivationFunctionType
AX = mybir.AxisListType.X

P = 128
D = 1024
KD = D // P
CTX, LAT, PAST = 128, 256, 128
TILES = (CTX + LAT) // P
TOK = TILES * P
MH, NOPE, ROPE, VH = 8, 64, 32, 64
QK = NOPE + ROPE
LORA = 256
KL = LORA // P
GH, DK, DV = 8, 64, 64
GW = GH * DV
CONV, CHUNK = 5, 64
EXPERTS, GROUPS, TOPG, TOPK = 64, 8, 4, 8
PER = EXPERTS // GROUPS
FE = 256
KF = FE // P
ROUTED = 2.5
EPS = 1e-6
GRID_W, THETA = 64, 10000.0
GAP = CONV // 2
PADW = TOK + 3 * GAP
OUTW = TOK + GAP
LEVELS = (1, 2, 4, 8, 16, 32)

C_CQ, C_CKV, C_KR, C_QKV, C_Z, C_AB, C_GA, C_GB = 0, 256, 512, 544, 2080, 2592, 2624, 3648


def tok_at(t):
    return t * P + (GAP if t else 0)


def constant_columns():
    i = np.arange(P)[:, None]
    j = np.arange(P)[None, :]
    same = (i // CHUNK) == (j // CHUNK)
    parts = {"ident": i == j, "incl0": same & (i <= j), "incl1": same & (i >= j),
             "strict0": same & (i < j), "strict1": same & (i > j), "block": same,
             "half0": (i < CHUNK) & (j >= 0), "half1": (i >= CHUNK) & (j >= 0),
             "before": i < j, "ones": (i >= 0) & (j >= 0), "iota": j + 1 + 0 * i}
    for s in LEVELS:
        low = ((i // s) == (j // s) + 1) & ((j // s) % 2 == 0)
        parts[f"level0_{s}"] = low
        parts[f"level1_{s}"] = low.T
    inv = THETA ** (-np.arange(ROPE // 4) / (ROPE // 4))
    n = np.arange(LAT)
    ang = np.stack([(n // GRID_W)[:, None] * inv, (n % GRID_W)[:, None] * inv], axis=1).reshape(LAT, ROPE // 2)
    parts["cos"] = np.cos(ang).reshape(LAT // P, P, ROPE // 2).transpose(1, 0, 2).reshape(P, -1)
    parts["sin"] = np.sin(ang).reshape(LAT // P, P, ROPE // 2).transpose(1, 0, 2).reshape(P, -1)
    g = np.arange(GROUPS)
    parts["earlier"] = np.broadcast_to((g[None, :] < g[:, None]).reshape(1, -1), (P, GROUPS * GROUPS))
    at, n = {}, 0
    for name, a in parts.items():
        at[name] = (n, n + a.shape[1])
        n += a.shape[1]
    return np.concatenate([np.asarray(a, np.float32) for a in parts.values()], axis=1), at


class Names:
    pass


class Count:

    def __init__(self, names):
        self.at = {n: i + 1 for i, n in enumerate(names)}
        self.done = 0
        assert len(self.at) == len(names)

    def __getitem__(self, name):
        return self.at[name]

    def step(self, *name):
        name = name if len(name) > 1 else name[0]
        self.done += 1
        assert self.at[name] == self.done, (name, self.at[name], self.done)
        return 1


def over(ap, n, axis):
    a = ap.unsqueeze(axis)
    shape = list(a.shape)
    shape[axis] = n
    return a.broadcast_to(shape)


RING = 3


def build(nc, a, o):
    g = Names()
    with ExitStack() as ctx:
        def sb(name, shape, dt=F32, **kw):
            return ctx.enter_context(nc.sbuf_tensor(name, shape, dt, **kw))

        def sem(name):
            return ctx.enter_context(nc.semaphore(name))

        cols, at = constant_columns()
        g.cst = sb("cst", [P, cols.shape[1]])
        g.c = {n: g.cst[:, lo:hi] for n, (lo, hi) in at.items()}
        g.sem, g.a, g.o, g.ctx = sem, a, o, ctx
        g.ps = ctx.enter_context(nc.psum_tensor("ps", [P, 8, 512], F32))
        g.mods_dram = nc.dram_tensor("mods_scratch", [2, 6, D], F32, kind="Internal").ap()
        g.ring = sb("ring", [P, RING, KD, 512])
        g.s_slot = [sem(f"slot_loaded{i}") for i in range(RING)]
        g.loads = 0
        phases(nc, g, sb, sem)


def slot(i):
    return i % RING


def loaded(i):
    return 32 * (i // RING + 1)


N_ADA = 6 * D // 512
IN_CHUNKS = [("cqkv", C_CQ), ("q", C_QKV), ("k", C_QKV + GW), ("v", C_QKV + 2 * GW), ("z", C_Z)]
GATE_CHUNKS = [("ga0", C_GA), ("gb0", C_GB), ("ga1", C_GA + 512), ("gb1", C_GB + 512)]
MERGE_LOADS = [x for n in range(2) for x in (f"ga{n}", f"gb{n}", ("ab", n))] + [("wo", 0), ("wo", 1)]
RING_LOADS = [("ada", n) for n in range(N_ADA)] + [c[0] for c in IN_CHUNKS] + MERGE_LOADS
LOAD = {n: i for i, n in enumerate(RING_LOADS)}
KP = 2
NPIECE = KD // KP


def load_slot(g, sp, i):
    name = RING_LOADS[i]
    half = KD // 2
    for h in range(2):
        if name in (("ab", 0), ("ab", 1)):
            src = g.a[("w_oa", "w_ob")[h]][0].rearrange("(p k) n -> p k n", k=half)[:, :, name[1] * 512:(name[1] + 1) * 512]
        else:
            if isinstance(name, tuple):
                w, c0 = g.a[{"ada": "w_ada", "wo": "w_o"}[name[0]]][0], name[1] * 512
            else:
                w, c0 = g.a["w_in"][0], dict(IN_CHUNKS + GATE_CHUNKS)[name]
            src = w.rearrange("(p k) n -> p k n", k=KD)[:, h * half:(h + 1) * half, c0:c0 + 512]
        sp.dma_start(g.ring[:, slot(i), h * half:(h + 1) * half], src).then_inc(g.s_slot[slot(i)], 16)


class Pieces:

    def __init__(self, nc, ctx, g, phase, base, depth):
        f32r = mybir.dt.float32r
        self.g, self.base, self.depth = g, base, depth
        self.hi = ctx.enter_context(nc.sbuf_tensor(phase + "_w_hi", [P, depth, KP, 512], f32r))
        self.lo = ctx.enter_context(nc.sbuf_tensor(phase + "_w_lo", [P, depth, KP, 512], f32r))
        self.hi_made, self.lo_made, self.used = (g.sem(phase + x) for x in ("_hi_made", "_lo_made", "_pieces_used"))

    def number(self, load, i):
        return (load - self.base) * NPIECE + i

    def split_up(self, load):
        return self.number(load, NPIECE)

    def make_hi(self, act, load, i):
        n, w = self.number(load, i), self.g.ring[:, slot(load), i * KP:(i + 1) * KP]
        if i == 0:
            act.wait_ge(self.g.s_slot[slot(load)], loaded(load))
        if n >= self.depth:
            act.wait_ge(self.used, n - self.depth + 1)
        act.activation(self.hi[:, n % self.depth], w, ACT.Copy).then_inc(self.hi_made, 1)

    def make_lo(self, eng, load, i):
        n, w = self.number(load, i), self.g.ring[:, slot(load), i * KP:(i + 1) * KP]
        eng.wait_ge(self.hi_made, n + 1)
        eng.tensor_tensor(self.lo[:, n % self.depth], w, self.hi[:, n % self.depth].bitcast(F32), ALU.subtract) \
            .then_inc(self.lo_made, 1)


PASSES = ((0, 0), (0, 1), (1, 0))


def run_ahead(last, depth):
    at = [(n, i) for n in range(last + 1) for i in range(NPIECE)]
    return [at[:depth]] + [at[depth + n * NPIECE:depth + (n + 1) * NPIECE] for n in range(last + 1)]


def phase_condition(nc, g):
    a, ps, c = g.a, g.ps, g.c
    with ExitStack() as ctx:
        def sb(name, shape):
            return ctx.enter_context(nc.sbuf_tensor(name, shape, F32))
        cond = sb("cond", [P, 2, KD])
        scond = sb("scond", [P, 2, KD])
        mods = sb("mods", [2, 6 * D])
        conds = ctx.enter_context(nc.sbuf_tensor("conds", [P, 2, 2, KD], mybir.dt.float32r))
        w = Pieces(nc, ctx, g, "ada", LOAD[("ada", 0)], 6)
        ahead = run_ahead(N_ADA - 1, w.depth)
        x = sb("x", [P, TILES, D])
        xn = x
        scratch = g.hT[:].rearrange("p k n -> p (k n)").rearrange("p (t d) -> p t d", d=D)
        gains = sb("gains", [2, 3, D])
        s_gain = g.sem("gains_of_mods_loaded")
        stat = sb("stat", [P, 4, TILES])
        modT = sb("modT", [P, 2, 2, KD])
        gpre = sb("gpre", [P, KD])
        scaleT = sb("scaleT", [P, 2, KD])
        convrow = sb("convrow", [CONV * 12, P])
        s_c, s_cst, s_b, s_x, s_conv, s_g = (g.sem(n) for n in
            ("cond_loaded", "const_loaded", "bias_loaded", "x_loaded", "convw_loaded", "gpre_loaded"))
        s_mods = g.sem("mods_stored")
        pe_done, dve_done, act_done = g.sem("cond_pe"), g.sem("cond_dve"), g.sem("cond_act")
        pe_order = ["modT", "convT", ("xT", 0), ("xT", 1), ("xT", 2)]
        PE = Count(pe_order)
        dve_order = ["cond_lo", "ms", "rms"] + [("xn", t) for t in range(TILES)] + [("mods", n) for n in range(5)] \
            + ["modT", "A1", "A", ("mods", 5), ("gain", 2), "convT", ("hT", 0), ("hT", 1), ("mods", 6), ("mods", 7),
               ("mods", 8), ("hT", 2), ("mods", 9), ("gain", 4), ("mods", 10), ("mods", 11), ("gain", 5)]
        V = Count(dve_order)
        A = Count(["scond", "cond_hi"] + [("ss", t) for t in range(TILES)] + ["rs"])
        with nc.Block() as block:
            @block.sync
            def _(sp):
                for v, src in ((0, a["c_ctx"]), (1, a["c"][0])):
                    sp.dma_start(cond[:, v, :], src.rearrange("(p k) -> p k", k=KD)).then_inc(s_c, 16)
                for n in range(RING):
                    load_slot(g, sp, n)
                sp.dma_start(mods[:], a["b_ada"][0].partition_broadcast(2)).then_inc(s_b, 16)
                sp.dma_start(g.cst[:], a["table"]).then_inc(s_cst, 16)
                for n in range(RING, LOAD["v"]):
                    sp.wait_ge(w.lo_made, w.split_up(n - RING))
                    load_slot(g, sp, n)
                sp.wait_ge(dve_done, V[("gain", 5)])
                sp.dma_start(g.mods_dram[:, 2:6, :].rearrange("v m d -> v (m d)"),
                             mods[:, 2 * D:6 * D]).then_inc(s_mods, 16)
                sp.wait_ge(s_mods, 16)

            @block.scalar
            def _(act):
                act.dma_start(x[:, 0, :], a["x_prompt"][0]).then_inc(s_x, 16)
                act.dma_start(x[:, 1:3, :], a["x_sample"][0].rearrange("(t p) d -> p t d", p=P)).then_inc(s_x, 16)
                act.dma_start(convrow[:], a["conv_w"][0].rearrange("j (m p) -> (j m) p", p=P)).then_inc(s_conv, 16)
                act.dma_start(gpre[:], a["g_pre_mix"][0].rearrange("(p k) -> p k", k=KD)).then_inc(s_g, 16)
                for i, name in enumerate(("g_post_mix", "g_pre_ffn", "g_post_ffn")):
                    act.dma_start(gains[:, i], a[name][0].partition_broadcast(2)).then_inc(s_gain, 16)
                act.wait_ge(s_c, 32)
                act.activation(scond[:], cond[:], ACT.Silu).then_inc(act_done, A.step("scond"))
                act.wait_ge(act_done, A["scond"])
                act.activation(conds[:, 0], scond[:], ACT.Copy).then_inc(act_done, A.step("cond_hi"))
                for n, i in ahead[0]:
                    w.make_hi(act, n, i)
                act.wait_ge(s_x, 32)
                for t in range(TILES):
                    act.activation(scratch[:, t, :], x[:, t, :], ACT.Square, accum_out=stat[:, 0, t:t + 1]) \
                        .then_inc(act_done, A.step("ss", t))
                act.wait_ge(dve_done, V["rms"])
                act.activation(stat[:, 3, :], stat[:, 2, :], ACT.Sqrt).then_inc(act_done, A.step("rs"))
                for some in ahead[1:]:
                    for n, i in some:
                        w.make_hi(act, n, i)

            @block.tensor
            def _(pe):
                def transposes(t):
                    for k in range(KD):
                        mm = pe.transpose(ps[:, 4 + 2 * (t % 2) + k // 4, (k % 4) * P:(k % 4 + 1) * P],
                                          xn[:, t, k::KD], c["ident"])
                    mm.then_inc(pe_done, PE.step("xT", t))

                pe.wait_ge(dve_done, V["cond_lo"])
                for n in range(N_ADA):
                    if n >= 4:
                        pe.wait_ge(dve_done, V[("mods", n - 4)])
                    for i in range(NPIECE):
                        at = w.number(n, i)
                        pe.wait_ge(w.hi_made, at + 1)
                        pe.wait_ge(w.lo_made, at + 1)
                        for k in range(KP):
                            for x, y in PASSES:
                                mm = pe.matmul(ps[0:2, n % 4, :], conds[:, x, :, i * KP + k],
                                               (w.hi, w.lo)[y][:, at % w.depth, k, :],
                                               start=(i == 0 and k == 0 and (x, y) == PASSES[0]),
                                               stop=(i == NPIECE - 1 and k == KP - 1 and (x, y) == PASSES[-1]))
                        mm.then_inc(w.used, 1)
                    if n == 4:
                        pe.wait_ge(s_cst, 16)
                        pe.wait_ge(dve_done, V[("mods", 3)])
                        for mk in range(2 * KD):
                            m, k = divmod(mk, KD)
                            mm = pe.transpose(ps[:, 4, 2 * mk:2 * mk + 2], mods[:, m * D + k:(m + 1) * D:KD],
                                              c["ident"][0:2, 0:2])
                        mm.then_inc(pe_done, PE.step("modT"))
                    if n == 5:
                        pe.wait_ge(dve_done, V["modT"])
                        pe.wait_ge(s_conv, 16)
                        pe.transpose(ps[:, 4, 0:CONV * 12], convrow[:], c["ident"][0:CONV * 12, 0:CONV * 12]) \
                            .then_inc(pe_done, PE.step("convT"))
                        pe.wait_ge(dve_done, V["convT"])
                        transposes(0)
                        transposes(1)
                    if n == 8:
                        pe.wait_ge(dve_done, V[("hT", 0)])
                        transposes(2)

            @block.vector
            def _(dve):
                dve.wait_ge(act_done, A["cond_hi"])
                dve.tensor_tensor(conds[:, 1], scond[:], conds[:, 0].bitcast(F32), ALU.subtract) \
                    .then_inc(dve_done, V.step("cond_lo"))
                for n, i in ahead[0]:
                    w.make_lo(dve, n, i)
                dve.wait_ge(act_done, A[("ss", TILES - 1)])
                dve.tensor_scalar(stat[:, 1, :], stat[:, 0, :], 1.0 / D, EPS, ALU.mult, ALU.add) \
                    .then_inc(dve_done, V.step("ms"))
                dve.wait_ge(dve_done, V["ms"])
                dve.reciprocal(stat[:, 2, :], stat[:, 1, :]).then_inc(dve_done, V.step("rms"))
                dve.wait_ge(act_done, A["rs"])
                for t in range(TILES):
                    dve.tensor_scalar(xn[:, t, :], x[:, t, :], stat[:, 3, t:t + 1], None, ALU.mult) \
                        .then_inc(dve_done, V.step("xn", t))
                dve.wait_ge(s_b, 16)

                def take_mods(n):
                    for m, i in ahead[n + 1]:
                        w.make_lo(dve, m, i)
                    dve.wait_ge(w.used, w.split_up(n))
                    dve.tensor_tensor(mods[:, n * 512:(n + 1) * 512], ps[0:2, n % 4, :],
                                      mods[:, n * 512:(n + 1) * 512], ALU.add).then_inc(dve_done, V.step("mods", n))

                def gained(m, i, plus):
                    row = mods[:, m * D:(m + 1) * D]
                    dve.wait_ge(dve_done, V[("mods", 2 * m + 1)])
                    dve.scalar_tensor_tensor(out=row, in0=row, scalar=plus, in1=gains[:, i], op0=ALU.add, op1=ALU.mult) \
                        .then_inc(dve_done, V.step("gain", m))

                def take_hT(t):
                    dve.wait_ge(pe_done, PE[("xT", t)])
                    v = min(t, 1)
                    for k in range(KD):
                        i = dve.tensor_scalar(g.hT[:, k, t * P:(t + 1) * P],
                                              ps[:, 4 + 2 * (t % 2) + k // 4, (k % 4) * P:(k % 4 + 1) * P],
                                              scaleT[:, v, k:k + 1], modT[:, v, 0, k:k + 1], ALU.mult, ALU.add)
                    i.then_inc(dve_done, V.step("hT", t))

                for n in range(5):
                    take_mods(n)
                dve.wait_ge(pe_done, PE["modT"])
                dve.tensor_copy(modT[:], ps[:, 4, 0:4 * KD].rearrange("p (m k v) -> p v m k", m=2, v=2)) \
                    .then_inc(dve_done, V.step("modT"))
                dve.wait_ge(dve_done, V["modT"])
                dve.wait_ge(s_g, 16)
                dve.tensor_scalar(scaleT[:], modT[:, :, 1, :], 1.0, None, ALU.add).then_inc(dve_done, V.step("A1"))
                dve.wait_ge(dve_done, V["A1"])
                dve.tensor_tensor(scaleT[:], scaleT[:], over(gpre[:], 2, 1), ALU.mult).then_inc(dve_done, V.step("A"))
                dve.wait_ge(dve_done, V["A"])
                take_mods(5)
                dve.wait_ge(s_gain, 48)
                gained(2, 0, 0.0)
                dve.wait_ge(pe_done, PE["convT"])
                dve.tensor_copy(g.wconv[:], ps[:, 4, 0:CONV * 12].rearrange("p (j m) -> p j m", j=CONV)) \
                    .then_inc(dve_done, V.step("convT"))
                take_hT(0)
                take_hT(1)
                for n in range(6, 9):
                    take_mods(n)
                take_hT(2)
                take_mods(9)
                gained(4, 1, 1.0)
                take_mods(10)
                take_mods(11)
                gained(5, 2, 0.0)


def phase_project(nc, g):
    a, ps = g.a, g.ps
    with ExitStack() as ctx:
        def sb(name, shape):
            return ctx.enter_context(nc.sbuf_tensor(name, shape, F32))
        hs = ctx.enter_context(nc.sbuf_tensor("hs", [P, 2, KD, TOK], mybir.dt.float32r))
        w = Pieces(nc, ctx, g, "in", LOAD["cqkv"], 6)
        loads = [LOAD[name] for name, _ in IN_CHUNKS]
        ahead = run_ahead(len(loads) - 1, w.depth)
        wsmall = sb("wsmall", [P, KD, 64])
        acc = sb("acc", [P, 2, OUTW])
        pad = sb("pad", [P, 2, PADW])
        s_small = g.sem("wsmall_loaded")
        pe_done, dve_done, act_done = g.sem("proj_pe"), g.sem("proj_dve"), g.sem("proj_act")
        units = [("cqkv", t) for t in range(TILES)] + [("small", t) for t in range(TILES)] \
            + [(n, m) for n in "qkv" for m in range(4)] + [("z", t) for t in range(TILES)]
        final = {name: max(m for n, m in units if n == name) for name, _ in IN_CHUNKS}
        PE = Count([u for u in units if final.get(u[0]) != u[1]])
        A = Count([("h_hi", t) for t in range(TILES)] + ["gaps"] + [("cqkv", t) for t in range(TILES)] + [("small", t) for t in range(TILES)]
                  + [x for i in range(12) for x in ((("pad", i),) + ((("silu", i - 1),) if i else ()))]
                  + [("silu", 11)] + [("z", t) for t in range(TILES)])
        V = Count([("h_lo", t) for t in range(TILES)]
                  + [(s, i) for i in range(12) for s in [f"tap{j}" for j in range(CONV)]])

        def wait_unit(eng, name, m):
            if final.get(name) == m:
                eng.wait_ge(w.used, w.split_up(LOAD[name]))
            else:
                eng.wait_ge(pe_done, PE[(name, m)])

        with nc.Block() as block:
            @block.sync
            def _(sp):
                ws = a["w_in"][0].rearrange("(p k) n -> p k n", k=KD)
                sp.dma_start(wsmall[:, :, 0:32], ws[:, :, C_KR:C_KR + 32]).then_inc(s_small, 16)
                sp.dma_start(wsmall[:, :, 32:64], ws[:, :, C_AB:C_AB + 32]).then_inc(s_small, 16)
                sp.dma_start(g.wuq[:], a["w_uq"][0].rearrange("(p j) n -> p j n", j=KL)).then_inc(g.s_attw, 16)
                sp.dma_start(g.wukv[:], a["w_ukv"][0].rearrange("(p j) n -> p j n", j=KL)).then_inc(g.s_attw, 16)
                for name in ("v", "z", "ga0", "gb0", ("ab", 0)):
                    n = LOAD[name]
                    sp.wait_ge(w.lo_made, w.split_up(n - RING))
                    load_slot(g, sp, n)

            @block.tensor
            def _(pe):
                for i, (name, m) in enumerate(units):
                    b = i % 8
                    if name == "small":
                        pe.wait_ge(s_small, 32)
                    if name == "cqkv":
                        pe.wait_ge(dve_done, V[("h_lo", m)])
                    if i >= 8:
                        was = units[i - 8]
                        pe.wait_ge(act_done, A[("pad", "qkv".index(was[0]) * 4 + was[1])
                                               if was[0] in "qkv" else was])
                    if name == "small":
                        for k in range(KD):
                            mm = pe.matmul(ps[:, b, 0:64], g.hT[:, k, m * P:(m + 1) * P], wsmall[:, k, :],
                                           start=(k == 0), stop=(k == KD - 1))
                        mm.then_inc(pe_done, PE.step(name, m))
                        continue
                    for p in range(NPIECE):
                        at = w.number(LOAD[name], p)
                        if m == 0:
                            pe.wait_ge(w.hi_made, at + 1)
                            pe.wait_ge(w.lo_made, at + 1)
                        for k in range(KP):
                            for x, y in PASSES:
                                ws = (w.hi, w.lo)[y][:, at % w.depth, k, :]
                                if name in ("cqkv", "z"):
                                    out, left, right = ps[:, b, :], hs[:, x, p * KP + k, m * P:(m + 1) * P], ws
                                else:
                                    out, left, right = ps[:, b, 0:TOK], ws[:, m * P:(m + 1) * P], hs[:, x, p * KP + k, :]
                                mm = pe.matmul(out, left, right, start=(p == 0 and k == 0 and (x, y) == PASSES[0]),
                                               stop=(p == NPIECE - 1 and k == KP - 1 and (x, y) == PASSES[-1]))
                        if final[name] == m:
                            mm.then_inc(w.used, 1)
                    if final[name] != m:
                        mm.then_inc(pe_done, PE.step(name, m))

            @block.scalar
            def _(act):
                for t in range(TILES):
                    act.activation(hs[:, 0, :, t * P:(t + 1) * P], g.hT[:, :, t * P:(t + 1) * P], ACT.Copy) \
                        .then_inc(act_done, A.step("h_hi", t))
                    for n, i in ahead[0][2 * t:2 * t + 2]:
                        w.make_hi(act, loads[n], i)
                for b in range(2):
                    for z in (0, GAP + CTX, PADW - GAP):
                        i = act.activation(pad[:, b, z:z + GAP], g.c["ident"][:, 0:GAP], ACT.Copy, scale=0.0)
                i.then_inc(act_done, A.step("gaps"))
                at = 0

                def splits(name, m):
                    if final.get(name) == m:
                        for n, i in ahead[LOAD[name] - w.base + 1]:
                            w.make_hi(act, loads[n], i)

                def take(dst, width, name, m):
                    nonlocal at
                    splits(name, m)
                    wait_unit(act, name, m)
                    act.activation(dst, ps[:, at % 8, 0:width], ACT.Copy).then_inc(act_done, A.step(name, m))
                    at += 1

                def silu(i):
                    act.wait_ge(dve_done, V[("tap4", i)])
                    act.activation(g.qkv[:, i, :], acc[:, i % 2, :], ACT.Silu).then_inc(act_done, A.step("silu", i))

                for t in range(TILES):
                    take(g.cqkv[:, t, :], 512, "cqkv", t)
                for t in range(TILES):
                    take(g.small[:, t, :], 64, "small", t)
                for i in range(12):
                    splits("qkv"[i // 4], i % 4)
                    wait_unit(act, "qkv"[i // 4], i % 4)
                    if i >= 2:
                        act.wait_ge(dve_done, V[("tap4", i - 2)])
                    act.activation(pad[:, i % 2, GAP:GAP + CTX], ps[:, at % 8, 0:CTX], ACT.Copy)
                    act.activation(pad[:, i % 2, 2 * GAP + CTX:2 * GAP + TOK], ps[:, at % 8, CTX:TOK], ACT.Copy) \
                        .then_inc(act_done, A.step("pad", i))
                    at += 1
                    if i:
                        silu(i - 1)
                silu(11)
                for t in range(TILES):
                    take(g.z[:, t, :], 512, "z", t)

            @block.vector
            def _(dve):
                for t in range(TILES):
                    tc = slice(t * P, (t + 1) * P)
                    dve.wait_ge(act_done, A[("h_hi", t)])
                    dve.tensor_tensor(hs[:, 1, :, tc], g.hT[:, :, tc], hs[:, 0, :, tc].bitcast(F32), ALU.subtract) \
                        .then_inc(dve_done, V.step("h_lo", t))
                    for n, i in ahead[0][2 * t:2 * t + 2]:
                        w.make_lo(dve, loads[n], i)
                for i in range(12):
                    if i == 0 or i % 4 == 3:
                        for n, p in ahead[1 if i == 0 else 2 + i // 4]:
                            w.make_lo(dve, loads[n], p)
                    dve.wait_ge(act_done, A[("pad", i)])
                    if i >= 2:
                        dve.wait_ge(act_done, A[("silu", i - 2)])
                    for j in range(CONV):
                        src = pad[:, i % 2, j:j + OUTW]
                        tap = g.wconv[:, j, i:i + 1]
                        if j == 0:
                            ins = dve.tensor_scalar(acc[:, i % 2, :], src, tap, None, ALU.mult)
                        else:
                            dve.wait_ge(dve_done, V[(f"tap{j - 1}", i)])
                            ins = dve.scalar_tensor_tensor(out=acc[:, i % 2, :], in0=src, scalar=tap,
                                                           in1=acc[:, i % 2, :], op0=ALU.mult, op1=ALU.add)
                        ins.then_inc(dve_done, V.step(f"tap{j}", i))


def phase_attention(nc, g):
    a, ps, c, o = g.a, g.ps, g.c, g.o
    KT = TILES + 1
    SCALE = float(QK) ** -0.5
    with ExitStack() as ctx:
        def sb(name, shape):
            return ctx.enter_context(nc.sbuf_tensor(name, shape, F32))
        wuq, wukv, s_w = g.wuq, g.wukv, g.s_attw
        grow = sb("grow", [P, 2, LORA])
        kr = sb("kr", [P, KT, ROPE])
        ckv = sb("ckv", [P, KT, LORA])
        cqn = sb("cqn", [P, TILES, LORA])
        stat = sb("astat", [P, 4, 6])
        cqT = sb("cqT", [P, KL, TOK])
        ckvT = sb("ckvT", [P, KL, KT * P])
        q = sb("q", [P, TILES, MH, QK])
        k = sb("k", [P, KT, MH, QK])
        v = sb("v", [P, KT, MH, VH])
        qT = sb("qT", [QK, MH, TOK])
        kT = sb("kT", [QK, MH, KT * P])
        prob = sb("prob", [P, 3, 3 * P])
        probT = sb("probT", [P, 2, 3, P])
        nmax = sb("nmax", [P, TILES, MH])
        rsum = sb("rsum", [P, TILES, MH])
        rinv = sb("rinv", [P, TILES, MH])
        rope = sb("ropetmp", [P, 4, MH, 2, 8])
        s_g, s_cache, s_out = (g.sem(n) for n in ("gains_loaded", "cache_loaded", "ckv_stored"))
        pe_done, dve_done, act_done = g.sem("att_pe"), g.sem("att_dve"), g.sem("att_act")
        units = [(t, h) for t in range(TILES) for h in range(MH)]
        nk = lambda t: 1 if t == 0 else 3
        k0 = lambda t: 0 if t == 0 else 1
        loop = []
        for i in range(len(units) + 3):
            if i < len(units):
                loop.append(("score", i))
            if 2 <= i < len(units) + 2:
                loop.append(("probT", i - 2))
            if i >= 3:
                loop.append(("pv", i - 3))
        SB = (0, 1, 7)
        PE = Count(["cqT", "ckvT"] + [("q", t) for t in range(TILES)] + [("kv", t) for t in range(KT)]
                   + [("qT", t) for t in range(TILES)] + [("kT", t) for t in range(KT)] + loop)
        rope_steps = lambda n: [(n, s) for s in ("ac", "bs", "bc", "as", "a", "b")]
        V = Count(["ms", "rms", "cqn0", "cqn", "ckv0", "ckv"] + rope_steps("kr1") + rope_steps("kr2")
                  + ["cqT"]
                  + [("q", t) for t in range(TILES)] + rope_steps("q1") + rope_steps("q2")
                  + [("kr", t) for t in range(KT)] + [("qT", t) for t in range(TILES)]
                  + [x for i in range(len(units) + 2) for x in
                     ([("max", i)] if i < len(units) else []) + ([("probT", i - 2)] if i >= 2 else [])]
                  + ["rinv", "o"])
        A = Count([("ss", i) for i in range(6)] + ["rs", "ckvT"] + [("kv", t) for t in range(KT)]
                  + [("kT", t) for t in range(KT)] + [("exp", i) for i in range(len(units))])
        with nc.Block() as block:
            @block.sync
            def _(sp):
                sp.dma_start(grow[:, 0, :], a["q_norm_g"][0].partition_broadcast(P)).then_inc(s_g, 16)
                sp.dma_start(grow[:, 1, :], a["kv_norm_g"][0].partition_broadcast(P)).then_inc(s_g, 16)
                sp.dma_start(ckv[:, 1, :], a["cache_ckv"][0, 0]).then_inc(s_cache, 16)
                sp.dma_start(kr[:, 1, :], a["cache_krope"][0, 0]).then_inc(s_cache, 16)
                sp.dma_start(o["krope"][0, 0], g.small[:, 0, 0:ROPE]).then_inc(s_out, 16)
                sp.wait_ge(dve_done, V["ckv"])
                sp.dma_start(o["ckv"][0, 0], ckv[:, 0, :]).then_inc(s_out, 16)
                sp.wait_ge(s_out, 32)

            @block.scalar
            def _(act):
                for i in range(6):
                    t, part = i % 3, i // 3
                    junk = cqn[:, t, :] if part == 0 else ckv[:, (0, 2, 3)[t], :]
                    act.activation(junk, g.cqkv[:, t, part * LORA:(part + 1) * LORA], ACT.Square,
                                   accum_out=stat[:, 0, i:i + 1]).then_inc(act_done, A.step("ss", i))
                act.wait_ge(dve_done, V["rms"])
                act.activation(stat[:, 3, :], stat[:, 2, :], ACT.Sqrt).then_inc(act_done, A.step("rs"))
                act.wait_ge(pe_done, PE["ckvT"])
                act.activation(ckvT[:], ps[:, 2:4, :], ACT.Copy).then_inc(act_done, A.step("ckvT"))
                for t in range(KT):
                    b = 2 * (t % 2)
                    act.wait_ge(pe_done, PE[("kv", t)])
                    src = ps[:, b:b + 2, :].rearrange("p b (h e) -> p (b h) e", e=P)
                    act.activation(k[:, t, :, 0:NOPE], src[:, :, 0:NOPE], ACT.Copy)
                    act.activation(v[:, t], src[:, :, NOPE:P], ACT.Copy).then_inc(act_done, A.step("kv", t))
                for t in range(KT):
                    b = 2 * (t % 2)
                    act.wait_ge(pe_done, PE[("kT", t)])
                    act.activation(kT[:, :, t * P:(t + 1) * P],
                                   ps[0:QK, b:b + 2, :].rearrange("p b (h e) -> p (b h) e", e=P), ACT.Copy) \
                        .then_inc(act_done, A.step("kT", t))
                for i, (t, h) in enumerate(units):
                    w = nk(t) * P
                    act.wait_ge(dve_done, V[("max", i)])
                    if i >= 3:
                        act.wait_ge(pe_done, PE[("probT", i - 3)])
                    act.activation(prob[:, i % 3, 0:w], ps[:, SB[i % 3], 0:w], ACT.Exp, bias=nmax[:, t, h:h + 1],
                                   accum_out=rsum[:, t, h:h + 1]).then_inc(act_done, A.step("exp", i))

            @block.tensor
            def _(pe):
                pe.wait_ge(dve_done, V["cqn"])
                for j in range(KL):
                    for t in range(TILES):
                        mm = pe.transpose(ps[:, j, t * P:(t + 1) * P], cqn[:, t, j::KL], c["ident"])
                mm.then_inc(pe_done, PE.step("cqT"))
                pe.wait_ge(dve_done, V["ckv"])
                pe.wait_ge(s_cache, 32)
                for j in range(KL):
                    for t in range(KT):
                        mm = pe.transpose(ps[:, 2 + j, t * P:(t + 1) * P], ckv[:, t, j::KL], c["ident"])
                mm.then_inc(pe_done, PE.step("ckvT"))
                pe.wait_ge(s_w, 32)
                pe.wait_ge(dve_done, V["cqT"])
                for t in range(TILES):
                    b = 4 + 2 * (t % 2)
                    if t >= 2:
                        pe.wait_ge(dve_done, V[("q", t - 2)])
                    for lo, hi in ((0, 512), (512, MH * QK)):
                        for j in range(KL):
                            mm = pe.matmul(ps[:, b + lo // 512, 0:hi - lo], cqT[:, j, t * P:(t + 1) * P],
                                           wuq[:, j, lo:hi], start=(j == 0), stop=(j == KL - 1))
                    mm.then_inc(pe_done, PE.step("q", t))
                pe.wait_ge(act_done, A["ckvT"])
                for t in range(KT):
                    b = 2 * (t % 2)
                    if t >= 2:
                        pe.wait_ge(act_done, A[("kv", t - 2)])
                    for n in range(2):
                        for j in range(KL):
                            mm = pe.matmul(ps[:, b + n, :], ckvT[:, j, t * P:(t + 1) * P],
                                           wukv[:, j, n * 512:(n + 1) * 512], start=(j == 0), stop=(j == KL - 1))
                    mm.then_inc(pe_done, PE.step("kv", t))
                for t in range(TILES):
                    b = 4 + 2 * (t % 2)
                    pe.wait_ge(dve_done, V[("q2", "b")])
                    if t >= 2:
                        pe.wait_ge(dve_done, V[("qT", t - 2)])
                    for h in range(MH):
                        mm = pe.transpose(ps[0:QK, b + h // 4, (h % 4) * P:(h % 4 + 1) * P], q[:, t, h, :], c["ident"])
                    mm.then_inc(pe_done, PE.step("qT", t))
                for t in range(KT):
                    b = 2 * (t % 2)
                    pe.wait_ge(act_done, A[("kv", KT - 1)])
                    pe.wait_ge(dve_done, V[("kr", t)])
                    if t >= 2:
                        pe.wait_ge(act_done, A[("kT", t - 2)])
                    for h in range(MH):
                        mm = pe.transpose(ps[0:QK, b + h // 4, (h % 4) * P:(h % 4 + 1) * P], k[:, t, h, :], c["ident"])
                    mm.then_inc(pe_done, PE.step("kT", t))
                pe.wait_ge(act_done, A[("kT", KT - 1)])
                pe.wait_ge(dve_done, V[("qT", TILES - 1)])
                for i in range(len(units) + 3):
                    if i < len(units):
                        t, h = units[i]
                        if i >= 3:
                            pe.wait_ge(act_done, A[("exp", i - 3)])
                        pe.matmul(ps[:, SB[i % 3], 0:nk(t) * P], qT[:, h, t * P:(t + 1) * P],
                                  kT[:, h, k0(t) * P:(k0(t) + nk(t)) * P], start=True, stop=True) \
                            .then_inc(pe_done, PE.step("score", i))
                    if 2 <= i < len(units) + 2:
                        u = i - 2
                        t, h = units[u]
                        pe.wait_ge(act_done, A[("exp", u)])
                        if u >= 2:
                            pe.wait_ge(dve_done, V[("probT", u - 2)])
                        for n in range(nk(t)):
                            mm = pe.transpose(ps[:, 2 + u % 2, n * P:(n + 1) * P],
                                              prob[:, u % 3, n * P:(n + 1) * P], c["ident"])
                        mm.then_inc(pe_done, PE.step("probT", u))
                    if i >= 3:
                        u = i - 3
                        t, h = units[u]
                        pe.wait_ge(dve_done, V[("probT", u)])
                        for n in range(nk(t)):
                            mm = pe.matmul(ps[:, 4 + t, h * VH:(h + 1) * VH], probT[:, u % 2, n, :],
                                           v[:, k0(t) + n, h, :], start=(n == 0), stop=(n == nk(t) - 1))
                        mm.then_inc(pe_done, PE.step("pv", u))

            @block.vector
            def _(dve):
                dve.wait_ge(act_done, A[("ss", 5)])
                dve.tensor_scalar(stat[:, 1, :], stat[:, 0, :], 1.0 / LORA, EPS, ALU.mult, ALU.add) \
                    .then_inc(dve_done, V.step("ms"))
                dve.wait_ge(dve_done, V["ms"])
                dve.reciprocal(stat[:, 2, :], stat[:, 1, :]).then_inc(dve_done, V.step("rms"))
                dve.wait_ge(act_done, A["rs"])
                dve.wait_ge(s_g, 32)
                for t in range(TILES):
                    i = dve.tensor_scalar(cqn[:, t, :], g.cqkv[:, t, 0:LORA], stat[:, 3, t:t + 1], None, ALU.mult)
                i.then_inc(dve_done, V.step("cqn0"))
                dve.wait_ge(dve_done, V["cqn0"])
                dve.tensor_tensor(cqn[:], cqn[:], over(grow[:, 0, :], TILES, 1), ALU.mult) \
                    .then_inc(dve_done, V.step("cqn"))
                key = (0, 2, 3)
                for t in range(TILES):
                    i = dve.tensor_scalar(ckv[:, key[t], :], g.cqkv[:, t, LORA:2 * LORA], stat[:, 3, 3 + t:4 + t],
                                          None, ALU.mult)
                i.then_inc(dve_done, V.step("ckv0"))
                dve.wait_ge(dve_done, V["ckv0"])
                for t in range(TILES):
                    i = dve.tensor_tensor(ckv[:, key[t], :], ckv[:, key[t], :], grow[:, 1, :], ALU.mult)
                i.then_inc(dve_done, V.step("ckv"))

                def rotate(name, dst, src, heads, t):
                    r = lambda n: rope[:, n, 0:heads]
                    x = src.rearrange("p h (x s f) -> p h x s f", x=2, s=2)
                    y = dst.rearrange("p h (x s f) -> p h x s f", x=2, s=2)
                    tab = lambda n: over(c[n][:, (t - 1) * 16:t * 16].rearrange("p (x f) -> p x f", x=2), heads, 1)
                    dve.tensor_tensor(r(0), x[:, :, :, 0], tab("cos"), ALU.mult).then_inc(dve_done, V.step(name, "ac"))
                    dve.tensor_tensor(r(1), x[:, :, :, 1], tab("sin"), ALU.mult).then_inc(dve_done, V.step(name, "bs"))
                    dve.tensor_tensor(r(2), x[:, :, :, 1], tab("cos"), ALU.mult).then_inc(dve_done, V.step(name, "bc"))
                    dve.tensor_tensor(r(3), x[:, :, :, 0], tab("sin"), ALU.mult).then_inc(dve_done, V.step(name, "as"))
                    dve.wait_ge(dve_done, V[(name, "as")])
                    dve.tensor_tensor(y[:, :, :, 0], r(0), r(1), ALU.subtract).then_inc(dve_done, V.step(name, "a"))
                    dve.tensor_tensor(y[:, :, :, 1], r(2), r(3), ALU.add).then_inc(dve_done, V.step(name, "b"))
                    dve.wait_ge(dve_done, V[(name, "b")])

                for t in (1, 2):
                    rotate(f"kr{t}", kr[:, t + 1:t + 2, :], g.small[:, t:t + 1, 0:ROPE], 1, t)
                dve.wait_ge(pe_done, PE["cqT"])
                dve.tensor_copy(cqT[:], ps[:, 0:2, 0:TOK]).then_inc(dve_done, V.step("cqT"))
                for t in range(TILES):
                    b = 4 + 2 * (t % 2)
                    dve.wait_ge(pe_done, PE[("q", t)])
                    flat = q[:, t].rearrange("p h e -> p (h e)")
                    dve.tensor_scalar(flat[:, 0:512], ps[:, b, :], SCALE, None, ALU.mult)
                    dve.tensor_scalar(flat[:, 512:MH * QK], ps[:, b + 1, 0:MH * QK - 512], SCALE, None, ALU.mult) \
                        .then_inc(dve_done, V.step("q", t))
                dve.wait_ge(dve_done, V[("q", TILES - 1)])
                for t in (1, 2):
                    rotate(f"q{t}", q[:, t, :, NOPE:QK], q[:, t, :, NOPE:QK], MH, t)
                dve.wait_ge(s_cache, 32)
                for t in range(KT):
                    src = g.small[:, 0, 0:ROPE] if t == 0 else kr[:, t, :]
                    dve.tensor_copy(k[:, t, :, NOPE:QK], over(src, MH, 1)).then_inc(dve_done, V.step("kr", t))
                for t in range(TILES):
                    b = 4 + 2 * (t % 2)
                    dve.wait_ge(pe_done, PE[("qT", t)])
                    dve.tensor_copy(qT[:, :, t * P:(t + 1) * P],
                                    ps[0:QK, b:b + 2, :].rearrange("p b (h e) -> p (b h) e", e=P)) \
                        .then_inc(dve_done, V.step("qT", t))
                for i in range(len(units) + 2):
                    if i < len(units):
                        t, h = units[i]
                        dve.wait_ge(pe_done, PE[("score", i)])
                        dve.tensor_reduce(nmax[:, t, h:h + 1], ps[:, SB[i % 3], 0:nk(t) * P], AX, ALU.max, negate=True) \
                            .then_inc(dve_done, V.step("max", i))
                    if i >= 2:
                        u = i - 2
                        t, h = units[u]
                        dve.wait_ge(pe_done, PE[("probT", u)])
                        if u >= 2:
                            dve.wait_ge(pe_done, PE[("pv", u - 2)])
                        dve.tensor_copy(probT[:, u % 2, 0:nk(t), :].rearrange("p n q -> p (n q)"),
                                        ps[:, 2 + u % 2, 0:nk(t) * P]).then_inc(dve_done, V.step("probT", u))
                dve.wait_ge(act_done, A[("exp", len(units) - 1)])
                dve.reciprocal(rinv[:], rsum[:]).then_inc(dve_done, V.step("rinv"))
                dve.wait_ge(dve_done, V["rinv"])
                dve.wait_ge(pe_done, PE[("pv", len(units) - 1)])
                for t in range(TILES):
                    i = dve.tensor_tensor(g.omla[:, t, :].rearrange("p (h e) -> p h e", h=MH),
                                          ps[:, 4 + t, :].rearrange("p (h e) -> p h e", h=MH),
                                          over(rinv[:, t, :], VH, 2), ALU.mult)
                i.then_inc(dve_done, V.step("o"))


def phase_delta(nc, g):
    a, ps, c, o = g.a, g.ps, g.c, g.o
    H2 = GH // 2
    N48 = 2 * TILES * GH
    DIRS = (0, 1)
    STORE = {0: 1, 1: 0, 2: 1}
    TR = [(t, r) for t in range(TILES) for r in DIRS]
    GROUPS_ = {0: [(0, 0), (0, 1)], 1: [(1, 0), (1, 1), (2, 0), (2, 1)]}
    SCANS = [(grp, n, r) for grp in (0, 1) for n in range(len(GROUPS_[grp])) for r in DIRS]

    def where(grp, n, r):
        seq = GROUPS_[grp]
        return seq[n] if r == 0 else seq[len(seq) - 1 - n]

    with ExitStack() as ctx:
        def sb(name, shape):
            return ctx.enter_context(nc.sbuf_tensor(name, shape, F32))
        ktok = sb("ktok", [P, TILES, GW])
        vtok = sb("vtok", [P, TILES, GW])
        LT = sb("LT", [P, 2, GH, P])
        X = sb("X", [P, 2, GH, P])
        Y = sb("Y", [P, 2, GH, P])
        PR = sb("PR", [P, 2, GH, P])
        kb = sb("kb", [P, 2, GW])
        kbg = sb("kbg", [P, 2, GW])
        vb = sb("vb", [P, 2, GW])
        kbT = LT[:, :, 0:H2, :]
        u = sb("u", [P, 2, 2, GH, DV])
        wT = sb("wT", [P, 2, 2, H2, P])
        aT = sb("aT", [P, 2, 2, GH, P])
        kd = sb("kd", [P, 2, 2, GW])
        S = sb("S", [P, 2, H2, DV])
        flatX = X[:].rearrange("p r h n -> p r (h n)")
        vn = flatX[:, :, 0:GW].rearrange("p r (s e) -> p r s e", s=GH)
        qs = flatX[:, :, GW:2 * GW].rearrange("p r (s e) -> p r s e", s=GH)
        og = g.qkv[:, 8:12, :].rearrange("p m n -> p (m n)")[:, 0:TILES * GW].rearrange(
            "p (t s e) -> p t s e", t=TILES, s=GH)
        sq = [x[:].rearrange("p r h n -> p (r h n)")[:, 0:4 * OUTW].rearrange("p (m n) -> p m n", m=4)
              for x in (X, LT)]
        spread = [x[:].rearrange("p r h n -> p (r h n)")[:, 0:TILES * GW].rearrange("p (t h d) -> p t h d", t=TILES, h=GH)
                  for x in (Y, PR)]
        norms = sb("norms", [P, 3, 2, TILES, GH])
        sq_out = LT[:].rearrange("p r h n -> p (r h n)")[:, 0:TILES * GW].rearrange(
            "p (t s e) -> p t s e", t=TILES, s=GH)
        arow = sb("arow", [P, 2, 2 * GH])
        gw = sb("gw", [P, 4, TILES, 2 * GH])
        gg = sb("gg", [P, TILES, 2, GH])
        beta = sb("beta", [P, TILES, 2, GH])
        gc = sb("gc", [P, 4, 2, TILES, GH])
        ex = sb("ex", [P, 4, 2, TILES, GH])
        glS = sb("glS", [P, 2, 2 * TILES, H2])
        gnrow = sb("gnrow", [P, DV])
        ostat = sb("ostat", [P, 4, TILES * GH])
        s_row, s_state, s_fin = g.sem("gdn_rows_loaded"), g.sem("state_loaded"), g.sem("state_stored")
        pe_done, dve_done, act_done, pool_done = (g.sem("gdn_" + n) for n in ("pe", "dve", "act", "pool"))

        def scan_after(t):
            return [s for s in SCANS if (s[0] == 0 and t == 0) or (s[0] == 1 and t == 2)]

        pe_o, dve_o, act_o, pool_o = [], [], [], ["state0", "og0"]
        act_o += [(x, n) for x in ("sq", "root") for n in "qk"]
        pe_o += [(x, n) for x in ("norm", "spread") for n in "qk"]
        dve_o += ["neps", "nrec"] + [(x, n) for x in ("expand", "normed") for n in "qk"]
        pe_o += ["vtok", "ktok"]
        act_o += ["vtok", "ktok"]
        dve_o += ["xa", "na"]
        act_o += ["expna", "ln", "expa", "expb"]
        dve_o += ["sp", "gg", "b1", "beta"]
        pe_o += ["cums"]
        dve_o += ["gc", "tdiff"]
        act_o += ["ex"]
        dve_o += ["glS"]
        for t in range(TILES):
            for r in DIRS:
                dve_o += [("kb", t, r), ("gtri", t, r)]
                pool_o += [("kbg", t, r), ("vb", t, r), ("kd", t, r)]
                pe_o += [("kbT", t, r), ("D", t, r)]
                act_o += [("kbT", t, r), ("E", t, r)]
            for r in DIRS:
                dve_o += [("D", t, r)]
                pool_o += [("Ei", t, r)]
                pe_o += [("KK", t, r), ("QK", t, r)]
            dve_o += [("Es", t, r) for r in DIRS]
            for r in DIRS:
                dve_o += [("LT", t, r), ("aT", t, r)]
                pe_o += [("L", t, r)]
            dve_o += [("X1", t, r) for r in DIRS] + [(x, t, r) for r in DIRS for x in ("Y1", "YI")]
            pool_o += [("X1", t, r) for r in DIRS]
            for s in LEVELS[1:]:
                for r in DIRS:
                    pe_o += [("P", t, r, s)]
                    dve_o += [("P", t, r, s)]
                for r in DIRS:
                    if s != LEVELS[-1]:
                        pe_o += [("X", t, r, s)]
                    pe_o += [("Y", t, r, s)]
                for r in DIRS:
                    if s != LEVELS[-1]:
                        dve_o += [("X", t, r, s)]
                    dve_o += [("Y", t, r, s)]
            for r in DIRS:
                pe_o += [("u", t, r), ("wT", t, r)]
                dve_o += [("u", t, r)]
                act_o += [("wT", t, r)]
            for sc in scan_after(t):
                pe_o += [("RQ", sc), ("OU", sc)]
                dve_o += [("vn", sc), ("qs", sc), ("Sg", sc), ("S", sc), ("o1", sc), ("o2", sc)]
        act_o += ["silu", "osq", "ors"]
        pool_o += ["zg"]
        dve_o += ["oss", "oms", "orec", "on", "out"]
        PE, V, A, G = Count(pe_o), Count(dve_o), Count(act_o), Count(pool_o)
        LAST = LEVELS[-1]
        slots = [(par * H2 + j, 2 * j + par, par, j) for par in range(2) for j in range(H2)]
        ctx_done = ("S", (0, 1, 1))

        def by_slot(x):
            return x.rearrange("p (j q) -> p q j", q=2)

        def heads(x):
            return x.rearrange("p (h d) -> p h d", h=GH)

        def banks(b):
            return ps[:, b:b + 2, :].rearrange("p b (j n) -> p (b j) n", j=H2)

        with nc.Block() as block:
            @block.sync
            def _(sp):
                sp.dma_start(arow[:, 0, :], a["a_log"][0].rearrange("r h -> (r h)").partition_broadcast(P)).then_inc(s_row, 16)
                sp.dma_start(arow[:, 1, :], a["dt_bias"][0].rearrange("r h -> (r h)").partition_broadcast(P)) \
                    .then_inc(s_row, 16)
                sp.dma_start(gnrow[:], a["gdn_norm_g"][0].partition_broadcast(P)).then_inc(s_row, 16)

                def state(x, r, par):
                    return x[0, 0, r].rearrange("(j q) k v -> q k j v", q=2)[par]

                sp.wait_ge(dve_done, V[ctx_done])
                for r in DIRS:
                    for par in range(2):
                        sp.dma_start(state(o["state"], r, par), S[par * DK:(par + 1) * DK, r]).then_inc(s_fin, 16)
                sp.wait_ge(s_fin, 64)
                for r in DIRS:
                    for par in range(2):
                        sp.dma_start(S[par * DK:(par + 1) * DK, r], state(a["state_delta"], r, par)).then_inc(s_state, 16)
                sp.wait_ge(s_state, 64)

            @block.gpsimd
            def _(pool):
                pool.memset(S[:], 0.0).then_inc(pool_done, G.step("state0"))
                pool.wait_ge(pe_done, PE["vtok"])
                pool.memset(og, 0.0).then_inc(pool_done, G.step("og0"))
                for t in range(TILES):
                    for r in DIRS:
                        d = STORE[t]
                        if t == 0 and r == 0:
                            pool.wait_ge(act_done, A["ktok"])
                            pool.wait_ge(dve_done, V["glS"])
                        if t:
                            pool.wait_ge(pe_done, PE[("wT", t - 1, 1)])
                        pool.wait_ge(dve_done, V[("kb", t, r)])
                        e = lambda n: over(ex[:, n, r, t, :], DK, 2)
                        pool.tensor_tensor(heads(kbg[:, r]), heads(kb[:, r]), e(0), ALU.mult) \
                            .then_inc(pool_done, G.step("kbg", t, r))
                        pool.tensor_tensor(heads(vb[:, r]), heads(vtok[:, t]), over(beta[:, t, r, :], DV, 2), ALU.mult) \
                            .then_inc(pool_done, G.step("vb", t, r))
                        if t == 2:
                            pool.wait_ge(pe_done, PE[("OU", (0, 1, 1))])
                        pool.tensor_tensor(heads(kd[:, d, r]), heads(ktok[:, t]), e(1), ALU.mult) \
                            .then_inc(pool_done, G.step("kd", t, r))
                    for r in DIRS:
                        pool.wait_ge(act_done, A[("E", t, r)])
                        pool.wait_ge(pe_done, PE[("D", t, r)])
                        pool.tensor_tensor(X[:, r], PR[:, r], over(c[f"incl{r}"], GH, 1), ALU.mult) \
                            .then_inc(pool_done, G.step("Ei", t, r))
                    for r in DIRS:
                        pool.wait_ge(dve_done, V[("X1", t, r)])
                        pool.tensor_tensor(X[:, r], X[:, r], over(c["ident"], GH, 1), ALU.add) \
                            .then_inc(pool_done, G.step("X1", t, r))
                zh = g.z[:].rearrange("p t (h e) -> p (t h) e", h=GH)
                pool.wait_ge(act_done, A["silu"])
                pool.wait_ge(s_row, 48)
                pool.tensor_tensor(zh, zh, over(gnrow[:], TILES * GH, 1), ALU.mult).then_inc(pool_done, G.step("zg"))

            @block.scalar
            def _(act):
                for i, n in enumerate("qk"):
                    act.activation(sq[i], g.qkv[:, 4 * i:4 * i + 4, :], ACT.Square).then_inc(act_done, A.step("sq", n))
                act.wait_ge(dve_done, V["nrec"])
                for i, n in enumerate("qk"):
                    act.activation(norms[:, 2, i], norms[:, 1, i], ACT.Sqrt, scale=1.0 / DK if n == "q" else 1.0) \
                        .then_inc(act_done, A.step("root", n))
                act.wait_ge(pe_done, PE["vtok"])
                act.activation(vtok[:], ps[:, 0:TILES, :], ACT.Copy).then_inc(act_done, A.step("vtok"))
                act.wait_ge(pe_done, PE["ktok"])
                act.activation(ktok[:], ps[:, 3:3 + TILES, :], ACT.Copy).then_inc(act_done, A.step("ktok"))
                act.wait_ge(dve_done, V["na"])
                act.activation(gw[:, 1], gw[:, 1], ACT.Exp).then_inc(act_done, A.step("expna"))
                act.wait_ge(act_done, A["expna"])
                act.activation(gw[:, 2], gw[:, 1], ACT.Ln, bias=1.0).then_inc(act_done, A.step("ln"))
                act.wait_ge(s_row, 48)
                act.activation(arow[:, 0, :], arow[:, 0, :], ACT.Exp).then_inc(act_done, A.step("expa"))
                act.activation(gw[:, 3], g.small[:, :, 48:64], ACT.Exp, scale=-1.0).then_inc(act_done, A.step("expb"))
                act.wait_ge(dve_done, V["tdiff"])
                act.activation(ex[:, 0], gc[:, 0], ACT.Exp)
                act.activation(ex[:, 2:4], gc[:, 2:4], ACT.Exp)
                act.activation(ex[:, 1], ex[:, 1], ACT.Exp).then_inc(act_done, A.step("ex"))
                for t in range(TILES):
                    for r in DIRS:
                        act.wait_ge(pe_done, PE[("kbT", t, r)])
                        act.activation(kbT[:, r].rearrange("p j n -> p (j n)"), ps[:, 4 * r + 2, :], ACT.Copy) \
                            .then_inc(act_done, A.step("kbT", t, r))
                        act.wait_ge(dve_done, V[("D", t, r)])
                        act.activation(PR[:, r], PR[:, r], ACT.Exp).then_inc(act_done, A.step("E", t, r))
                    for r in DIRS:
                        act.wait_ge(pe_done, PE[("wT", t, r)])
                        if t == 2:
                            act.wait_ge(pe_done, PE[("OU", (0, 1, 1))])
                        act.activation(wT[:, STORE[t], r].rearrange("p j n -> p (j n)"), ps[:, 4 * r + 3, :],
                                       ACT.Copy).then_inc(act_done, A.step("wT", t, r))
                act.activation(g.z[:], g.z[:], ACT.Silu).then_inc(act_done, A.step("silu"))
                act.wait_ge(dve_done, V[("o2", SCANS[-1])])
                act.activation(sq_out, og, ACT.Square).then_inc(act_done, A.step("osq"))
                act.wait_ge(dve_done, V["orec"])
                act.activation(ostat[:, 3], ostat[:, 2], ACT.Sqrt).then_inc(act_done, A.step("ors"))

            @block.tensor
            def _(pe):
                for i, n in enumerate("qk"):
                    pe.wait_ge(act_done, A[("sq", n)])
                    for t in range(TILES):
                        for m in range(4):
                            at = (i * TILES + t) * GH + 2 * m
                            mm = pe.matmul(ps[:, 7, at:at + 2], sq[i][:, m, tok_at(t):tok_at(t) + P],
                                           c["block"][:, 0:P:CHUNK], start=True, stop=True)
                    mm.then_inc(pe_done, PE.step("norm", n))
                for i, n in enumerate("qk"):
                    pe.wait_ge(dve_done, V[("expand", n)])
                    for t in range(TILES):
                        for m in range(4):
                            mm = pe.transpose(ps[:, 4 * i + m, tok_at(t):tok_at(t) + P],
                                              spread[i][:, t, 2 * m:2 * m + 2, :].rearrange("p h d -> p (h d)"),
                                              c["ident"])
                    mm.then_inc(pe_done, PE.step("spread", n))
                pe.wait_ge(dve_done, V[("normed", "q")])
                for t in range(TILES):
                    for m in range(4):
                        mm = pe.transpose(ps[:, t, m * P:(m + 1) * P], g.qkv[:, 8 + m, tok_at(t):tok_at(t) + P],
                                          c["ident"])
                mm.then_inc(pe_done, PE.step("vtok"))
                pe.wait_ge(dve_done, V[("normed", "k")])
                for t in range(TILES):
                    for m in range(4):
                        mm = pe.transpose(ps[:, 3 + t, m * P:(m + 1) * P], g.qkv[:, 4 + m, tok_at(t):tok_at(t) + P],
                                          c["ident"])
                mm.then_inc(pe_done, PE.step("ktok"))
                pe.wait_ge(dve_done, V["gg"])
                gv = gg[:].rearrange("p t r h -> p r t h")
                for r in DIRS:
                    pe.matmul(ps[:, 6, r * 24:(r + 1) * 24], c[f"incl{r}"], gv[:, r], start=True, stop=True)
                for n, m in enumerate(("block", "half0", "half1")):
                    mm = pe.matmul(ps[:, 6, (n + 1) * N48:(n + 2) * N48], c[m], gv, start=True, stop=True)
                mm.then_inc(pe_done, PE.step("cums"))
                for t in range(TILES):
                    tc = slice(tok_at(t), tok_at(t) + P)
                    for r in DIRS:
                        pe.wait_ge(dve_done, V[("kb", t, r)])
                        if t == 0:
                            pe.wait_ge(act_done, A["ktok"])
                            pe.wait_ge(dve_done, V["gc"])
                        else:
                            pe.wait_ge(dve_done, V[("u", t - 1, r)])
                            pe.wait_ge(act_done, A[("wT", t - 1, r)])
                            if t == 1:
                                pe.wait_ge(dve_done, V[("o2", (0, 1, r))])
                        for m in range(H2):
                            mm = pe.transpose(ps[:, 4 * r + 2, m * P:(m + 1) * P], kb[:, r, m * P:(m + 1) * P], c["ident"])
                        mm.then_inc(pe_done, PE.step("kbT", t, r))
                        pe.wait_ge(dve_done, V[("gtri", t, r)])
                        for b in range(2):
                            mm = pe.matmul(ps[:, 4 * r + b, :], c["ones"],
                                           X[:, r, 4 * b:4 * b + 4].rearrange("p h n -> p (h n)"), start=True, stop=True)
                        mm.then_inc(pe_done, PE.step("D", t, r))
                    for r in DIRS:
                        pe.wait_ge(act_done, A[("kbT", t, r)])
                        for s, h, par, j in slots:
                            rows = slice(par * DK, (par + 1) * DK)
                            mm = pe.matmul(ps[:, 4 * r + 2 + par, j * P:(j + 1) * P], g.qkv[rows, 4 + j, tc],
                                           kbT[rows, r, j, :], start=True, stop=True)
                        mm.then_inc(pe_done, PE.step("KK", t, r))
                        pe.wait_ge(dve_done, V[("D", t, r)])
                        for s, h, par, j in slots:
                            rows = slice(par * DK, (par + 1) * DK)
                            mm = pe.matmul(ps[:, 4 * r + par, j * P:(j + 1) * P], g.qkv[rows, 4 + j, tc],
                                           g.qkv[rows, j, tc], start=True, stop=True)
                        mm.then_inc(pe_done, PE.step("QK", t, r))
                    for r in DIRS:
                        pe.wait_ge(dve_done, V[("aT", t, r)])
                        for s, h, par, j in slots:
                            mm = pe.transpose(ps[:, 4 * r + par, j * P:(j + 1) * P], LT[:, r, s, :], c["ident"])
                        mm.then_inc(pe_done, PE.step("L", t, r))
                    for lv in LEVELS[1:]:
                        for r in DIRS:
                            if lv == 2:
                                pe.wait_ge(pool_done, G[("X1", t, r)])
                                pe.wait_ge(dve_done, V[("YI", t, r)])
                            else:
                                pe.wait_ge(dve_done, V[("Y", t, r, lv // 2)])
                            for s, h, par, j in slots:
                                mm = pe.matmul(ps[:, 4 * r + par, j * P:(j + 1) * P], LT[:, r, s, :], X[:, r, s, :],
                                               start=True, stop=True)
                            mm.then_inc(pe_done, PE.step("P", t, r, lv))
                        for r in DIRS:
                            pe.wait_ge(dve_done, V[("P", t, r, lv)])
                            if lv != LAST:
                                for s, h, par, j in slots:
                                    mm = pe.matmul(ps[:, 4 * r + 2 + par, j * P:(j + 1) * P], Y[:, r, s, :],
                                                   PR[:, r, s, :], start=True, stop=True)
                                mm.then_inc(pe_done, PE.step("X", t, r, lv))
                            for s, h, par, j in slots:
                                mm = pe.matmul(ps[:, 4 * r + par, j * P:(j + 1) * P], PR[:, r, s, :], Y[:, r, s, :],
                                               start=True, stop=True)
                            mm.then_inc(pe_done, PE.step("Y", t, r, lv))
                    for r in DIRS:
                        pe.wait_ge(dve_done, V[("Y", t, r, LAST)])
                        pe.wait_ge(pool_done, G[("vb", t, r)])
                        for s, h, par, j in slots:
                            mm = pe.matmul(ps[:, 4 * r + 2, s * DV:(s + 1) * DV], Y[:, r, s, :],
                                           vb[:, r, h * DV:(h + 1) * DV], start=True, stop=True)
                        mm.then_inc(pe_done, PE.step("u", t, r))
                        for s, h, par, j in slots:
                            mm = pe.matmul(ps[par * DK:(par + 1) * DK, 4 * r + 3, j * P:(j + 1) * P],
                                           kbg[:, r, h * DK:(h + 1) * DK], Y[:, r, s, :], start=True, stop=True)
                        mm.then_inc(pe_done, PE.step("wT", t, r))
                    for sc in scan_after(t):
                        grp, n, r = sc
                        st, half = where(*sc)
                        d, lo = STORE[st], half * CHUNK
                        rr = slice(lo, lo + CHUNK)
                        if n == 0:
                            pe.wait_ge(act_done, A[("wT", t, r)])
                            pe.wait_ge(dve_done, V[("u", t, r)])
                            if grp == 0:
                                pe.wait_ge(pool_done, G["state0"])
                            else:
                                pe.wait_ge(s_state, 64)
                        else:
                            pe.wait_ge(dve_done, V[("o2", (grp, n - 1, r))])
                        for s, h, par, j in slots:
                            rows = slice(par * DK, (par + 1) * DK)
                            pe.matmul(ps[rr, 4 * r + par, j * DV:(j + 1) * DV], wT[rows, d, r, j, rr], S[rows, r, j, :],
                                      start=True, stop=True)
                            mm = pe.matmul(ps[rr, 4 * r + par, (H2 + j) * DV:(H2 + j + 1) * DV],
                                           g.qkv[rows, j, tok_at(st) + lo:tok_at(st) + lo + CHUNK], S[rows, r, j, :],
                                           start=True, stop=True)
                        mm.then_inc(pe_done, PE.step("RQ", sc))
                        pe.wait_ge(dve_done, V[("vn", sc)])
                        pe.wait_ge(pool_done, G[("kd", st, r)])
                        for s, h, par, j in slots:
                            pe.matmul(ps[par * DK:(par + 1) * DK, 4 * r + 3, j * DV:(j + 1) * DV],
                                      kd[rr, d, r, h * DK:(h + 1) * DK], vn[rr, r, s, :], start=True, stop=True)
                        for s, h, par, j in slots:
                            mm = pe.matmul(ps[rr, 4 * r + 2, s * DV:(s + 1) * DV], aT[rr, d, r, s, rr], vn[rr, r, s, :],
                                           start=True, stop=True)
                        mm.then_inc(pe_done, PE.step("OU", sc))

            @block.vector
            def _(dve):
                dve.wait_ge(pe_done, PE[("norm", "k")])
                dve.tensor_scalar(norms[:, 0].rearrange("p i t h -> p (i t h)"), ps[:, 7, 0:N48], EPS, None, ALU.add) \
                    .then_inc(dve_done, V.step("neps"))
                dve.wait_ge(dve_done, V["neps"])
                dve.reciprocal(norms[:, 1], norms[:, 0]).then_inc(dve_done, V.step("nrec"))
                for i, n in enumerate("qk"):
                    dve.wait_ge(act_done, A[("root", n)])
                    dve.tensor_copy(spread[i], over(norms[:, 2, i], DK, 3)).then_inc(dve_done, V.step("expand", n))
                for i, n in enumerate("qk"):
                    dve.wait_ge(pe_done, PE[("spread", n)])
                    for cols in (slice(0, P), slice(tok_at(1), OUTW)):
                        x = g.qkv[:, 4 * i:4 * i + 4, cols]
                        ins = dve.tensor_tensor(x, x, ps[:, 4 * i:4 * i + 4, cols], ALU.mult)
                    ins.then_inc(dve_done, V.step("normed", n))
                dve.wait_ge(s_row, 48)
                dve.tensor_tensor(gw[:, 0], g.small[:, :, 32:48], over(arow[:, 1, :], TILES, 1), ALU.add) \
                    .then_inc(dve_done, V.step("xa"))
                dve.wait_ge(dve_done, V["xa"])
                dve.scalar_tensor_tensor(out=gw[:, 1], in0=gw[:, 0], scalar=-1.0, in1=gw[:, 0], op0=ALU.mult,
                                         op1=ALU.min).then_inc(dve_done, V.step("na"))
                dve.wait_ge(act_done, A["expb"])
                dve.scalar_tensor_tensor(out=gw[:, 2], in0=gw[:, 0], scalar=0.0, in1=gw[:, 2], op0=ALU.max,
                                         op1=ALU.add).then_inc(dve_done, V.step("sp"))
                dve.wait_ge(dve_done, V["sp"])
                dve.scalar_tensor_tensor(out=gg[:].rearrange("p t r h -> p t (r h)"), in0=gw[:, 2], scalar=-1.0,
                                         in1=over(arow[:, 0, :], TILES, 1), op0=ALU.mult, op1=ALU.mult) \
                    .then_inc(dve_done, V.step("gg"))
                dve.tensor_scalar(gw[:, 3], gw[:, 3], 1.0, None, ALU.add).then_inc(dve_done, V.step("b1"))
                dve.wait_ge(dve_done, V["b1"])
                dve.reciprocal(beta[:].rearrange("p t r h -> p t (r h)"), gw[:, 3]).then_inc(dve_done, V.step("beta"))
                dve.wait_ge(pe_done, PE["cums"])
                dve.tensor_copy(gc[:].rearrange("p n r t h -> p (n r t h)"), ps[:, 6, 0:4 * N48]) \
                    .then_inc(dve_done, V.step("gc"))
                dve.wait_ge(dve_done, V["gc"])
                dve.tensor_tensor(ex[:, 1], gc[:, 1], gc[:, 0], ALU.subtract).then_inc(dve_done, V.step("tdiff"))
                dve.wait_ge(act_done, A["ex"])
                for par in range(2):
                    rows = slice(par * DK, (par + 1) * DK)
                    i = dve.tensor_copy(glS[rows], ex[rows, 2:4, :, :, par::2].rearrange("p n r t j -> p n (r t) j"))
                i.then_inc(dve_done, V.step("glS"))
                for t in range(TILES):
                    d = STORE[t]
                    for r in DIRS:
                        if t == 0:
                            dve.wait_ge(act_done, A["ktok"])
                            dve.wait_ge(dve_done, V["glS"])
                        else:
                            dve.wait_ge(pool_done, G[("kbg", t - 1, r)])
                            dve.wait_ge(pe_done, PE[("wT", t - 1, 1)])
                            if t == 1:
                                dve.wait_ge(pe_done, PE[("OU", (0, 1, 1))])
                                dve.wait_ge(dve_done, V[("o2", (0, 1, 1))])
                        dve.tensor_tensor(heads(kb[:, r]), heads(ktok[:, t]), over(beta[:, t, r, :], DK, 2), ALU.mult) \
                            .then_inc(dve_done, V.step("kb", t, r))
                        for par in range(2):
                            i = dve.tensor_tensor(X[:, r, par * H2:(par + 1) * H2], over(c[f"incl{r}"], H2, 1),
                                                  over(gg[:, t, r, par::2], P, 2), ALU.mult)
                        i.then_inc(dve_done, V.step("gtri", t, r))
                    for r in DIRS:
                        dve.wait_ge(pe_done, PE[("D", t, r)])
                        for s, h, par, j in slots:
                            i = dve.tensor_scalar(PR[:, r, s, :], ps[:, 4 * r + par, j * P:(j + 1) * P],
                                                  gc[:, 0, r, t, h:h + 1], 0.0, ALU.subtract, ALU.min)
                        i.then_inc(dve_done, V.step("D", t, r))
                    for r in DIRS:
                        dve.wait_ge(act_done, A[("E", t, r)])
                        dve.tensor_tensor(Y[:, r], PR[:, r], over(c[f"strict{r}"], GH, 1), ALU.mult) \
                            .then_inc(dve_done, V.step("Es", t, r))
                    for r in DIRS:
                        dve.wait_ge(pe_done, PE[("KK", t, r)])
                        dve.wait_ge(dve_done, V[("Es", t, r)])
                        dve.tensor_tensor(LT[:, r], banks(4 * r + 2), Y[:, r], ALU.mult) \
                            .then_inc(dve_done, V.step("LT", t, r))
                        dve.wait_ge(pe_done, PE[("QK", t, r)])
                        dve.wait_ge(pool_done, G[("Ei", t, r)])
                        if t == 2:
                            dve.wait_ge(pe_done, PE[("OU", (0, 1, 1))])
                        dve.tensor_tensor(aT[:, d, r], banks(4 * r), X[:, r], ALU.mult) \
                            .then_inc(dve_done, V.step("aT", t, r))
                    for r in DIRS:
                        dve.wait_ge(pe_done, PE[("L", t, r)])
                        dve.wait_ge(dve_done, V[("aT", t, r)])
                        dve.scalar_tensor_tensor(out=X[:, r], in0=banks(4 * r), scalar=-1.0,
                                                 in1=over(c[f"level{r}_1"], GH, 1), op0=ALU.mult, op1=ALU.mult) \
                            .then_inc(dve_done, V.step("X1", t, r))
                    for r in DIRS:
                        dve.scalar_tensor_tensor(out=Y[:, r], in0=LT[:, r], scalar=-1.0,
                                                 in1=over(c[f"level{1 - r}_1"], GH, 1), op0=ALU.mult, op1=ALU.mult) \
                            .then_inc(dve_done, V.step("Y1", t, r))
                        dve.wait_ge(dve_done, V[("Y1", t, r)])
                        dve.tensor_tensor(Y[:, r], Y[:, r], over(c["ident"], GH, 1), ALU.add) \
                            .then_inc(dve_done, V.step("YI", t, r))
                    for lv in LEVELS[1:]:
                        for r in DIRS:
                            dve.wait_ge(pe_done, PE[("P", t, r, lv)])
                            dve.tensor_tensor(PR[:, r], banks(4 * r), over(c[f"level{r}_{lv}"], GH, 1), ALU.mult) \
                                .then_inc(dve_done, V.step("P", t, r, lv))
                        for r in DIRS:
                            if lv != LAST:
                                dve.wait_ge(pe_done, PE[("Y", t, r, lv)])
                                dve.tensor_tensor(X[:, r], X[:, r], banks(4 * r + 2), ALU.subtract) \
                                    .then_inc(dve_done, V.step("X", t, r, lv))
                            dve.wait_ge(pe_done, PE[("Y", t, r, lv)])
                            dve.tensor_tensor(Y[:, r], Y[:, r], banks(4 * r), ALU.subtract) \
                                .then_inc(dve_done, V.step("Y", t, r, lv))
                    for r in DIRS:
                        dve.wait_ge(pe_done, PE[("u", t, r)])
                        dve.tensor_copy(u[:, d, r].rearrange("p s e -> p (s e)"), ps[:, 4 * r + 2, :]) \
                            .then_inc(dve_done, V.step("u", t, r))
                    for sc in scan_after(t):
                        grp, n, r = sc
                        st, half = where(*sc)
                        sd, rr = STORE[st], slice(half * CHUNK, (half + 1) * CHUNK)
                        pair = lambda lo: ps[rr, 4 * r:4 * r + 2, lo:lo + H2 * DV].rearrange(
                            "p b (j e) -> p b j e", j=H2)
                        sl = lambda x: x.rearrange("p (q j) e -> p q j e", q=2)
                        dve.wait_ge(pe_done, PE[("RQ", sc)])
                        dve.tensor_tensor(sl(vn[rr, r]), sl(u[rr, sd, r]), pair(0), ALU.subtract) \
                            .then_inc(dve_done, V.step("vn", sc))
                        for par in range(2):
                            i = dve.tensor_tensor(qs[rr, r, par * H2:(par + 1) * H2],
                                                  ps[rr, 4 * r + par, H2 * DV:2 * H2 * DV].rearrange(
                                                      "p (j e) -> p j e", j=H2),
                                                  over(ex[rr, 0, r, st, par::2], DV, 2), ALU.mult)
                        i.then_inc(dve_done, V.step("qs", sc))
                        dve.tensor_tensor(S[:, r], S[:, r], over(glS[:, half, r * TILES + st, :], DV, 2), ALU.mult) \
                            .then_inc(dve_done, V.step("Sg", sc))
                        dve.wait_ge(pe_done, PE[("OU", sc)])
                        dve.wait_ge(dve_done, V[("Sg", sc)])
                        dve.tensor_tensor(S[:, r], S[:, r], ps[:, 4 * r + 3, 0:H2 * DV].rearrange(
                            "p (j e) -> p j e", j=H2), ALU.add).then_inc(dve_done, V.step("S", sc))
                        dve.wait_ge(pool_done, G["og0"])
                        dve.tensor_tensor(qs[rr, r], qs[rr, r], ps[rr, 4 * r + 2, :].rearrange(
                            "p (s e) -> p s e", s=GH), ALU.add).then_inc(dve_done, V.step("o1", sc))
                        dve.wait_ge(dve_done, V[("o1", sc)])
                        dve.tensor_tensor(og[rr, st], og[rr, st], qs[rr, r], ALU.add) \
                            .then_inc(dve_done, V.step("o2", sc))
                flat = og.rearrange("p t s e -> p (t s) e")
                dve.wait_ge(act_done, A["osq"])
                dve.tensor_reduce(ostat[:, 0], sq_out.rearrange("p t s e -> p (t s) e"), AX, ALU.add) \
                    .then_inc(dve_done, V.step("oss"))
                dve.wait_ge(dve_done, V["oss"])
                dve.tensor_scalar(ostat[:, 1], ostat[:, 0], 1.0 / DV, EPS, ALU.mult, ALU.add) \
                    .then_inc(dve_done, V.step("oms"))
                dve.wait_ge(dve_done, V["oms"])
                dve.reciprocal(ostat[:, 2], ostat[:, 1]).then_inc(dve_done, V.step("orec"))
                dve.wait_ge(act_done, A["ors"])
                dve.tensor_tensor(flat, flat, over(ostat[:, 3], DV, 2), ALU.mult).then_inc(dve_done, V.step("on"))
                dve.wait_ge(dve_done, V["on"])
                dve.wait_ge(pool_done, G["zg"])
                for t in range(TILES):
                    zt = g.z[:, t].rearrange("p (j q e) -> p q j e", j=H2, q=2)
                    i = dve.tensor_tensor(zt, zt, og[:, t].rearrange("p (q j) e -> p q j e", q=2), ALU.mult)
                i.then_inc(dve_done, V.step("out"))


def phase_merge(nc, g):
    a, ps, c = g.a, g.ps, g.c
    KO = GW // P
    T = range(TILES)
    F32R = mybir.dt.float32r
    with ExitStack() as ctx:
        def sb(name, shape, dt=F32):
            return ctx.enter_context(nc.sbuf_tensor(name, shape, dt))
        w = Pieces(nc, ctx, g, "merge", LOAD["ga0"], 4)
        ahead = run_ahead(len(MERGE_LOADS) - 1, w.depth)
        h_hi = sb("h_hi", [P, KD, TOK], F32R)
        h_lo = sb("h_lo", [P, KD, TOK], F32R)
        hs = (h_hi, h_lo)
        oT = sb("oT", [P, 2, 2, KO, TOK], F32R)
        sgb = sb("sgb", [P, TILES, 512])
        merged = sb("merged", [P, TILES, D])
        gate = sb("gate", [P, 2, D])
        stat = sb("mstat", [P, TILES, 6])
        s_x, s_row = (g.sem(n) for n in ("x_again_loaded", "gate1_loaded"))
        pe_done, dve_done, act_done = (g.sem("merge_" + n) for n in ("pe", "dve", "act"))
        half = lambda n: slice(n * 512, (n + 1) * 512)
        tile = lambda t: slice(t * P, (t + 1) * P)
        units = [(x, n, t) for n in range(2) for x, t in
                 [("ga", t) for t in T] + [("gb", t) for t in T] + [(y, t) for t in T for y in "AB"]]
        bank = {u: i % 8 for i, u in enumerate(units)}
        o_bank = {(0, 0): 6, (0, 1): 7, (0, 2): 0, (1, 0): 1, (1, 1): 2, (1, 2): 3}
        for (n, t), b in o_bank.items():
            bank[("o", n, t)] = b
        load_of = lambda x, n: LOAD[f"{x}{n}"] if x in ("ga", "gb") else LOAD[("wo" if x == "o" else "ab", n)]
        closing = lambda x, t: t == TILES - 1
        oT_bank = {(0, t): 5 + t for t in T} | {(1, t): t for t in T}
        turns_of = lambda v: [("oT", v, t) for t in T]
        open_units = [u for u in units[:-2] if not closing(u[0], u[2])]
        pe_o = open_units[:2] + turns_of(0) + open_units[2:4] + turns_of(1) + open_units[4:]
        pe_o += [("mT", 0), ("mT", 1), ("o", 0, 0),
                 ("mT", 2), ("o", 0, 1), ("o", 1, 0), ("o", 1, 1)]
        PE = Count(pe_o)
        A = Count([("h_hi", t) for t in T] + [("ga", 0, t) for t in T] + turns_of(0) + [("gb", 0, t) for t in T]
                  + turns_of(1) + [(x, 1, t) for x in ("ga", "gb") for t in T]
                  + [("mT", 0), ("mT", 1), ("ss", 0, 0), ("mT", 2), ("ss", 0, 1), ("ss", 0, 2)]
                  + [y for t in T for y in [("ss", 1, t), ("rs", t)] + [("ss2", t - 1)] * (t > 0)] + [("ss2", 2)])
        V = Count([("h_lo", t) for t in T] + turns_of(0) + turns_of(1)
                  + [(x, 0, t) for t in T for x in ("A", "B", "sum")]
                  + [(x, 1, 0) for x in ("A", "B", "sum")] + [(x, 1, 1) for x in ("A", "B", "sum")]
                  + [("mT", 0)] + [(x, 1, 2) for x in ("A", "B", "sum")] + [("mT", 1), ("mT", 2)]
                  + [(x, t) for t in T for x in ("sq", "ms", "rec", "yn0", "yn1", "x1")])

        def wait_unit(eng, x, n, t):
            if closing(x, t):
                eng.wait_ge(w.used, w.number(load_of(x, n), NPIECE // 2 if x == "A" else NPIECE))
            else:
                eng.wait_ge(pe_done, PE[(x, n, t)])

        def read_out(eng, u):
            if u[0] in ("ga", "gb"):
                eng.wait_ge(act_done, A[u])
            else:
                eng.wait_ge(dve_done, V[u])

        with nc.Block() as block:
            @block.sync
            def _(sp):
                for v in range(2):
                    sp.dma_start(gate[:, v], g.mods_dram[v, 2].partition_broadcast(P)).then_inc(s_row, 16)
                sp.dma_start(g.x1[:, 0, :], a["x_prompt"][0]).then_inc(s_x, 16)
                sp.dma_start(g.x1[:, 1:3, :], a["x_sample"][0].rearrange("(t p) d -> p t d", p=P)).then_inc(s_x, 16)
                for name in MERGE_LOADS[RING:]:
                    n = LOAD[name]
                    sp.wait_ge(w.lo_made, w.split_up(n - RING))
                    load_slot(g, sp, n)
                sp.wait_ge(w.lo_made, w.split_up(LOAD[("ab", 1)]))
                for m, name in enumerate(("ws_gate", "ws_up")):
                    sp.dma_start(g.wsg[:, m], a[name][0].rearrange("(p k) n -> p k n", k=KD)).then_inc(g.s_ws, 16)
                sp.wait_ge(w.lo_made, w.split_up(LOAD[("wo", 0)]))
                sp.dma_start(g.wsd, a["ws_down"][0].rearrange("(p k) n -> p k n", k=KF)).then_inc(g.s_ws, 16)
                sp.wait_ge(w.lo_made, w.split_up(LOAD[("wo", 1)]))
                for v in range(2):
                    for m in range(2):
                        sp.dma_start(g.rows[:, v, m], g.mods_dram[v, 3 + m].partition_broadcast(P)).then_inc(g.s_rows, 16)

            @block.scalar
            def _(act):
                def splits(load):
                    for n, i in ahead[load - w.base + 1]:
                        w.make_hi(act, w.base + n, i)

                def turned(t):
                    act.wait_ge(pe_done, PE[("mT", t)])
                    act.activation(h_hi[:, :, tile(t)],
                                   ps[:, 2 * t:2 * t + 2, :].rearrange("p b (k n) -> p (b k) n", k=4), ACT.Copy) \
                        .then_inc(act_done, A.step("mT", t))

                def squares(n, t):
                    wait_unit(act, "o", n, t)
                    act.activation(merged[:, t, half(n)], ps[:, bank[("o", n, t)], :], ACT.Square,
                                   accum_out=stat[:, t, n:n + 1]).then_inc(act_done, A.step("ss", n, t))

                def squares2(t):
                    act.wait_ge(dve_done, V[("x1", t)])
                    act.activation(merged[:, t, :], g.x1[:, t, :], ACT.Square, accum_out=g.ss2[:, t:t + 1]) \
                        .then_inc(act_done, A.step("ss2", t))

                for t in T:
                    act.activation(h_hi[:, :, tile(t)], g.hT[:, :, tile(t)], ACT.Copy) \
                        .then_inc(act_done, A.step("h_hi", t))
                    for n, i in ahead[0][2 * t:2 * t + 2]:
                        w.make_hi(act, w.base + n, i)
                for n in range(2):
                    for x in ("ga", "gb"):
                        for t in T:
                            if t == TILES - 1:
                                splits(load_of(x, n))
                            wait_unit(act, x, n, t)
                            if x == "gb" and n:
                                act.wait_ge(dve_done, V[("sum", 0, t)])
                            act.activation(merged[:, t, half(n)] if x == "ga" else sgb[:, t], ps[:, bank[(x, n, t)], :],
                                           ACT.Sigmoid).then_inc(act_done, A.step(x, n, t))
                        if n == 0:
                            v = ("ga", "gb").index(x)
                            for t in T:
                                act.wait_ge(pe_done, PE[("oT", v, t)])
                                act.activation(oT[:, 0, v, :, tile(t)],
                                               ps[:, oT_bank[(v, t)], :].rearrange("p (k n) -> p k n", k=KO),
                                               ACT.Copy).then_inc(act_done, A.step("oT", v, t))
                    if n == 0:
                        splits(load_of("A", n))
                turned(0)
                splits(load_of("A", 1))
                turned(1)
                squares(0, 0)
                turned(2)
                squares(0, 1)
                splits(load_of("o", 0))
                squares(0, 2)
                for t in T:
                    squares(1, t)
                    act.wait_ge(dve_done, V[("rec", t)])
                    act.activation(stat[:, t, 5:6], stat[:, t, 4:5], ACT.Sqrt).then_inc(act_done, A.step("rs", t))
                    if t:
                        squares2(t - 1)
                squares2(TILES - 1)

            @block.tensor
            def _(pe):
                def turn_outputs(v):
                    for t in T:
                        if v:
                            pe.wait_ge(act_done, A[("ga", 0, t)])
                        for k in range(KO):
                            mm = pe.transpose(ps[:, oT_bank[(v, t)], k * P:(k + 1) * P],
                                              (g.omla, g.z)[v][:, t, k::KO], c["ident"])
                        mm.then_inc(pe_done, PE.step("oT", v, t))

                def product(x, n, t):
                    load = load_of(x, n)
                    those = {"A": range(0, NPIECE // 2), "B": range(NPIECE // 2, NPIECE)}.get(x, range(NPIECE))
                    for p in those:
                        at = w.number(load, p)
                        if t == 0:
                            pe.wait_ge(w.hi_made, at + 1)
                            pe.wait_ge(w.lo_made, at + 1)
                        for k in range(KP):
                            kk = p * KP + k
                            for y, z in PASSES:
                                if x in ("A", "B"):
                                    left = oT[:, y, "AB".index(x), kk % KO, tile(t)]
                                else:
                                    left = hs[y][:, kk, tile(t)]
                                mm = pe.matmul(ps[:, bank[(x, n, t)], :], left, (w.hi, w.lo)[z][:, at % w.depth, k, :],
                                               start=(p == those[0] and k == 0 and (y, z) == PASSES[0]),
                                               stop=(p == those[-1] and k == KP - 1 and (y, z) == PASSES[-1]))
                        if closing(x, t):
                            mm.then_inc(w.used, 1)
                    if not closing(x, t):
                        mm.then_inc(pe_done, PE.step(x, n, t))

                def turn(t):
                    pe.wait_ge(dve_done, V[("sum", 1, t)])
                    for k in range(KD):
                        mm = pe.transpose(ps[:, 2 * t + k // 4, (k % 4) * P:(k % 4 + 1) * P], merged[:, t, k::KD],
                                          c["ident"])
                    mm.then_inc(pe_done, PE.step("mT", t))

                def turned_back(t):
                    pe.wait_ge(act_done, A[("mT", t)])
                    pe.wait_ge(dve_done, V[("mT", t)])

                for i, (x, n, t) in enumerate(units[:-2]):
                    if i >= 8:
                        read_out(pe, units[i - 8])
                    if i < TILES:
                        pe.wait_ge(dve_done, V[("h_lo", t)])
                    if i == 5:
                        pe.wait_ge(dve_done, V[("oT", 0, 0)])
                    if i == 6:
                        pe.wait_ge(dve_done, V[("oT", 1, TILES - 1)])
                    product(x, n, t)
                    if (x, n, t) == ("ga", 0, TILES - 1):
                        turn_outputs(0)
                    if (x, n, t) == ("gb", 0, TILES - 1):
                        turn_outputs(1)
                read_out(pe, ("gb", 1, 2))
                turn(0)
                for i in (len(units) - 2, len(units) - 1):
                    read_out(pe, units[i - 8])
                    product(*units[i])
                turn(1)
                turned_back(0)
                read_out(pe, ("A", 1, 2))
                product("o", 0, 0)
                turn(2)
                turned_back(1)
                product("o", 0, 1)
                turned_back(2)
                product("o", 0, 2)
                for t in T:
                    product("o", 1, t)

            @block.vector
            def _(dve):
                def splits(load):
                    for n, i in ahead[load - w.base + 1]:
                        w.make_lo(dve, w.base + n, i)

                for t in T:
                    dve.wait_ge(act_done, A[("h_hi", t)])
                    dve.tensor_tensor(hs[1][:, :, tile(t)], g.hT[:, :, tile(t)], h_hi[:, :, tile(t)].bitcast(F32),
                                      ALU.subtract).then_inc(dve_done, V.step("h_lo", t))
                    for n, i in ahead[0][2 * t:2 * t + 2]:
                        w.make_lo(dve, w.base + n, i)

                def outputs_lo(v):
                    for t in T:
                        dve.wait_ge(act_done, A[("oT", v, t)])
                        dve.tensor_tensor(oT[:, 1, v, :, tile(t)],
                                          ps[:, oT_bank[(v, t)], :].rearrange("p (k n) -> p k n", k=KO),
                                          oT[:, 0, v, :, tile(t)].bitcast(F32), ALU.subtract) \
                            .then_inc(dve_done, V.step("oT", v, t))

                def gated(n, t):
                    m, s = merged[:, t, half(n)], sgb[:, t]
                    wait_unit(dve, "A", n, t)
                    dve.wait_ge(act_done, A[("ga", n, t)])
                    dve.tensor_tensor(m, m, ps[:, bank[("A", n, t)], :], ALU.mult).then_inc(dve_done, V.step("A", n, t))
                    wait_unit(dve, "B", n, t)
                    dve.wait_ge(act_done, A[("gb", n, t)])
                    dve.tensor_tensor(s, s, ps[:, bank[("B", n, t)], :], ALU.mult).then_inc(dve_done, V.step("B", n, t))
                    dve.wait_ge(dve_done, V[("B", n, t)])
                    dve.tensor_tensor(m, m, s, ALU.add).then_inc(dve_done, V.step("sum", n, t))

                def turned(t):
                    dve.wait_ge(act_done, A[("mT", t)])
                    dve.tensor_tensor(hs[1][:, :, tile(t)],
                                      ps[:, 2 * t:2 * t + 2, :].rearrange("p b (k n) -> p (b k) n", k=4),
                                      h_hi[:, :, tile(t)].bitcast(F32), ALU.subtract).then_inc(dve_done, V.step("mT", t))

                for v, x in enumerate(("ga", "gb")):
                    splits(load_of(x, 0))
                    outputs_lo(v)
                gated(0, 0)
                gated(0, 1)
                splits(load_of("A", 0))
                gated(0, 2)
                for x in ("ga", "gb"):
                    splits(load_of(x, 1))
                gated(1, 0)
                gated(1, 1)
                turned(0)
                splits(load_of("A", 1))
                gated(1, 2)
                turned(1)
                turned(2)
                splits(load_of("o", 0))
                dve.wait_ge(s_row, 32)
                dve.wait_ge(s_x, 32)
                for t in T:
                    col = lambda i: stat[:, t, i:i + 1]
                    dve.wait_ge(act_done, A[("ss", 1, t)])
                    dve.tensor_tensor(col(2), col(0), col(1), ALU.add).then_inc(dve_done, V.step("sq", t))
                    dve.wait_ge(dve_done, V[("sq", t)])
                    dve.tensor_scalar(col(3), col(2), 1.0 / D, EPS, ALU.mult, ALU.add).then_inc(dve_done, V.step("ms", t))
                    dve.wait_ge(dve_done, V[("ms", t)])
                    dve.reciprocal(col(4), col(3)).then_inc(dve_done, V.step("rec", t))
                    dve.wait_ge(act_done, A[("rs", t)])
                    for n in range(2):
                        dve.scalar_tensor_tensor(out=merged[:, t, half(n)], in0=ps[:, bank[("o", n, t)], :],
                                                 scalar=col(5), in1=gate[:, min(t, 1), half(n)], op0=ALU.mult,
                                                 op1=ALU.mult).then_inc(dve_done, V.step(f"yn{n}", t))
                    dve.wait_ge(dve_done, V[("yn1", t)])
                    dve.tensor_tensor(g.x1[:, t, :], g.x1[:, t, :], merged[:, t, :], ALU.add) \
                        .then_inc(dve_done, V.step("x1", t))


def phase_route(nc, g):
    a, ps, c = g.a, g.ps, g.c
    E = EXPERTS
    with ExitStack() as ctx:
        def sb(name, shape, dt=F32):
            return ctx.enter_context(nc.sbuf_tensor(name, shape, dt))
        rows, wsg, wsd = g.rows, g.wsg, g.wsd
        wr = sb("wr", [P, KD, E])
        ebias = sb("ebias", [P, E])
        stat = sb("rstat", [P, 4, TILES])
        s = sb("score", [P, TILES, E])
        sel = sb("sel", [P, TILES, E])
        m8 = sb("m8", [P, TILES, GROUPS, 8])
        grp = sb("grp", [P, TILES, GROUPS])
        cmp = sb("cmp", [P, 2, TILES, GROUPS * GROUPS])
        rank = sb("rank", [P, 3, TILES, GROUPS])
        top = sb("top", [P, TILES, 8])
        rep = sb("rep", [P, TILES, E])
        gates = sb("gates", [P, TILES, E])
        gsum = sb("gsum", [P, 2, TILES])
        pmax = sb("pmax", [P, 1])
        nf = sb("nf", [1, 4])
        sact = sb("sact", [P, 2, FE])
        sactT = sb("sactT", [P, 2, KF, P])
        s_row, s_wr, s_ws = g.s_rows, g.sem("router_loaded"), g.s_ws
        pe_done, dve_done, act_done, pool_done = (g.sem("route_" + n) for n in ("pe", "dve", "act", "pool"))
        T = range(TILES)
        PE = Count([("hT", t) for t in T] + [("logit", t) for t in T] + [("gu", 0), ("gu", 1), ("pos", 0), ("pos", 1),
                   ("pos", 2), "pmaxT", ("actT", 0), ("actT", 1), ("gu", 2), ("y", 0), ("y", 1), ("actT", 2), ("y", 2)])
        A = Count(["rs"] + [("hT", t) for t in T] + ["sig"] + [("h2_hi", t) for t in T]
                  + [("silu", 0), ("silu", 1), ("actT", 0), ("actT", 1), ("silu", 2), ("y", 0), ("y", 1), ("actT", 2),
                     ("y", 2)])
        V = Count(["ms", "rec"] + [x for t in T for x in (("h0", t), ("h", t))]
                  + ["sel", "m8", "grp", "gt", "eq", "eqe", "cmp", "rank", "gm", "pen", "selm0", "selm", "top",
                     "rep", "mask", "gs", "gsum", "grec", "gates", "gate_hi", "gate_lo", ("h2_lo", 0), ("h2_lo", 1), ("h2_lo", 2), ("act", 0),
                     ("act", 1), "pos", "pmax", "nmax", "n1", "n2", "n3",
                     ("act", 2)])
        with nc.Block() as block:
            @block.sync
            def _(sp):
                sp.dma_start(wr[:], a["w_router"][0].rearrange("(p k) n -> p k n", k=KD)).then_inc(s_wr, 16)
                sp.dma_start(ebias[:], a["e_bias"][0].partition_broadcast(P)).then_inc(s_wr, 16)
                sp.wait_ge(dve_done, V[("h", TILES - 1)])
                load_expert_half(g, sp, 0, 0, 0)
                load_expert_half(g, sp, 0, 0, 1)

            @block.scalar
            def _(act):
                act.wait_ge(dve_done, V["rec"])
                act.activation(stat[:, 3], stat[:, 2], ACT.Sqrt).then_inc(act_done, A.step("rs"))
                for t in T:
                    act.wait_ge(pe_done, PE[("hT", t)])
                    act.activation(g.hT[:, :, t * P:(t + 1) * P],
                                   ps[:, 2 * t:2 * t + 2, :].rearrange("p b (k n) -> p (b k) n", k=4), ACT.Copy) \
                        .then_inc(act_done, A.step("hT", t))
                act.wait_ge(pe_done, PE[("logit", 2)])
                act.activation(s[:].rearrange("p t e -> p (t e)"), ps[:, 6, 0:TILES * E], ACT.Sigmoid) \
                    .then_inc(act_done, A.step("sig"))
                for t in T:
                    act.activation(g.h2s[:, 0, t, :], g.h2[:, t, :], ACT.Copy).then_inc(act_done, A.step("h2_hi", t))

                def silu(t):
                    act.wait_ge(pe_done, PE[("gu", t)])
                    if t == 2:
                        act.wait_ge(pe_done, PE[("actT", 0)])
                    act.activation(sact[:, t % 2], ps[:, t % 2, 0:FE], ACT.Silu).then_inc(act_done, A.step("silu", t))

                def turned(t):
                    act.wait_ge(pe_done, PE[("actT", t)])
                    act.activation(sactT[:, t % 2].rearrange("p j n -> p (j n)"), ps[:, 3 - t % 2, 0:KF * P], ACT.Copy) \
                        .then_inc(act_done, A.step("actT", t))

                def take_y(t):
                    b = 4 + 2 * (t % 2)
                    act.wait_ge(pe_done, PE[("y", t)])
                    act.activation(g.y[:, t, :].rearrange("p (b n) -> p b n", b=2), ps[:, b:b + 2, :], ACT.Copy) \
                        .then_inc(act_done, A.step("y", t))

                silu(0)
                silu(1)
                turned(0)
                turned(1)
                silu(2)
                take_y(0)
                take_y(1)
                turned(2)
                take_y(2)

            @block.tensor
            def _(pe):
                for t in T:
                    pe.wait_ge(dve_done, V[("h", t)])
                    for k in range(KD):
                        mm = pe.transpose(ps[:, 2 * t + k // 4, (k % 4) * P:(k % 4 + 1) * P], g.h2[:, t, k::KD],
                                          c["ident"])
                    mm.then_inc(pe_done, PE.step("hT", t))
                pe.wait_ge(s_wr, 32)
                for t in T:
                    pe.wait_ge(act_done, A[("hT", t)])
                    for k in range(KD):
                        mm = pe.matmul(ps[:, 6, t * E:(t + 1) * E], g.hT[:, k, t * P:(t + 1) * P], wr[:, k, :],
                                       start=(k == 0), stop=(k == KD - 1))
                    mm.then_inc(pe_done, PE.step("logit", t))
                pe.wait_ge(s_ws, 48)

                def gate_up(t):
                    for k in range(KD):
                        mm = pe.matmul(ps[:, t % 2, :], g.hT[:, k, t * P:(t + 1) * P], wsg[:, :, k, :],
                                       start=(k == 0), stop=(k == KD - 1))
                    mm.then_inc(pe_done, PE.step("gu", t))

                def turn(t):
                    pe.wait_ge(dve_done, V[("act", t)])
                    if t == 1:
                        pe.wait_ge(dve_done, V["nmax"])
                    if t == 2:
                        pe.wait_ge(act_done, A[("actT", 0)])
                    for j in range(KF):
                        mm = pe.transpose(ps[:, 3 - t % 2, j * P:(j + 1) * P], sact[:, t % 2, j::KF], c["ident"])
                    mm.then_inc(pe_done, PE.step("actT", t))

                def down(t):
                    pe.wait_ge(act_done, A[("actT", t)])
                    if t == 2:
                        pe.wait_ge(act_done, A[("y", 0)])
                    for n in range(2):
                        for j in range(KF):
                            mm = pe.matmul(ps[:, 4 + 2 * (t % 2) + n, :], sactT[:, t % 2, j, :],
                                           wsd[:, j, n * 512:(n + 1) * 512], start=(j == 0), stop=(j == KF - 1))
                    mm.then_inc(pe_done, PE.step("y", t))

                gate_up(0)
                gate_up(1)
                pe.wait_ge(dve_done, V["mask"])
                for t in T:
                    for q in range(t + 1):
                        mm = pe.matmul(ps[:, 7, t * E:(t + 1) * E], c["before" if q == t else "ones"], rep[:, q, :],
                                       start=(q == 0), stop=(q == t))
                    mm.then_inc(pe_done, PE.step("pos", t))
                pe.wait_ge(dve_done, V["pmax"])
                pe.transpose(ps[0:1, 2, 0:P], pmax[:], c["ident"]).then_inc(pe_done, PE.step("pmaxT"))
                turn(0)
                turn(1)
                gate_up(2)
                down(0)
                down(1)
                turn(2)
                down(2)

            @block.vector
            def _(dve):
                dve.tensor_scalar(stat[:, 1], g.ss2[:], 1.0 / D, EPS, ALU.mult, ALU.add).then_inc(dve_done, V.step("ms"))
                dve.wait_ge(dve_done, V["ms"])
                dve.reciprocal(stat[:, 2], stat[:, 1]).then_inc(dve_done, V.step("rec"))
                dve.wait_ge(s_row, 64)
                dve.wait_ge(act_done, A["rs"])
                for t in T:
                    v = min(t, 1)
                    dve.scalar_tensor_tensor(out=g.h2[:, t, :], in0=g.x1[:, t, :], scalar=stat[:, 3, t:t + 1],
                                             in1=rows[:, v, 1, :], op0=ALU.mult, op1=ALU.mult) \
                        .then_inc(dve_done, V.step("h0", t))
                    dve.wait_ge(dve_done, V[("h0", t)])
                    dve.tensor_tensor(g.h2[:, t, :], g.h2[:, t, :], rows[:, v, 0, :], ALU.add) \
                        .then_inc(dve_done, V.step("h", t))
                dve.wait_ge(act_done, A["sig"])
                dve.tensor_tensor(sel[:], s[:], over(ebias[:], TILES, 1), ALU.add).then_inc(dve_done, V.step("sel"))
                dve.wait_ge(dve_done, V["sel"])
                for t in T:
                    for q in range(GROUPS):
                        i = dve.max(m8[:, t, q, :], sel[:, t, q * PER:(q + 1) * PER])
                i.then_inc(dve_done, V.step("m8"))
                dve.wait_ge(dve_done, V["m8"])
                dve.tensor_tensor(grp[:], m8[:, :, :, 0], m8[:, :, :, 1], ALU.add).then_inc(dve_done, V.step("grp"))
                dve.wait_ge(dve_done, V["grp"])
                sq = lambda x: x.rearrange("p t (i j) -> p t i j", i=GROUPS)
                dve.tensor_tensor(sq(cmp[:, 0]), over(grp[:], GROUPS, 2), over(grp[:], GROUPS, 3), ALU.is_gt) \
                    .then_inc(dve_done, V.step("gt"))
                dve.tensor_tensor(sq(cmp[:, 1]), over(grp[:], GROUPS, 2), over(grp[:], GROUPS, 3), ALU.is_equal) \
                    .then_inc(dve_done, V.step("eq"))
                dve.wait_ge(dve_done, V["eq"])
                dve.tensor_tensor(cmp[:, 1], cmp[:, 1], over(c["earlier"], TILES, 1), ALU.mult) \
                    .then_inc(dve_done, V.step("eqe"))
                dve.wait_ge(dve_done, V["eqe"])
                dve.tensor_tensor(cmp[:, 0], cmp[:, 0], cmp[:, 1], ALU.add).then_inc(dve_done, V.step("cmp"))
                dve.wait_ge(dve_done, V["cmp"])
                dve.tensor_reduce(rank[:, 0], sq(cmp[:, 0]), AX, ALU.add).then_inc(dve_done, V.step("rank"))
                dve.wait_ge(dve_done, V["rank"])
                dve.tensor_scalar(rank[:, 1], rank[:, 0], TOPG - 0.5, None, ALU.is_lt).then_inc(dve_done, V.step("gm"))
                dve.wait_ge(dve_done, V["gm"])
                dve.tensor_scalar(rank[:, 2], rank[:, 1], 1e30, -1e30, ALU.mult, ALU.add).then_inc(dve_done, V.step("pen"))
                per = lambda x: x.rearrange("p t (q e) -> p t q e", q=GROUPS)
                dve.tensor_tensor(per(sel[:]), per(sel[:]), over(rank[:, 1], PER, 3), ALU.mult) \
                    .then_inc(dve_done, V.step("selm0"))
                dve.wait_ge(dve_done, V["selm0"])
                dve.tensor_tensor(per(sel[:]), per(sel[:]), over(rank[:, 2], PER, 3), ALU.add) \
                    .then_inc(dve_done, V.step("selm"))
                dve.wait_ge(dve_done, V["selm"])
                for t in T:
                    i = dve.max(top[:, t, :], sel[:, t, :])
                i.then_inc(dve_done, V.step("top"))
                dve.wait_ge(dve_done, V["top"])
                for t in T:
                    i = dve.match_replace(rep[:, t, :], top[:, t, :], sel[:, t, :], -3e38)
                i.then_inc(dve_done, V.step("rep"))
                dve.wait_ge(dve_done, V["rep"])
                dve.tensor_tensor(rep[:], rep[:], sel[:], ALU.not_equal).then_inc(dve_done, V.step("mask"))
                dve.wait_ge(dve_done, V["mask"])
                dve.tensor_tensor(s[:], s[:], rep[:], ALU.mult).then_inc(dve_done, V.step("gs"))
                dve.wait_ge(dve_done, V["gs"])
                dve.tensor_reduce(gsum[:, 0], s[:], AX, ALU.add).then_inc(dve_done, V.step("gsum"))
                dve.wait_ge(dve_done, V["gsum"])
                dve.reciprocal(gsum[:, 1], gsum[:, 0]).then_inc(dve_done, V.step("grec"))
                dve.wait_ge(dve_done, V["grec"])
                for t in T:
                    i = dve.tensor_scalar(gates[:, t, :], s[:, t, :], gsum[:, 1, t:t + 1], ROUTED, ALU.mult, ALU.mult)
                i.then_inc(dve_done, V.step("gates"))

                dve.wait_ge(dve_done, V["gates"])
                dve.tensor_copy(g.gate2[:, :, :, 0], gates[:]).then_inc(dve_done, V.step("gate_hi"))
                dve.wait_ge(dve_done, V["gate_hi"])
                dve.tensor_tensor(g.gate2[:, :, :, 1], gates[:], g.gate2[:, :, :, 0].bitcast(F32), ALU.subtract) \
                    .then_inc(dve_done, V.step("gate_lo"))
                for t in T:
                    dve.wait_ge(act_done, A[("h2_hi", t)])
                    dve.tensor_tensor(g.h2s[:, 1, t, :], g.h2[:, t, :], g.h2s[:, 0, t, :].bitcast(F32), ALU.subtract) \
                        .then_inc(dve_done, V.step("h2_lo", t))

                def shared_act(t):
                    dve.wait_ge(act_done, A[("silu", t)])
                    dve.tensor_tensor(sact[:, t % 2], sact[:, t % 2], ps[:, t % 2, FE:2 * FE], ALU.mult) \
                        .then_inc(dve_done, V.step("act", t))

                shared_act(0)
                shared_act(1)
                dve.wait_ge(pe_done, PE[("pos", 2)])
                flat = lambda x: x[:].rearrange("p t e -> p (t e)")
                dve.scalar_tensor_tensor(out=flat(g.pos), in0=ps[:, 7, 0:TILES * E], scalar=1.0, in1=flat(rep),
                                         op0=ALU.add, op1=ALU.mult).then_inc(dve_done, V.step("pos"))
                dve.wait_ge(dve_done, V["pos"])
                dve.tensor_reduce(pmax[:], flat(g.pos), AX, ALU.max).then_inc(dve_done, V.step("pmax"))
                dve.wait_ge(pe_done, PE["pmaxT"])
                dve.tensor_reduce(nf[:, 0:1], ps[0:1, 2, 0:P], AX, ALU.max).then_inc(dve_done, V.step("nmax"))
                dve.wait_ge(dve_done, V["nmax"])
                dve.tensor_scalar(nf[:, 1:2], nf[:, 0:1], P + 0.5, None, ALU.is_gt).then_inc(dve_done, V.step("n1"))
                dve.tensor_scalar(nf[:, 2:3], nf[:, 0:1], 2 * P + 0.5, 1.0, ALU.is_gt, ALU.add) \
                    .then_inc(dve_done, V.step("n2"))
                dve.wait_ge(dve_done, V["n2"])
                dve.tensor_tensor(g.passes[:], nf[:, 1:2], nf[:, 2:3], ALU.add).then_inc(dve_done, V.step("n3"))
                shared_act(2)


def expert_slots(g, b):
    flat = lambda i: g.ring[:, i].rearrange("p k n -> p (k n)")
    return (flat(b).rearrange("p (m k n) -> p m k n", m=2, k=KD),
            flat(2)[:, b * KF * D:(b + 1) * KF * D].rearrange("p (j n) -> p j n", j=KF))


def load_expert_half(g, sp, e, b, half):
    wgu, wd = expert_slots(g, b)
    if half == 0:
        for m, w in enumerate((g.a["w_gate"], g.a["w_up"])):
            sp.dma_start(wgu[:, m], w[0, bass.ds(e, 1)].rearrange("e (p k) n -> p (e k) n", k=KD)) \
                .then_inc(g.s_gu[b], 16)
    else:
        sp.dma_start(wd, g.a["w_down"][0, bass.ds(e, 1)].rearrange("e (p j) n -> p (e j) n", j=KF)) \
            .then_inc(g.s_dn[b], 16)


class Event:

    def __init__(self, sem, ahead=0):
        self.sem, self.ahead = sem, ahead

    def value(self, i):
        return i + 1 + self.ahead


def phase_experts(nc, g):
    a, ps, c = g.a, g.ps, g.c
    T = range(TILES)
    PAIRS = EXPERTS // 2
    B = range(2)
    KP = 2
    GP = KD // KP
    NP = GP + KF
    PW = KP * 2 * FE
    assert PW == D
    F32R = mybir.dt.float32r
    with ExitStack() as ctx:
        def sb(name, shape, dt=F32R):
            return ctx.enter_context(nc.sbuf_tensor(name, shape, dt))
        wgu, wd = zip(*(expert_slots(g, b) for b in B))
        hi = sb("w_hi", [P, NP, PW])
        lo = sb("w_lo", [P, NP, PW])
        hot = sb("hot", [P, TILES, 2, P])
        hotT = sb("hotT", [P, 2, TOK])
        gcol = sb("gcol", [P, 2, TILES, 2])
        gslot = sb("gslot", [P, 2], F32)
        hgT = sb("hgT", [P, 2, KD, 2, P])
        sil = sb("sil", [P, 2, FE], F32)
        actT = sb("actT", [P, 2, 2, KF, P])
        ye = sb("ye", [P, 2, 2, D])
        s_gu, s_dn = g.s_gu, g.s_dn

        def event(name, ahead):
            return Event(g.sem(name), ahead)

        hot_made, gate_ps, gslot_sb = (event(n, 1) for n in ("hot_made", "slot_gates", "gslot_copied"))
        hg_ps, hgT_hi, hgT_lo = (event(n, 2) for n in ("gathered", "hgT_hi", "hgT_lo"))
        actT_ps, hotT_ps, silu, actT_hi, hotT_sb, ye_hi, act_done, actT_lo, ye_lo = (
            event(n, 2) for n in ("act_turned", "hot_turned", "silu_done", "actT_hi", "hotT_copied", "ye_hi",
                                  "act_done", "actT_lo", "ye_lo"))
        used, hi_made = event("pieces_used", NP), event("hi_made", NP)
        lo_gu, lo_dn = event("lo_gate_up_made", 2 * GP), event("lo_down_made", 2 * KF)
        units = [(t, n) for t in T for n in range(2)]
        U = len(units)
        y_ps, y_added = event("y_summed", U), event("y_added", 2 * U)
        YB = (6, 7, 5)
        GU, AT, HT, DN = 2, 3, 4, 6
        HG = (slice(0, 2), slice(4, 6))
        HK = KD // 2

        def wait(eng, ev, i):
            eng.wait_ge(ev.sem, ev.value(i))

        def turns(eng, own, prologue, body, epilogue):
            for ev in own:
                eng.sem_inc(ev.sem, ev.ahead)
            passes = eng.value_load(g.passes[0:1, 0:1], min_val=1, max_val=TILES)
            with eng.Fori(0, passes) as turn:
                first = turn * PAIRS
                prologue(first, 0)
                body(first, 0, True, False)
                with eng.Fori(1, PAIRS - 1) as pair:
                    body(first + pair, pair * 2, False, False)
                body(first + (PAIRS - 1), EXPERTS - 2, False, True)
                if epilogue:
                    epilogue(first + (PAIRS - 1), turn)
            return passes

        with nc.Block() as block:
            @block.sync
            def _(sp):
                def load(q, e, b):
                    n = 2 * q + b
                    for half, (ev, per) in enumerate(((lo_gu, GP), (lo_dn, KF))):
                        wait(sp, ev, (n - 2) * per + per - 1)
                        load_expert_half(g, sp, e, b, half)

                def body(q, e, first, last):
                    load(q, e + 1, 1)
                    load(q + 1, 0 if last else e + 2, 0)
                passes = turns(sp, (), lambda q, e: None, body, None)
                g.last_loads = [(s_gu[0], passes * (PAIRS * 32) + 32), (s_dn[0], passes * (PAIRS * 16) + 16)]

            @block.scalar
            def _(act):
                def split(q, b, i):
                    n = 2 * q + b
                    if i == 0:
                        act.wait_ge(s_gu[b], q * 32 + 32)
                    if i == GP:
                        act.wait_ge(s_dn[b], q * 16 + 16)
                    wait(act, used, (n - 1) * NP + i)
                    if i < GP:
                        act.activation(hi[:, i].rearrange("p (m k n) -> p m k n", m=2, k=KP),
                                       wgu[b][:, :, i * KP:(i + 1) * KP, :], ACT.Copy).then_inc(hi_made.sem, 1)
                    else:
                        act.activation(hi[:, i], wd[b][:, i - GP, :], ACT.Copy).then_inc(hi_made.sem, 1)

                def take_hg(q, h):
                    wait(act, hg_ps, 2 * q + h)
                    wait(act, used, (2 * q - 1) * NP + GP - 1)
                    act.activation(hgT[:, 0, h * HK:(h + 1) * HK].rearrange("p (b k) e n -> p b (k e n)", b=2),
                                   ps[:, HG[h], :], ACT.Copy).then_inc(hgT_hi.sem, 1)

                def take_silu(q, b):
                    n = 2 * q + b
                    wait(act, used, n * NP + GP - 1)
                    wait(act, actT_ps, n - 2)
                    act.activation(sil[:, b], ps[:, GU, 0:FE], ACT.Silu).then_inc(silu.sem, 1)

                def take_actT(q, b):
                    n = 2 * q + b
                    wait(act, actT_ps, n)
                    wait(act, used, (n - 2) * NP + NP - 1)
                    act.activation(actT[:, b, 0].rearrange("p j n -> p (j n)"), ps[:, AT, 0:KF * P], ACT.Copy) \
                        .then_inc(actT_hi.sem, 1)

                def take_hotT(q, b):
                    n = 2 * q + b
                    wait(act, hotT_ps, n)
                    act.activation(hotT[:, b, :], ps[:, (HT, GU)[b], 0:TOK], ACT.Copy).then_inc(hotT_sb.sem, 1)

                def take_ye(q, b):
                    n = 2 * q + b
                    wait(act, used, n * NP + NP - 1)
                    act.activation(ye[:, b, 0].rearrange("p (b n) -> p b n", b=2), ps[:, DN:DN + 2, :], ACT.Copy) \
                        .then_inc(ye_hi.sem, 1)

                def prologue(q, e):
                    take_hg(q, 0)
                    take_hg(q, 1)
                    for i in range(NP):
                        split(q, 0, i)

                def body(q, e, first, last):
                    split(q, 1, 0)
                    split(q, 1, 1)
                    take_silu(q, 0)
                    split(q, 1, 2)
                    take_actT(q, 0)
                    split(q, 1, 3)
                    take_hotT(q, 0)
                    take_hotT(q, 1)
                    split(q, 1, 4)
                    take_ye(q, 0)
                    split(q, 1, 5)
                    if not last:
                        split(q + 1, 0, 0)
                        split(q + 1, 0, 1)
                    take_silu(q, 1)
                    if not last:
                        split(q + 1, 0, 2)
                    take_actT(q, 1)
                    if not last:
                        take_hg(q + 1, 0)
                        split(q + 1, 0, 3)
                        take_hg(q + 1, 1)
                        split(q + 1, 0, 4)
                    take_ye(q, 1)
                    if not last:
                        split(q + 1, 0, 5)
                turns(act, (hgT_hi, silu, actT_hi, hotT_sb, ye_hi, hi_made), prologue, body, None)

            @block.gpsimd
            def _(pool):
                def split(q, b):
                    n = 2 * q + b
                    for j in range(KF):
                        wait(pool, hi_made, n * NP + GP + j)
                        pool.tensor_tensor(lo[:, GP + j], wd[b][:, j, :], hi[:, GP + j].bitcast(F32), ALU.subtract) \
                            .then_inc(lo_dn.sem, 1)

                def body(q, e, first, last):
                    split(q, 1)
                    if not last:
                        split(q + 1, 0)
                turns(pool, (lo_dn,), lambda q, e: split(q, 0), body, None)

            @block.tensor
            def _(pe):
                def gather(q, h):
                    if h == 0:
                        wait(pe, hot_made, q)
                        wait(pe, actT_hi, 2 * q - 2)
                        wait(pe, actT_lo, 2 * q - 2)
                        for b in B:
                            for t in T:
                                mm = pe.matmul(ps[:, AT, KF * P + 2 * b:KF * P + 2 * b + 2], hot[:, t, b, :],
                                               gcol[:, b, t, :], start=(t == 0), stop=(t == TILES - 1))
                        mm.then_inc(gate_ps.sem, 1)
                        wait(pe, hgT_hi, 2 * q - 2)
                        wait(pe, hgT_lo, 2 * q - 2)
                    else:
                        wait(pe, hotT_sb, 2 * q - 2)
                        wait(pe, y_added, (q - 2) * U + 5)
                    for k in range(HK):
                        for i, (part, t) in enumerate([(x, t) for x in range(2) for t in T]):
                            mm = pe.matmul(ps[:, HG[h].start + k // 2, (k % 2) * 2 * P:(k % 2 + 1) * 2 * P],
                                           g.h2s[:, part, t, h * HK + k::KD], hot[:, t],
                                           start=(i == 0), stop=(i == 2 * TILES - 1))
                    mm.then_inc(hg_ps.sem, 1)

                def gate_up(q, b):
                    n = 2 * q + b
                    wait(pe, act_done, n - 1)
                    if b:
                        wait(pe, hotT_sb, n)
                    for i in range(GP):
                        if b == 0 and i in (0, GP // 2):
                            wait(pe, hgT_hi, n + i // (GP // 2))
                            wait(pe, hgT_lo, n + i // (GP // 2))
                        wait(pe, hi_made, n * NP + i)
                        wait(pe, lo_gu, n * GP + i)
                        w = [x[:, i].rearrange("p (m k n) -> p m k n", m=2, k=KP) for x in (hi, lo)]
                        for k in range(KP):
                            kk = i * KP + k
                            for x, y in ((0, 0), (0, 1), (1, 0)):
                                mm = pe.matmul(ps[:, GU, :], hgT[:, x, kk, b, :], w[y][:, :, k, :],
                                               start=(kk == 0 and (x, y) == (0, 0)),
                                               stop=(kk == KD - 1 and (x, y) == (1, 0)))
                        mm.then_inc(used.sem, 1)

                def turn_act(q, b, last):
                    wait(pe, act_done, 2 * q + b)
                    wait(pe, gslot_sb, q + (b and not last))
                    for j in range(KF):
                        mm = pe.transpose(ps[:, AT, j * P:(j + 1) * P], sil[:, b, j::KF], c["ident"])
                    mm.then_inc(actT_ps.sem, 1)

                def down(q, b):
                    n = 2 * q + b
                    wait(pe, actT_hi, n)
                    wait(pe, actT_lo, n)
                    if b:
                        wait(pe, ye_hi, n - 1)
                        wait(pe, ye_lo, n - 1)
                    for j in range(KF):
                        wait(pe, hi_made, n * NP + GP + j)
                        wait(pe, lo_dn, n * KF + j)
                        for m in range(2):
                            if not b and j == 0:
                                wait(pe, y_added, q * U - 3 + m)
                            for x, y in ((0, 0), (0, 1), (1, 0)):
                                mm = pe.matmul(ps[:, DN + m, :], actT[:, b, x, j, :],
                                               (hi, lo)[y][:, GP + j, m * 512:(m + 1) * 512],
                                               start=(j == 0 and (x, y) == (0, 0)),
                                               stop=(j == KF - 1 and (x, y) == (1, 0)))
                        mm.then_inc(used.sem, 1)

                def scatter(q, turn=None, part=range(U)):
                    if part[0] == 0:
                        for ev in (ye_hi, ye_lo, hotT_sb):
                            wait(pe, ev, 2 * q + 1)
                    for i in part:
                        t, m = units[i]
                        wait(pe, y_added, q * U + (i - 3))
                        for j, (b, x) in enumerate([(b, x) for b in B for x in range(2)]):
                            mm = pe.matmul(ps[:, YB[i % 3], :], hotT[:, b, t * P:(t + 1) * P],
                                           ye[:, b, x, m * 512:(m + 1) * 512], start=(j == 0), stop=(j == 3))
                        mm.then_inc(y_ps.sem, 1)

                def turn_hot(q, b):
                    n = 2 * q + b
                    if b == 0:
                        wait(pe, hotT_sb, n - 2)
                    for t in T:
                        mm = pe.transpose(ps[:, (HT, GU)[b], t * P:(t + 1) * P], hot[:, t, b, :].bitcast(F32), c["ident"])
                    mm.then_inc(hotT_ps.sem, 1)

                def prologue(q, e):
                    gather(q, 0)
                    gather(q, 1)

                def body(q, e, first, last):
                    gate_up(q, 0)
                    if not first:
                        scatter(q - 1, part=range(0, 2))
                    turn_act(q, 0, last)
                    if not first:
                        scatter(q - 1, part=range(2, U))
                    turn_hot(q, 0)
                    turn_hot(q, 1)
                    down(q, 0)
                    gate_up(q, 1)
                    if not last:
                        gather(q + 1, 0)
                    turn_act(q, 1, last)
                    if not last:
                        gather(q + 1, 1)
                    down(q, 1)
                turns(pe, (hg_ps, gate_ps, actT_ps, hotT_ps, used, y_ps), prologue, body, scatter)

            @block.vector
            def _(dve):
                def make_hot(q, e):
                    wait(dve, hotT_ps, 2 * q - 1)
                    for b in B:
                        for t in T:
                            dve.tensor_scalar(hot[:, t, b, :], c["iota"], g.pos[:, t, bass.ds(e + b, 1)], None,
                                              ALU.is_equal)
                        i = dve.tensor_copy(gcol[:, b],
                                            g.gate2[:, :, bass.ds(e + b, 1), :].rearrange("p t e x -> p (t e) x"))
                    i.then_inc(hot_made.sem, 1)

                def take_gate(q):
                    wait(dve, gate_ps, q)
                    wait(dve, act_done, 2 * q - 1)
                    dve.tensor_reduce(gslot[:], ps[:, AT, KF * P:KF * P + 4].rearrange("p (b x) -> p b x", b=2),
                                      AX, ALU.add).then_inc(gslot_sb.sem, 1)

                def take_hg(q, h):
                    wait(dve, hgT_hi, 2 * q + h)
                    two = lambda x: x[:, h * HK:(h + 1) * HK].rearrange("p (b k) e n -> p b (k e n)", b=2)
                    dve.tensor_tensor(two(hgT[:, 1]), ps[:, HG[h], :], two(hgT[:, 0].bitcast(F32)),
                                      ALU.subtract).then_inc(hgT_lo.sem, 1)

                def split(q, b, i):
                    n = 2 * q + b
                    wait(dve, hi_made, n * NP + i)
                    dve.tensor_tensor(lo[:, i].rearrange("p (m k n) -> p m k n", m=2, k=KP),
                                      wgu[b][:, :, i * KP:(i + 1) * KP, :],
                                      hi[:, i].bitcast(F32).rearrange("p (m k n) -> p m k n", m=2, k=KP),
                                      ALU.subtract).then_inc(lo_gu.sem, 1)

                def take_act(q, b):
                    n = 2 * q + b
                    wait(dve, silu, n)
                    wait(dve, gslot_sb, q)
                    dve.scalar_tensor_tensor(out=sil[:, b], in0=ps[:, GU, FE:2 * FE], scalar=gslot[:, b:b + 1],
                                             in1=sil[:, b], op0=ALU.mult, op1=ALU.mult).then_inc(act_done.sem, 1)

                def take_actT(q, b):
                    n = 2 * q + b
                    wait(dve, actT_hi, n)
                    dve.tensor_tensor(actT[:, b, 1].rearrange("p j n -> p (j n)"), ps[:, AT, 0:KF * P],
                                      actT[:, b, 0].bitcast(F32).rearrange("p j n -> p (j n)"), ALU.subtract) \
                        .then_inc(actT_lo.sem, 1)

                def take_ye(q, b):
                    n = 2 * q + b
                    wait(dve, ye_hi, n)
                    dve.tensor_tensor(ye[:, b, 1].rearrange("p (b n) -> p b n", b=2), ps[:, DN:DN + 2, :],
                                      ye[:, b, 0].bitcast(F32).rearrange("p (b n) -> p b n", b=2), ALU.subtract) \
                        .then_inc(ye_lo.sem, 1)

                def add_y(q, part=range(U)):
                    for i in part:
                        t, m = units[i]
                        yt = g.y[:, t, m * 512:(m + 1) * 512]
                        wait(dve, y_ps, q * U + i)
                        wait(dve, y_added, q * U + (i - U))
                        dve.tensor_tensor(yt, yt, ps[:, YB[i % 3], :], ALU.add).then_inc(y_added.sem, 1)

                def prologue(q, e):
                    make_hot(q, e)
                    take_gate(q)
                    take_hg(q, 0)
                    take_hg(q, 1)
                    for i in range(GP):
                        split(q, 0, i)

                def body(q, e, first, last):
                    split(q, 1, 0)
                    split(q, 1, 1)
                    take_act(q, 0)
                    if not first:
                        add_y(q - 1, range(0, 2))
                    take_actT(q, 0)
                    if not first:
                        add_y(q - 1, range(2, 4))
                    split(q, 1, 2)
                    if not first:
                        add_y(q - 1, range(4, U))
                    split(q, 1, 3)
                    if not last:
                        make_hot(q + 1, e + 2)
                    take_ye(q, 0)
                    if not last:
                        split(q + 1, 0, 0)
                        split(q + 1, 0, 1)
                    take_act(q, 1)
                    if not last:
                        split(q + 1, 0, 2)
                        take_gate(q + 1)
                    take_actT(q, 1)
                    if not last:
                        take_hg(q + 1, 0)
                        split(q + 1, 0, 3)
                        take_hg(q + 1, 1)
                    take_ye(q, 1)

                def epilogue(q, turn):
                    add_y(q)
                    wait(dve, hot_made, q)
                    dve.tensor_scalar(g.pos[:], g.pos[:], -float(P), None, ALU.add).then_inc(g.s_pos, 1)
                    dve.wait_ge(g.s_pos, turn + 1)
                turns(dve, (hot_made, gslot_sb, act_done, hgT_lo, actT_lo, ye_lo, lo_gu, y_added), prologue, body, epilogue)


def phase_output(nc, g):
    a = g.a
    with ExitStack() as ctx:
        def sb(name, shape):
            return ctx.enter_context(nc.sbuf_tensor(name, shape, F32))
        gate = sb("gate_out", [P, 2, D])
        tmp = sb("tmp", [P, TILES, D])
        stat = sb("ostat2", [P, 4, TILES])
        s_row, s_out = g.sem("gate2_loaded"), g.sem("y_stored")
        dve_done, act_done = g.sem("out_dve"), g.sem("out_act")
        T = range(TILES)
        V = Count(["ms", "rec"] + [(x, t) for t in T for x in ("yn", "x2")])
        A = Count([("ss", t) for t in T] + ["rs"])
        with nc.Block() as block:
            @block.sync
            def _(sp):
                for v, (s, value) in enumerate(g.last_loads):
                    sp.wait_ge(s, value)
                    sp.dma_start(gate[:, v], g.mods_dram[v, 5].partition_broadcast(P)).then_inc(s_row, 16)
                for t in T:
                    sp.wait_ge(dve_done, V[("x2", t)])
                    dst = g.o["y_prompt"][0] if t == 0 else g.o["y_sample"][0, (t - 1) * P:t * P]
                    sp.dma_start(dst, g.x1[:, t, :]).then_inc(s_out, 16)
                sp.wait_ge(s_out, 16 * TILES)

            @block.scalar
            def _(act):
                for t in T:
                    act.activation(tmp[:, t, :], g.y[:, t, :], ACT.Square, accum_out=stat[:, 0, t:t + 1]) \
                        .then_inc(act_done, A.step("ss", t))
                act.wait_ge(dve_done, V["rec"])
                act.activation(stat[:, 3], stat[:, 2], ACT.Sqrt).then_inc(act_done, A.step("rs"))

            @block.vector
            def _(dve):
                dve.wait_ge(act_done, A[("ss", 2)])
                dve.tensor_scalar(stat[:, 1], stat[:, 0], 1.0 / D, EPS, ALU.mult, ALU.add).then_inc(dve_done, V.step("ms"))
                dve.wait_ge(dve_done, V["ms"])
                dve.reciprocal(stat[:, 2], stat[:, 1]).then_inc(dve_done, V.step("rec"))
                dve.wait_ge(act_done, A["rs"])
                dve.wait_ge(s_row, 32)
                for t in T:
                    dve.scalar_tensor_tensor(out=tmp[:, t, :], in0=g.y[:, t, :], scalar=stat[:, 3, t:t + 1],
                                             in1=gate[:, min(t, 1)], op0=ALU.mult, op1=ALU.mult) \
                        .then_inc(dve_done, V.step("yn", t))
                    dve.wait_ge(dve_done, V[("yn", t)])
                    dve.tensor_tensor(g.x1[:, t, :], g.x1[:, t, :], tmp[:, t, :], ALU.add) \
                        .then_inc(dve_done, V.step("x2", t))


def phases(nc, g, sb, sem):
    with ExitStack() as early:
        def eb(name, shape):
            return early.enter_context(nc.sbuf_tensor(name, shape, F32))
        g.hT = eb("hT", [P, KD, TOK])
        g.small = eb("small", [P, TILES, 64])
        g.z = eb("z", [P, TILES, GW])
        g.omla = eb("omla", [P, TILES, GW])
        with nc.sbuf_tensor("wconv", [P, CONV, 12], F32) as g.wconv, nc.sbuf_tensor("qkv", [P, 12, OUTW], F32) as g.qkv:
            phase_condition(nc, g)
            with nc.sbuf_tensor("cqkv", [P, TILES, 2 * LORA], F32) as g.cqkv, \
                    nc.sbuf_tensor("wuq", [P, KL, MH * QK], F32) as g.wuq, \
                    nc.sbuf_tensor("wukv", [P, KL, MH * (NOPE + VH)], F32) as g.wukv:
                g.s_attw = sem("attw_loaded")
                phase_project(nc, g)
                phase_attention(nc, g)
            phase_delta(nc, g)
        g.x1 = sb("x1", [P, TILES, D], side="right")
        g.ss2 = sb("ss2", [P, TILES], side="right")
        in_slot = lambda i: g.ring[:, i].rearrange("p k n -> p (k n)")
        g.rows = in_slot(0).rearrange("p (v m d) -> p v m d", v=2, m=2)
        g.wsg = in_slot(1).rearrange("p (m k n) -> p m k n", m=2, k=KD)
        g.wsd = in_slot(2)[:, KF * D:].rearrange("p (k n) -> p k n", k=KF)
        g.s_rows, g.s_ws = sem("ffn_rows_loaded"), sem("shared_loaded")
        g.s_gu = [sem(f"gate_up_loaded{b}") for b in range(2)]
        g.s_dn = [sem(f"down_loaded{b}") for b in range(2)]
        phase_merge(nc, g)
    F32R = mybir.dt.float32r
    g.y = sb("y", [P, TILES, D])
    g.h2s = sb("h2s", [P, 2, TILES, D], F32R)
    g.gate2 = sb("gate2", [P, TILES, EXPERTS, 2], F32R)
    g.pos = sb("pos", [P, TILES, EXPERTS])
    g.passes = sb("passes", [1, 1], mybir.dt.int32)
    g.s_pos = sem("pos_shifted")
    with nc.sbuf_tensor("h2", [P, TILES, D], F32) as g.h2, nc.sbuf_tensor("h2T", [P, KD, TOK], F32) as g.hT:
        phase_route(nc, g)
    phase_experts(nc, g)
    phase_output(nc, g)


_INS = ["x_prompt", "x_sample", "cache_ckv", "cache_krope", "state_delta", "c", "c_ctx", "w_ada", "b_ada",
        "g_pre_mix", "g_post_mix", "g_pre_ffn", "g_post_ffn", "w_in", "q_norm_g", "kv_norm_g", "w_uq", "w_ukv",
        "conv_w", "a_log", "dt_bias", "gdn_norm_g", "w_oa", "w_ob", "w_o", "w_router", "e_bias", "w_gate", "w_up",
        "w_down", "ws_gate", "ws_up", "ws_down"]
_OUTS = [("y_prompt", (1, CTX, D)), ("y_sample", (1, LAT, D)), ("ckv", (1, 1, CTX, LORA)),
         ("krope", (1, 1, CTX, ROPE)), ("state", (1, 1, 2, GH, DK, DV))]


def kernel(**inputs):
    from concourse import bacc
    from concourse.bass_utils import run_bass_kernel_spmd

    nc = bacc.Bacc("TRN2", target_bir_lowering=False, num_devices=1)
    arrays = {f"in_{n}": np.ascontiguousarray(inputs[n]) for n in _INS}
    arrays["in_table"] = constant_columns()[0]
    a = {n[3:]: nc.dram_tensor(n, v.shape, F32, kind="ExternalInput").ap() for n, v in arrays.items()}
    o = {n: nc.dram_tensor(f"out_{n}", s, F32, kind="ExternalOutput").ap() for n, s in _OUTS}
    build(nc, a, o)
    r = run_bass_kernel_spmd(nc, [arrays], core_ids=[0])
    return tuple(r.results[0][f"out_{n}"] for n, _ in _OUTS)
```
